# Optimizing a Trainium2 kernel written in Bass

```python
import jax, jax.numpy as jnp
from jax import lax
import numpy as np
import math

D_MODEL = 1024
BATCH = 1
SEQ = 2048
DEPTH = 1

MLA_HEADS = 4
QK_NOPE_DIM = 128
QK_ROPE_DIM = 64
QK_DIM = QK_NOPE_DIM + QK_ROPE_DIM
V_HEAD_DIM = 128
Q_LORA_RANK = 512
KV_LORA_RANK = 256
MLA_WIDTH = MLA_HEADS * V_HEAD_DIM
ROPE_THETA = 10000.0
Q_BLOCK = 128
POOL_WINDOWS = (2, 4, 8, 16)
POOL_GROUPS = len(POOL_WINDOWS)
POOL_WIDTH = D_MODEL - MLA_WIDTH
POOL_GROUP_DIM = POOL_WIDTH // POOL_GROUPS
MIX_WIDTH = MLA_WIDTH + POOL_WIDTH
IN_SPLITS = (Q_LORA_RANK, KV_LORA_RANK, QK_ROPE_DIM, MLA_WIDTH, POOL_WIDTH, POOL_WIDTH)
IN_WIDTH = sum(IN_SPLITS)
RMS_EPS = 1e-6
LN_EPS = 1e-5


def rms_norm(x, g):
    xf = x.astype(jnp.float32)
    inv = lax.rsqrt(jnp.mean(xf * xf, axis=-1, keepdims=True) + RMS_EPS)
    return (xf * inv).astype(x.dtype) * g

def layer_norm(x, g, b):
    xf = x.astype(jnp.float32)
    mu = jnp.mean(xf, axis=-1, keepdims=True)
    var = jnp.mean(jnp.square(xf - mu), axis=-1, keepdims=True)
    return ((xf - mu) * lax.rsqrt(var + LN_EPS)).astype(x.dtype) * g + b

def rope_cos_sin(positions, dtype):
    half = QK_ROPE_DIM // 2
    inv_freq = ROPE_THETA ** (-jnp.arange(half, dtype=jnp.float32) / half)
    ang = positions.astype(jnp.float32)[..., None] * inv_freq
    return jnp.cos(ang).astype(dtype), jnp.sin(ang).astype(dtype)

def apply_rope(t, cos, sin):
    t1, t2 = jnp.split(t, 2, axis=-1)
    return jnp.concatenate([t1 * cos - t2 * sin, t1 * sin + t2 * cos], axis=-1)

def mla_branch(x_q, x_kv, k_rope_raw, positions, q_norm_g, w_uq, kv_norm_g, w_ukv):
    B, S, _ = x_q.shape
    cos, sin = rope_cos_sin(positions, x_q.dtype)
    q = (rms_norm(x_q, q_norm_g) @ w_uq).reshape(B, S, MLA_HEADS, QK_DIM)
    q_nope, q_rope = q[..., :QK_NOPE_DIM], q[..., QK_NOPE_DIM:]
    q_rope = apply_rope(q_rope, cos[:, :, None, :], sin[:, :, None, :])
    kv = (rms_norm(x_kv, kv_norm_g) @ w_ukv).reshape(B, S, MLA_HEADS, QK_NOPE_DIM + V_HEAD_DIM)
    k_nope, v = kv[..., :QK_NOPE_DIM], kv[..., QK_NOPE_DIM:]
    k_rope = apply_rope(k_rope_raw, cos, sin)
    scale = QK_DIM ** -0.5
    nb = S // Q_BLOCK
    qn_b = q_nope.reshape(B, nb, Q_BLOCK, MLA_HEADS, QK_NOPE_DIM).transpose(1, 0, 2, 3, 4)
    qr_b = q_rope.reshape(B, nb, Q_BLOCK, MLA_HEADS, QK_ROPE_DIM).transpose(1, 0, 2, 3, 4)
    pos_b = positions.reshape(B, nb, Q_BLOCK).transpose(1, 0, 2)
    neg = jnp.finfo(jnp.float32).min

    def attend(args):
        qn, qr, pq = args
        s = (jnp.einsum('bqhd,bkhd->bhqk', qn, k_nope)
             + jnp.einsum('bqhr,bkr->bhqk', qr, k_rope)).astype(jnp.float32) * scale
        mask = pq[:, None, :, None] >= positions[:, None, None, :]
        p = jax.nn.softmax(jnp.where(mask, s, neg), axis=-1)
        return jnp.einsum('bhqk,bkhd->bqhd', p.astype(v.dtype), v)

    o = lax.map(attend, (qn_b, qr_b, pos_b))
    return o.transpose(1, 0, 2, 3, 4).reshape(B, S, MLA_WIDTH)

def pool_branch(u, pool_w, pool_scale):
    B, S, _ = u.shape
    uf = u.astype(jnp.float32).reshape(B, S, POOL_GROUPS, POOL_GROUP_DIM)
    cs = jnp.concatenate([jnp.zeros((B, 1, POOL_GROUPS, POOL_GROUP_DIM), jnp.float32),
                          jnp.cumsum(uf, axis=1)], axis=1)
    hi = jnp.arange(S) + 1
    means = []
    for g, w in enumerate(POOL_WINDOWS):
        lo = jnp.maximum(hi - w, 0)
        cnt = (hi - lo).astype(jnp.float32)[None, :, None]
        means.append((cs[:, hi, g] - cs[:, lo, g]) / cnt)
    pooled = jnp.stack(means, axis=2) - uf
    mixed = jnp.einsum('bsgc,gcd->bsgd', pooled.astype(u.dtype), pool_w)
    return mixed.reshape(B, S, POOL_WIDTH) * pool_scale

def first_inputs(seed: int = 0) -> dict:
    key = jax.random.key(seed)
    ks = jax.random.split(key, 12)
    beta = (8.0 * DEPTH) ** -0.25
    nrm = jax.random.normal
    return {
        "x": nrm(ks[0], (BATCH, SEQ, D_MODEL), jnp.float32),
        "positions": jnp.broadcast_to(jnp.arange(SEQ, dtype=jnp.int32), (BATCH, SEQ)),
        "w_in": nrm(ks[1], (D_MODEL, IN_WIDTH), jnp.float32) * D_MODEL ** -0.5,
        "q_norm_g": 1.0 + 0.05 * nrm(ks[2], (Q_LORA_RANK,), jnp.float32),
        "w_uq": nrm(ks[3], (Q_LORA_RANK, MLA_HEADS * QK_DIM), jnp.float32) * Q_LORA_RANK ** -0.5,
        "kv_norm_g": 1.0 + 0.05 * nrm(ks[4], (KV_LORA_RANK,), jnp.float32),
        "w_ukv": nrm(ks[5], (KV_LORA_RANK, MLA_HEADS * (QK_NOPE_DIM + V_HEAD_DIM)), jnp.float32) * KV_LORA_RANK ** -0.5,
        "pool_w": nrm(ks[6], (POOL_GROUPS, POOL_GROUP_DIM, POOL_GROUP_DIM), jnp.float32) * POOL_GROUP_DIM ** -0.5,
        "pool_scale": 1.0 + 0.1 * nrm(ks[7], (POOL_WIDTH,), jnp.float32),
        "w_out": nrm(ks[8], (MIX_WIDTH, D_MODEL), jnp.float32) * (MIX_WIDTH ** -0.5) * beta,
        "ln_g": 1.0 + 0.05 * nrm(ks[9], (DEPTH, D_MODEL), jnp.float32),
        "ln_b": 0.02 * nrm(ks[10], (DEPTH, D_MODEL), jnp.float32),
    }

def first_block(x, positions, w_in, q_norm_g, w_uq, kv_norm_g, w_ukv, pool_w, pool_scale, w_out, ln_g, ln_b):
    alpha = (2.0 * DEPTH) ** 0.25
    splits = [int(c) for c in np.cumsum(IN_SPLITS)[:-1]]
    for layer in range(DEPTH):
        h = x @ w_in
        x_q, x_kv, k_rope_raw, gate_a, u_pool, gate_b = jnp.split(h, splits, axis=-1)
        y_a = mla_branch(x_q, x_kv, k_rope_raw, positions, q_norm_g, w_uq, kv_norm_g, w_ukv) * jax.nn.silu(gate_a)
        y_b = pool_branch(u_pool, pool_w, pool_scale) * jax.nn.silu(gate_b)
        mix = jnp.concatenate([y_a, y_b], axis=-1) @ w_out
        x = layer_norm(alpha * x + mix, ln_g[layer], ln_b[layer])
    return x


N_META = 16
MIX_WIDTH_2 = D_MODEL
ATTN_WIDTH = MIX_WIDTH_2 // 2
HGRN_WIDTH = MIX_WIDTH_2 - ATTN_WIDTH
ATTN_HEADS = 8
ATTN_HEAD_DIM = ATTN_WIDTH // ATTN_HEADS
KV_RANK = 128
IDX_HEADS = 4
IDX_DIM = 64
TOPK_MAX = 256
HGRN_EXPAND = 128
HGRN_HEADS = HGRN_WIDTH // HGRN_EXPAND
HGRN_CHUNK = 64
REL_BUCKETS = 32
REL_MAX_DIST = 128
DN_ALPHA = (2 * DEPTH) ** 0.25
DN_BETA = (8 * DEPTH) ** -0.25
EPS = 1e-6

IN_SIZES = (ATTN_WIDTH, KV_RANK, IDX_HEADS * IDX_DIM, IDX_DIM, IDX_HEADS, ATTN_WIDTH,
            HGRN_WIDTH, HGRN_WIDTH, HGRN_WIDTH, HGRN_WIDTH)
N_IN = sum(IN_SIZES)
IN_OFFSETS = tuple(int(v) for v in np.cumsum(IN_SIZES)[:-1])


def layer_norm_2(x, g, b):
    xf = x.astype(jnp.float32)
    mu = jnp.mean(xf, axis=-1, keepdims=True)
    var = jnp.mean(jnp.square(xf - mu), axis=-1, keepdims=True)
    return ((xf - mu) * lax.rsqrt(var + EPS) * g + b).astype(x.dtype)

def rms_norm_2(x, g):
    xf = x.astype(jnp.float32)
    return (xf * lax.rsqrt(jnp.mean(jnp.square(xf), axis=-1, keepdims=True) + EPS) * g).astype(x.dtype)

def t5_bucket(dist):
    n = jnp.maximum(dist, 0)
    max_exact = REL_BUCKETS // 2
    nf = jnp.maximum(n, 1).astype(jnp.float32)
    large = max_exact + (jnp.log(nf / max_exact) / math.log(REL_MAX_DIST / max_exact)
                         * (REL_BUCKETS - max_exact)).astype(jnp.int32)
    large = jnp.minimum(large, REL_BUCKETS - 1)
    return jnp.where(n < max_exact, n, large)

def dsa_attention(q, c, qi, ki, wi, rel_bias, w_uk, w_uv):
    B, E = c.shape[0], c.shape[1]
    S = E - N_META
    k_top = min(TOPK_MAX, S // 4)
    scale = ATTN_HEAD_DIM ** -0.5
    q_lat = jnp.einsum('bthd,hdc->bthc', q, w_uk)
    c_m, c_r = c[:, :N_META], c[:, N_META:]
    ql_m, ql_r = q_lat[:, :N_META], q_lat[:, N_META:]
    qi_r, ki_r = qi[:, N_META:], ki[:, N_META:]
    wi_r = wi[:, N_META:] * (IDX_HEADS ** -0.5)
    meta_pos = jnp.arange(N_META)
    key_pos = jnp.arange(S)
    b_idx = jnp.arange(B)[:, None, None]

    lg = jnp.einsum('bqhc,bmc->bqhm', ql_m, c_m).astype(jnp.float32) * scale
    bm = rel_bias[t5_bucket(meta_pos[:, None] - meta_pos[None, :])]
    lg = lg + jnp.transpose(bm, (0, 2, 1))[None].astype(jnp.float32)
    lg = jnp.where((meta_pos[:, None] >= meta_pos[None, :])[None, :, None, :], lg, -jnp.inf)
    o_m = jnp.einsum('bqhm,bmc->bqhc', jax.nn.softmax(lg, axis=-1).astype(c.dtype), c_m)

    def block(bi):
        start = bi * Q_BLOCK
        q_pos = start + jnp.arange(Q_BLOCK)
        ql = lax.dynamic_slice_in_dim(ql_r, start, Q_BLOCK, axis=1)
        qib = lax.dynamic_slice_in_dim(qi_r, start, Q_BLOCK, axis=1)
        wib = lax.dynamic_slice_in_dim(wi_r, start, Q_BLOCK, axis=1)
        s_h = jax.nn.relu(jnp.einsum('bqhd,bkd->bqhk', qib, ki_r).astype(jnp.float32) * (IDX_DIM ** -0.5))
        s_idx = jnp.einsum('bqhk,bqh->bqk', s_h, wib.astype(jnp.float32))
        causal = key_pos[None, :] <= q_pos[:, None]
        s_idx = jnp.where(causal[None], s_idx, -jnp.inf)
        _, sel = lax.top_k(s_idx, k_top)
        valid = sel <= q_pos[None, :, None]
        c_sel = c_r[b_idx, sel]
        lg_s = jnp.einsum('bqhc,bqkc->bqhk', ql, c_sel).astype(jnp.float32) * scale
        bs = rel_bias[t5_bucket(q_pos[None, :, None] - sel)]
        lg_s = lg_s + jnp.moveaxis(bs, -1, 2).astype(jnp.float32)
        lg_s = jnp.where(valid[:, :, None, :], lg_s, -jnp.inf)
        lg_m = jnp.einsum('bqhc,bmc->bqhm', ql, c_m).astype(jnp.float32) * scale
        bmr = rel_bias[t5_bucket(N_META + q_pos[:, None] - meta_pos[None, :])]
        lg_m = lg_m + jnp.transpose(bmr, (0, 2, 1))[None].astype(jnp.float32)
        p = jax.nn.softmax(jnp.concatenate([lg_m, lg_s], axis=-1), axis=-1).astype(c.dtype)
        return (jnp.einsum('bqhm,bmc->bqhc', p[..., :N_META], c_m)
                + jnp.einsum('bqhk,bqkc->bqhc', p[..., N_META:], c_sel))

    o_r = lax.map(block, jnp.arange(S // Q_BLOCK))
    o_r = jnp.moveaxis(o_r, 0, 1).reshape(B, S, ATTN_HEADS, KV_RANK)
    o_lat = jnp.concatenate([o_m, o_r], axis=1)
    return jnp.einsum('bthc,hcd->bthd', o_lat, w_uv).reshape(B, E, ATTN_WIDTH)

def hgrn2(q, f_raw, i, lb):
    B, E = q.shape[0], q.shape[1]
    dt = q.dtype
    qf = jax.nn.silu(q.astype(jnp.float32)) * (HGRN_EXPAND ** -0.5)
    f = lb + (1.0 - lb) * jax.nn.sigmoid(f_raw.astype(jnp.float32))
    g = jnp.log(f)
    k = 1.0 - f
    v = i.astype(jnp.float32)
    pad = HGRN_CHUNK - N_META

    def to_chunks(a):
        a = jnp.pad(a, ((0, 0), (pad, 0), (0, 0)))
        n = a.shape[1] // HGRN_CHUNK
        return a.reshape(B, n, HGRN_CHUNK, HGRN_HEADS, HGRN_EXPAND).transpose(1, 0, 3, 2, 4)

    tri = jnp.tril(jnp.ones((HGRN_CHUNK, HGRN_CHUNK), dtype=bool))

    def step(state, inp):
        qc, kc, vc, gc = inp
        bcum = jnp.cumsum(gc, axis=2)
        o_inter = jnp.einsum('bhtk,bhkv->bhtv', qc * jnp.exp(bcum), state)
        diff = bcum[:, :, :, None, :] - bcum[:, :, None, :, :]
        decay = jnp.exp(jnp.where(tri[:, :, None], diff, -jnp.inf))
        scores = jnp.sum(qc[:, :, :, None, :] * decay * kc[:, :, None, :, :], axis=-1)
        o_intra = jnp.einsum('bhts,bhsv->bhtv', scores, vc)
        b_last = bcum[:, :, -1:, :]
        new_state = (jnp.exp(b_last[:, :, 0, :])[..., None] * state
                     + jnp.einsum('bhsk,bhsv->bhkv', kc * jnp.exp(b_last - bcum), vc))
        return new_state, o_inter + o_intra

    s0 = jnp.zeros((B, HGRN_HEADS, HGRN_EXPAND, HGRN_EXPAND), jnp.float32)
    _, outs = lax.scan(step, s0, (to_chunks(qf), to_chunks(k), to_chunks(v), to_chunks(g)))
    n = outs.shape[0]
    o = outs.transpose(1, 0, 3, 2, 4).reshape(B, n * HGRN_CHUNK, HGRN_HEADS, HGRN_EXPAND)[:, pad:]
    return o.astype(dt)

def second_inputs(seed: int = 0) -> dict:
    key = jax.random.key(seed)
    ks = jax.random.split(key, 12)
    nrm = jax.random.normal
    x = nrm(ks[0], (BATCH, SEQ, D_MODEL), jnp.float32)
    meta_tokens = nrm(ks[1], (N_META, D_MODEL), jnp.float32)
    rel_bias = 0.5 * nrm(ks[2], (REL_BUCKETS, ATTN_HEADS), jnp.float32)
    hgrn_lb_raw = nrm(ks[3], (DEPTH, HGRN_WIDTH), jnp.float32)
    w_in = nrm(ks[4], (DEPTH, D_MODEL, N_IN), jnp.float32) * D_MODEL ** -0.5
    kv_norm_g = 1.0 + 0.1 * nrm(ks[5], (DEPTH, KV_RANK), jnp.float32)
    w_uk = nrm(ks[6], (DEPTH, ATTN_HEADS, ATTN_HEAD_DIM, KV_RANK), jnp.float32) * ATTN_HEAD_DIM ** -0.5
    w_uv = nrm(ks[7], (DEPTH, ATTN_HEADS, KV_RANK, ATTN_HEAD_DIM), jnp.float32) * (KV_RANK ** -0.5 * DN_BETA)
    hgrn_norm_g = 1.0 + 0.1 * nrm(ks[8], (DEPTH, HGRN_EXPAND), jnp.float32)
    w_out = nrm(ks[9], (DEPTH, MIX_WIDTH_2, D_MODEL), jnp.float32) * (MIX_WIDTH_2 ** -0.5 * DN_BETA)
    ln_g = 1.0 + 0.1 * nrm(ks[10], (DEPTH, D_MODEL), jnp.float32)
    ln_b = 0.02 * nrm(ks[11], (DEPTH, D_MODEL), jnp.float32)
    return {"x": x, "meta_tokens": meta_tokens, "rel_bias": rel_bias, "hgrn_lb_raw": hgrn_lb_raw,
            "w_in": w_in, "kv_norm_g": kv_norm_g, "w_uk": w_uk, "w_uv": w_uv,
            "hgrn_norm_g": hgrn_norm_g, "w_out": w_out, "ln_g": ln_g, "ln_b": ln_b}

def second_block(x, meta_tokens, rel_bias, hgrn_lb_raw, w_in, kv_norm_g, w_uk, w_uv,
              hgrn_norm_g, w_out, ln_g, ln_b):
    B = x.shape[0]
    h = jnp.concatenate([jnp.broadcast_to(meta_tokens[None].astype(x.dtype), (B, N_META, D_MODEL)), x], axis=1)
    E = h.shape[1]
    lb_p = jax.nn.softmax(hgrn_lb_raw.astype(jnp.float32), axis=0)
    lb_all = jnp.cumsum(lb_p, axis=0) - lb_p[0:1]
    for l in range(DEPTH):
        proj = h @ w_in[l]
        (q_a, c_kv, q_idx, k_idx, w_idx, gate_a,
         q_h, f_h, i_h, gate_h) = jnp.split(proj, IN_OFFSETS, axis=-1)
        a = dsa_attention(q_a.reshape(B, E, ATTN_HEADS, ATTN_HEAD_DIM), rms_norm_2(c_kv, kv_norm_g[l]),
                          q_idx.reshape(B, E, IDX_HEADS, IDX_DIM), k_idx, w_idx,
                          rel_bias, w_uk[l], w_uv[l])
        a = a * jax.nn.silu(gate_a)
        r = hgrn2(q_h, f_h, i_h, lb_all[l])
        r = rms_norm_2(r, hgrn_norm_g[l]).reshape(B, E, HGRN_WIDTH) * jax.nn.silu(gate_h)
        y = jnp.concatenate([a, r], axis=-1) @ w_out[l]
        h = layer_norm_2(DN_ALPHA * h + y, ln_g[l], ln_b[l])
    return h[:, N_META:]


def setup_inputs(seed=0):
    out = dict(first_inputs(seed))
    for name, value in second_inputs(seed + 1).items():
        if name != "x":
            out[name + "_2"] = value
    return out


def reference(
    x, positions, w_in, q_norm_g, w_uq, kv_norm_g, w_ukv, pool_w, pool_scale, w_out, ln_g, ln_b,
    meta_tokens_2, rel_bias_2, hgrn_lb_raw_2, w_in_2, kv_norm_g_2, w_uk_2, w_uv_2,
    hgrn_norm_g_2, w_out_2, ln_g_2, ln_b_2,
):
    x = first_block(
        x, positions, w_in, q_norm_g, w_uq, kv_norm_g, w_ukv, pool_w, pool_scale, w_out, ln_g,
        ln_b,
    )
    return second_block(
        x, meta_tokens_2, rel_bias_2, hgrn_lb_raw_2, w_in_2, kv_norm_g_2, w_uk_2, w_uv_2,
        hgrn_norm_g_2, w_out_2, ln_g_2, ln_b_2,
    )


_drawn_inputs = setup_inputs


def setup_inputs(seed=0):
    import zlib

    import numpy as np

    out = dict(_drawn_inputs(seed))
    spreads = {}
    factors = {'q_norm_g': 8.0,
     'w_uq': 3.011,
     'kv_norm_g': 8.0,
     'pool_scale': 3.042,
     'ln_b': 2.718,
     'meta_tokens_2': 7.056,
     'rel_bias_2': 8.0,
     'kv_norm_g_2': 8.0,
     'hgrn_norm_g_2': 2.89,
     'ln_b_2': 2.676}
    for name, (base, spread) in spreads.items():
        noise = np.random.default_rng([zlib.crc32(name.encode()), seed]).standard_normal(out[name].shape)
        drawn = base * np.exp(spread * noise) if base else spread * noise
        out[name] = __import__('jax').numpy.asarray(drawn.astype(out[name].dtype))
    for name, factor in factors.items():
        out[name] = (out[name] * factor).astype(out[name].dtype)
    return out
```

```python
import concourse.bass as bass
import numpy as np
from concourse import mybir
from contextlib import ExitStack

D = 1024
S = 2048
P = 128
KC = D // P
TB = 512
G = S // TB
NB = S // P
BG = TB // P
H1 = 4
QR, KVR = 512, 256
ROPE = 64
QK_DIM = 192
RMS_EPS, LN_EPS = 1e-6, 1e-5
ALPHA = 2.0 ** 0.25
POOL_W = (2, 4, 8, 16)
HALO = 16
META = 16
H2, DH2 = 8, 64
HI = 4
TOPK = 256
H3 = 4
LEVELS = (64, 32, 16, 8, 4, 2, 1)
NEAR = 2 * P
ROUNDS = 24
MASKED = -1e30
HUGE = 3e38

RING = 6
SLOTS = 4

VEC = {}
_at = 0
for _name, _n in (("q_g", 4), ("kv_g", 2), ("pool_scale", 4), ("ln_g", 8), ("ln_b", 8),
                  ("kv_g2", 1), ("hgrn_g", 1), ("ln_g2", 8), ("ln_b2", 8), ("lb_raw", 4),
                  ("inv_freq", 1), ("rope_sign", 1)):
    VEC[_name] = _at
    _at += _n
NVEC = _at


def first_pair_steps(g):
    yield from [("kv", g, j) for j in range(2)]
    yield from [("krope", g, j) for j in range(2)]
    yield ("kv_sq", g)
    yield from [("k_nope", g, h) for h in range(H1)]
    yield from [("v", g, b) for b in range(BG)]


def mla_units(g):
    return [(BG * g + b, h) for b in range(BG) for h in range(H1)]


def mla_tiles(g):
    units = mla_units(g)
    for u in range(len(units) + 2):
        if u < len(units):
            yield from [("score", *units[u], c) for c in range(S // TB)]
        if 2 <= u and units[u - 2][1] == H1 - 1:
            yield ("o_t", units[u - 2][0])
        if 1 <= u <= len(units):
            yield from [("prob_t", *units[u - 1], c) for c in range(S // TB)]


def query_tiles(g):
    yield from [("xq", g, j) for j in range(4)]
    yield ("q_sq", g)
    yield from [("q_nope", g, h) for h in range(H1)]
    yield from [("q_rope", g, j) for j in range(4)]
    yield from [("gate_a", g, j) for j in range(4)]
    yield from [("u", g, j) for j in range(4)]
    yield from [("gate_b", g, j) for j in range(4)]
    yield from [("mix", g, j) for j in range(4)]


def out_tiles(g, tag):
    yield from [(tag + "out", g, c) for c in range(KC)]
    yield (tag + "mean", g)
    yield (tag + "var", g)


META_TILES = ([("t5_row",)] + [("t5", j) for j in range(4)] + [("m_c",), ("m_c_sq",), ("m_v",)] + [("m_f", h) for h in range(H3)] + [("m_i",), ("m_k_t",), ("m_u",)])


def second_steps(g):
    yield from [("f", g, 0), ("f", g, 1), ("hq", g, 0), ("hq", g, 1), ("i", g)]
    between = [[("gate_h", g, j)] for j in range(4)] + [[("c", g)], [("c_sq", g)] + [("v2", g, b) for b in range(BG)],
               [("ki", g)], [("qi", g, 0)], [("qi", g, 1)], [("qa", g, 0)], [("qa", g, 1)],
               [("qa", g, 2)], [("qa", g, 3)]] + [[("gate2", g, j)] for j in range(4)] + [
                   [("ql", g, h) for h in range(H2)], [("wi", g)]]
    for pair in range(2):
        if pair:
            yield from [("f", g, 2), ("f", g, 3), ("hq", g, 2), ("hq", g, 3)]
        for lev in range(len(LEVELS) + 1):
            yield from between.pop(0)
            yield ("level", g, pair, lev)
        yield ("state", g, pair)
    for rest in between:
        yield from rest


def tiles_of(step):
    kind, g = step[0], step[1]
    if kind == "i":
        return [("i", g, b) for b in range(BG)]
    if kind == "level":
        return [(*step, e) for e in range(2)]
    if kind == "state":
        pair = step[2]
        return ([("kd_t", g, pair, b) for b in range(BG)] + [t for b in range(BG) for t in (("o_h", g, pair, b), ("u_h", g, pair, b))]
                + [("h_sq", g, pair, e) for e in range(2)])
    return [step]


def keys_of(i):
    return (i + 1) * P


def near_width(i):
    return min(NEAR, keys_of(i))


def far_chunks(i):
    n = keys_of(i) - near_width(i)
    return [(c, min(TB, n - c)) for c in range(0, n, TB)]


def index_chunks(i):
    n = keys_of(i)
    return [(c, min(TB, n - c)) for c in range(0, n, TB)]


def needs_topk(i):
    return keys_of(i) > TOPK


def prob_tiles(i):
    return -(-(i + 1) // BG)


def prob_tiles_before(i, h):
    return H2 * sum(prob_tiles(b) for b in range(i)) + h * prob_tiles(i)


def index_adds_before(i):
    return HI * sum(len(index_chunks(b)) for b in range(i) if needs_topk(b))


def index_tiles(i):
    if needs_topk(i):
        yield from [("index", i, c, h) for c in range(len(index_chunks(i))) for h in range(HI)]


def dsa_units(g):
    return [(BG * g + b, h) for b in range(BG) for h in range(H2)]


def ended(units, u, back):
    return units[u - back][0] if 0 <= u - back < len(units) and units[u - back][1] == H2 - 1 else None


def dsa_tiles(g):
    units = dsa_units(g)
    yield from index_tiles(BG * g)
    for u in range(len(units) + 4):
        if u < len(units):
            i, h = units[u]
            if h == 0:
                if i + 1 < BG * (g + 1):
                    yield from index_tiles(i + 1)
                yield ("score_m", i)
            yield from [("far", i, h, c) for c in range(len(far_chunks(i)))]
            yield ("near", i, h)
        if ended(units, u, 2) is not None:
            yield ("pm_t", ended(units, u, 2))
        if 1 <= u <= len(units):
            i, h = units[u - 1]
            yield from [("p2_t", i, h, c) for c in range(prob_tiles(i))]
        if ended(units, u, 3) is not None:
            yield ("o2_t", ended(units, u, 3))


def schedule():
    tiles = []
    for g in range(G):
        tiles += first_pair_steps(g)
    for g in range(G):
        tiles += query_tiles(g)
        tiles += mla_tiles(g)
        tiles += out_tiles(g, "1")
    tiles += META_TILES
    for g in range(G):
        for step in second_steps(g):
            tiles += tiles_of(step)
        tiles += dsa_tiles(g)
        tiles += out_tiles(g, "2")
    return tiles


TILES = schedule()
T = {name: n for n, name in enumerate(TILES)}
assert len(T) == len(TILES)



def weight_of(name):
    kind = name[0]
    if kind == "kv":
        return ("w_in_kv", name[2])
    if kind == "krope":
        return ("w_in_kv", 2 + name[2])
    if kind in ("xq", "gate_a", "u", "gate_b"):
        return ("w_in_q", 4 * ("xq", "gate_a", "u", "gate_b").index(kind) + name[2])
    if kind in ("q_nope", "q_rope"):
        return ("w_uq", 4 * (kind == "q_rope") + name[2])
    if kind == "1out":
        return ("w_out", name[2])
    if kind == "2out":
        return ("w_out2", name[2])
    if kind in SECOND_CHUNKS:
        return ("w_in2", SECOND_CHUNKS[kind] + (name[2] if len(name) > 2 else 0))
    if kind == "m_c":
        return ("w_in2", SECOND_CHUNKS["c"])
    if kind == "m_f":
        return ("w_in2", SECOND_CHUNKS["f"] + name[1])
    return None


SECOND_CHUNKS = {"c": 0, "ki": 1, "qi": 2, "qa": 4, "gate2": 8, "hq": 12, "f": 16, "gate_h": 20}


def stream_of(tiles):
    out = []
    for name in tiles:
        if weight_of(name):
            out.append((name, *weight_of(name), name))
        if name[0] == "m_v" or (name[0] == "v2" and name[2] == 0):
            out.append((("w_uv",) + name[1:2], "w_uv", 0, name if name[0] == "m_v" else ("v2", name[1], BG - 1)))
        if name[0] == "ql" and name[2] == 0:
            out.append((("w_uk", name[1]), "w_uk", 0, ("ql", name[1], H2 - 1)))
        if name[0] == "m_i" or (name[0] == "i" and name[2] == 0):
            out += [(("w_i", name[1:2], j), "w_i", j, name if name[0] == "m_i" else ("i", name[1], BG - 1)) for j in range(4)]
    return out


def program(nc, A, out_t):
    f32, bf16, i32 = mybir.dt.float32, mybir.dt.bfloat16, mybir.dt.int32
    ALU, ACT, AX = mybir.AluOpType, mybir.ActivationFunctionType, mybir.AxisListType
    u8, u16 = mybir.dt.uint8, mybir.dt.uint16
    x1_t = nc.dram_tensor("x1_t", (P, KC, S), f32, kind="Internal").ap()
    t5_rows = nc.dram_tensor("t5_rows", (H2, 3 * P), f32, kind="Internal").ap()
    STREAM = stream_of(TILES)
    WSLOT = {name: n for n, (name, _, _, _) in enumerate(STREAM)}

    ctx = ExitStack()
    with ctx:
        def sem(name):
            return ctx.enter_context(nc.semaphore(name))

        def alloc(stack, name, shape, dt=f32):
            return stack.enter_context(nc.sbuf_tensor(name, shape, dt))

        ring = [alloc(ctx, f"weights{i}", [P, KC * P]) for i in range(SLOTS)]
        ident = alloc(ctx, "ident", [P, P])
        ones = alloc(ctx, "ones", [P, P])
        vec = alloc(ctx, "vec", [P, NVEC])
        eps = alloc(ctx, "eps", [P, 2])
        x_t = alloc(ctx, "x_t", [P, KC, TB])
        y_t = alloc(ctx, "y_t", [P, KC, TB])
        probs = alloc(ctx, "probs", [P, 2 * S])
        prob_t = alloc(ctx, "prob_t", [P, 2, TB])
        gate = alloc(ctx, "gate", [P, 4, TB])
        std = alloc(ctx, "std", [P, TB])
        rstd = alloc(ctx, "rstd", [P, TB])
        tmp = alloc(ctx, "tmp", [P, 2, TB])
        o_sb = alloc(ctx, "o_sb", [P, TB])
        stat = alloc(ctx, "stat", [P, 64])

        one = ExitStack()
        k_nope = alloc(one, "k_nope", [P, H1, S])
        k_rope = alloc(one, "k_rope", [P, S])
        val = alloc(one, "val", [P, NB, TB])
        q_nope = alloc(one, "q_nope", [P, H1, TB])
        q_rope = alloc(one, "q_rope", [P, H1, TB])
        lat = alloc(one, "lat", [P, 4, TB])
        cos = alloc(one, "cos", [P, TB])
        sin = alloc(one, "sin", [P, TB])
        pos_k = alloc(one, "pos_k", [P, S])
        pos_i = probs[:, 0:S].bitcast(i32)
        pos_q = alloc(one, "pos_q", [P, NB])
        pos_qi = alloc(one, "pos_qi", [P, NB], i32)
        mask = alloc(one, "mask", [P, S], bf16)
        pool_w = alloc(one, "pool_w", [P, 4, P])
        pool_cnt = alloc(one, "pool_cnt", [P, 4, HALO])
        halo = alloc(one, "halo", [P, 4, HALO])
        w_ukv = gate[:, :, :]
        u_in = probs[:, 0:4 * (TB + HALO)].rearrange("p (j t) -> p j t", j=4)
        u_sum = probs[:, 4 * (TB + HALO):6 * (TB + HALO)].rearrange("p (j t) -> p j t", j=2)
        one.close()

        two = ExitStack()
        c_t = alloc(two, "c_t", [P, S])
        v2 = alloc(two, "v2", [P, NB, TB])
        ki = alloc(two, "ki", [P, S])
        qa = alloc(two, "qa", [P, 4, TB])
        ql = alloc(two, "ql", [P, H2, TB])
        qi = alloc(two, "qi", [P, HI, TB])
        wi = alloc(two, "wi", [P, BG, HI])
        bias = alloc(two, "bias", [P, H2, NEAR])
        state = alloc(two, "state", [P, H3, P])
        index = alloc(two, "index", [P, S])
        sel = alloc(two, "sel", [P, 2, S], bf16)
        x_meta = alloc(two, "x_meta", [P, KC, META])
        v_meta = alloc(two, "v_meta", [P, TB])
        c_meta = alloc(two, "c_meta", [P, P])
        s_meta = alloc(two, "s_meta", [P, H2, META])
        p_meta = alloc(two, "p_meta", [P, P])
        pm_t = alloc(two, "pm_t", [P, P])
        causal = alloc(two, "causal", [P, P])
        lev_mask = alloc(two, "lev_mask", [P, len(LEVELS) + 1, P], u8)
        halves = alloc(two, "halves", [P, ROUNDS])
        steps_ = alloc(two, "steps", [P, ROUNDS])
        mids = alloc(two, "mids", [P, ROUNDS])
        counts = alloc(two, "counts", [P, ROUNDS])
        w_wi = alloc(two, "w_wi", [P, KC, HI])
        mx = alloc(two, "mx", [P, H2, 8])
        m2 = alloc(two, "m2", [P, 2, H2])
        sums2 = alloc(two, "sums2", [P, 2, H2])
        lb = alloc(two, "lb", [P, 2, H3])
        decay = alloc(two, "decay", [P, 2, BG])
        two.close()
        mask_i = probs[:, S:S + KC * P].bitcast(i32)
        anti, rel, t5_hot, t5_row = qa[:, 1, 0:P], qa[0:32, 3, 0:H2], qa[0:32, 0, 0:3 * P], qa[0:H2, 2, 0:3 * P]
        hf, hk, hb, hqb = (probs[:, n * 1024:(n + 1) * 1024].rearrange("p (e t) -> p e t", e=2) for n in range(4))
        he = index[:, 0:1024].rearrange("p (e t) -> p e t", e=2)
        ha = index[:, 1024:2048].rearrange("p (e t) -> p e t", e=2)
        h_i = sel[:, :, :].bitcast(f32).rearrange("p a n -> p (a n)").rearrange("p (b n) -> p b n", b=BG)
        kd_t = prob_t[:, :, :]
        near = x_t[:, 0:4, :].rearrange("p k t -> p (k t)").rearrange("p (h n) -> p h n", h=H2)
        x_hi = x_t[:, 4:8, :].rearrange("p k t -> p (k t)")
        rank = x_hi[:, 0:1024].bitcast(u16)
        above = x_hi[:, 1024:1536].bitcast(u8)
        band = x_hi[:, 1536:2048].bitcast(u8)

        banks = [ctx.enter_context(nc.psum_tensor(f"bank{i}", [P, TB], f32)) for i in range(RING)]
        o_acc = [ctx.enter_context(nc.psum_tensor(f"o_acc{i}", [P, TB], f32)) for i in range(2)]

        tile_ready = sem("tile_ready")
        drained = [sem(f"drained{i}") for i in range(RING)]
        w_here = [sem(f"w_here{i}") for i in range(SLOTS)]
        const_here = sem("const_here")
        ukv_here = sem("ukv_here")
        x_here = sem("x_here")
        ident_made = sem("ident_made")
        const_made = sem("const_made")
        act_step = sem("act_step")
        dve_step = sem("dve_step")
        pool_step = sem("pool_step")
        rope_arg = sem("rope_arg")
        rope_made = sem("rope_made")
        k_normed = sem("k_normed")
        k_stored = sem("k_stored")
        q_normed = sem("q_normed")
        q_rotated = sem("q_rotated")
        halo_kept = sem("halo_kept")
        win_summed = sem("win_summed")
        pooled = sem("pooled")
        row_max = sem("row_max")
        probs_made = sem("probs_made")
        pv_done = sem("pv_done")
        o_scaled = sem("o_scaled")
        centred = sem("centred")
        squared = sem("squared")
        scaled = sem("scaled")
        x_out = sem("x_out")
        stored = sem("stored")
        const2_here = sem("const2_here")
        t5_made = sem("t5_made")
        t5_here = sem("t5_here")
        std_read = sem("std_read")
        c_normed = sem("c_normed")
        lb_arg = sem("lb_arg")
        lb_exp = sem("lb_exp")
        f_made = sem("f_made")
        f_log = sem("f_log")
        f_summed = sem("f_summed")
        lev_diff = sem("lev_diff")
        lev_exp = sem("lev_exp")
        lev_made = sem("lev_made")
        h_free = sem("h_free")
        o_squared = sem("o_squared")
        u_meta = sem("u_meta")
        lev_diff_meta = sem("lev_diff_meta")
        index_added = sem("index_added")
        sel_made = sem("sel_made")
        near_made = sem("near_made")
        row_max2 = sem("row_max2")
        probs2_made = sem("probs2_made")
        pm_arg = sem("pm_arg")
        pm_made = sem("pm_made")
        pv2_done = sem("pv2_done")
        pvm_done = sem("pvm_done")
        o2_scaled = sem("o2_scaled")
        gates_made = sem("gates_made")
        stored2 = sem("stored2")
        block = ctx.enter_context(nc.Block())

        def counter(semaphore):
            count = [0]

            def step(eng, ins):
                count[0] += 1
                ins.then_inc(semaphore, 1)
                eng.wait_ge(semaphore, count[0])
            return step

        def wait_tile(eng, *name):
            eng.wait_ge(tile_ready, T[name] + 1)

        def wait_drained(eng, *name):
            n = T[name]
            eng.wait_ge(drained[n % RING], n // RING + 1)

        def bank(*name):
            return banks[T[name] % RING]

        def drains(ins, *name):
            ins.then_inc(drained[T[name] % RING], 1)

        def sq_view(buf):
            return buf[:].rearrange("p (k t) -> p k t", k=KC)

        POOL_STEPS = 4 + (0 + 1 + 2 + 3) + 4

        def prev_unit(units, u, g, back):
            return units[u - back] if u >= back else mla_units(g - 1)[u - back]

        def out_norm(tag, g, dve, step, V):
            for c in range(KC):
                wait_tile(dve, tag + "out", g, c)
                drains(V.scalar_tensor_tensor(out=x_t[:, c, :], in0=x_t[:, c, :], scalar=ALPHA,
                                              in1=bank(tag + "out", g, c)[:], op0=ALU.mult, op1=ALU.add), tag + "out", g, c)
            wait_tile(dve, tag + "mean", g)
            drains(V.tensor_scalar(rstd[:], bank(tag + "mean", g)[:], -1.0 / D, None, ALU.mult), tag + "mean", g)
            wait_drained(dve, tag + "mean", g)
            V.tensor_tensor(x_t[:], x_t[:], rstd[:].unsqueeze(1).broadcast_to([P, KC, TB]), ALU.add).then_inc(centred, 1)
            wait_drained(dve, tag + "var", g)
            dve.wait_ge(centred, g + 1 + (0 if tag == "1" else G))
            if tag == "1":
                step(dve, V.reciprocal(rstd[:], std[:]))
            else:
                V.reciprocal(rstd[:], std[:]).then_inc(std_read, 1)
                dve.wait_ge(std_read, N_STD[g] + 1)
            V.tensor_tensor(x_t[:], x_t[:], rstd[:].unsqueeze(1).broadcast_to([P, KC, TB]), ALU.mult).then_inc(scaled, 1)

        SECOND_CONSTANTS = ((rel, A["rel"]), (t5_hot, A["t5_hot"]), (anti, A["anti"]), (x_meta[:], A["meta_t"]),
                            (causal[:], A["causal"]), (mask_i, A["lev_mask"]), (halves[:], A["halves"]),
                            (w_wi[:], A["w_wi"]), (v_meta[:], A["block_diag"]))
        N_CONST2 = 16 * len(SECOND_CONSTANTS)

        def second_begins(eng):
            eng.wait_ge(stored, 16 * G)
            eng.wait_ge(const2_here, N_CONST2)

        def level_no(g, pair, k):
            return (2 * g + pair) * (len(LEVELS) + 2) + k

        C_STD, H_STD, N_STD = {}, {}, {}
        reads = 1
        for g in range(G):
            for st in second_steps(g):
                if st[0] == "c_sq":
                    C_STD[g] = reads
                    reads += 1
                if st[0] == "state":
                    for e in range(2):
                        H_STD[(g, 2 * st[2] + e)] = reads
                        reads += 1
            N_STD[g] = reads
            reads += 1

        def halved(ap, w):
            return ap.rearrange("p e (n t) -> p (e n) t", t=2 * w)

        @block.sync
        def _(sp):
            for dst, src in ((ident[:], A["ident"]), (vec[:], A["vec"]), (pool_w[:], A["pool_w"]),
                             (pool_cnt[:], A["pool_cnt"]), (pos_qi[:], A["pos_q"]),
                             (pos_i, A["pos_k"].broadcast_to([P, S])), (w_ukv, A["w_ukv"])):
                sp.dma_start(dst, src).then_inc(const_here, 16)

            def load_x(g, src):
                for k in range(0, KC, 4):
                    sp.dma_start(x_t[:, k:k + 4, :], src[:, k:k + 4, g * TB:(g + 1) * TB]).then_inc(x_here, 16)

            sent = 0
            for name, arr, idx, _ in STREAM:
                if name[0] == "kv" and name[2] == 0:
                    if name[1] > 0:
                        wait_tile(sp, "krope", name[1] - 1, 1)
                    load_x(name[1], A["x_t"])
                if name[0] == "xq" and name[2] == 0:
                    if name[1] == 0:
                        wait_tile(sp, "krope", G - 1, 1)
                    else:
                        sp.wait_ge(stored, 16 * name[1])
                    load_x(name[1], A["x_t"])
                if name[0] == "m_c":
                    sp.wait_ge(stored, 16 * G)
                    for dst, src in SECOND_CONSTANTS:
                        sp.dma_start(dst, src).then_inc(const2_here, 16)
                if name[0] == "f" and name[2] == 0:
                    if name[1] > 0:
                        sp.wait_ge(stored2, 16 * name[1])
                    load_x(name[1], x1_t)
                if name[0] == "2out" and name[2] == 0:
                    sp.wait_ge(row_max2, H2 * BG * (name[1] + 1))
                    load_x(name[1], x1_t)
                if sent >= SLOTS:
                    wait_tile(sp, *STREAM[sent - SLOTS][3])
                src = A[arr][idx]
                sp.dma_start(ring[sent % SLOTS][:, 0:src.shape[1]], src).then_inc(w_here[sent % SLOTS], 16)
                sent += 1
                if name[0] in ("1out", "2out") and name[2] == KC - 1:
                    g = name[1]
                    first = name[0] == "1out"
                    sp.wait_ge(x_out, g + 1 + (0 if first else G))
                    dst = x1_t if first else out_t
                    sp.dma_start(dst[:, :, g * TB:(g + 1) * TB], x_t[:]).then_inc(stored if first else stored2, 16)
            sp.wait_ge(stored2, 16 * G)

        @block.gpsimd
        def _(pool):
            step = counter(pool_step)
            pool.memset(ones[:], 1.0).then_inc(const_made, 1)
            pool.memset(eps[:, 0:1], RMS_EPS).then_inc(const_made, 1)
            pool.memset(eps[:, 1:2], LN_EPS).then_inc(const_made, 1)
            pool.memset(halo[:], 0.0).then_inc(const_made, 1)
            pool.memset(q_rope[:], 0.0).then_inc(const_made, 1)
            pool.wait_ge(const_made, 5)
            for g in range(G):
                for j in range(4):
                    wait_drained(pool, "u", g, j)
                    step(pool, pool.tensor_copy(u_in[:, j, 0:HALO], halo[:, j, :]))
                    src = u_in[:, j, :]
                    for s in range(j + 1):
                        lo = 2 ** (s + 1) - 1
                        if s == 0 and j > 0:
                            pool.wait_ge(pooled, 4 * g + j)
                        if s == 0 and j == 0:
                            wait_tile(pool, "q_rope", g, 3)
                        dst = u_sum[:, s % 2, :]
                        ins = pool.tensor_tensor(dst[:, lo:], src[:, lo:], src[:, lo - 2 ** s:TB + HALO - 2 ** s], ALU.add)
                        if s < j:
                            step(pool, ins)
                        src = dst
                    ins.then_inc(win_summed, 1)
                for j in range(4):
                    ins = pool.tensor_copy(halo[:, j, :], u_in[:, j, TB:TB + HALO])
                    step(pool, ins)
            pool.wait_ge(win_summed, 4 * G)

            second_begins(pool)
            pool.memset(qi[:], 0.0).then_inc(const_made, 1)
            pool.wait_ge(t5_made, 1)
            pool.dma_start(t5_rows, t5_row).then_inc(t5_here, 16)
            pool.wait_ge(t5_here, 16)
            pool.dma_start(index[:].rearrange("p (h n) -> p h n", h=H2),
                           bass.AP(t5_rows.tensor, 0, [[1, P], [3 * P, H2], [1, NEAR]])).then_inc(t5_here, 16)
            for g in range(G):
                for pair in range(2):
                    pool.wait_ge(f_summed, 2 * g + pair + 1)
                    for k, w in enumerate(LEVELS):
                        n = level_no(g, pair, k)
                        if n > 0:
                            pool.wait_ge(lev_made, n)
                        b, e = halved(hb, w), halved(he, w)
                        mid = b[:, :, w - 1:w].broadcast_to([P, 2 * TB // (2 * w), w])
                        pool.tensor_tensor(e[:, :, 0:w], mid, b[:, :, 0:w], ALU.subtract).then_inc(lev_diff, 1)
                        pool.tensor_tensor(e[:, :, w:2 * w], b[:, :, w:2 * w], mid, ALU.subtract).then_inc(lev_diff, 1)
                    pool.wait_ge(lev_made, level_no(g, pair, len(LEVELS) + 1))
                    b, e = halved(hb, P // 2), halved(he, P // 2)
                    pool.tensor_tensor(e, b[:, :, P - 1:P].broadcast_to([P, 2 * BG, P]), b, ALU.subtract).then_inc(lev_diff, 1)
                for step_ in second_steps(g):
                    pass
                wait_tile(pool, *tiles_of(step_)[-1])
                for b in range(BG):
                    i = BG * g + b
                    pool.wait_ge(sel_made, i + 1)
                    wn = near_width(i)
                    n = keys_of(i)
                    for h in range(H2):
                        if b > 0:
                            pool.wait_ge(row_max2, H2 * (i - 1) + h + 1)
                        pool.tensor_tensor(near[:, h, NEAR - wn:], bias[:, h, NEAR - wn:], sel[:, i % 2, n - wn:n],
                                           ALU.add).then_inc(near_made, 1)

        @block.scalar
        def _(act):
            step = counter(act_step)
            A_ = nc.scalar.activation

            def rope_tables(n):
                act.wait_ge(rope_arg, n + 1)
                step(act, A_(cos[:], cos[:], ACT.Sin))
                A_(sin[:], sin[:], ACT.Sin).then_inc(rope_made, 1)

            def latents(tag, g, n, sq, gain, before):
                for j in range(n):
                    wait_tile(act, tag, g, j)
                    step(act, A_(sq[:, j, :], bank(tag, g, j)[:], ACT.Square))
                    if j == 0 and before is not None:
                        wait_tile(act, *before)
                    drains(A_(lat[:, j, :], bank(tag, g, j)[:], ACT.Copy, scale=vec[:, gain + j:gain + j + 1]), tag, g, j)

            def root(name, width, e, free=None):
                wait_tile(act, *name)
                if free is not None:
                    act.wait_ge(*free)
                drains(A_(std[:], bank(*name)[:], ACT.Sqrt, scale=1.0 / width, bias=eps[:, e:e + 1]), *name)

            act.wait_ge(const_here, 16 * 7)
            act.wait_ge(const_made, 5)
            for g in range(G):
                rope_tables(g)
                if g > 0:
                    wait_tile(act, "kv_sq", g - 1)
                latents("kv", g, 2, y_t, VEC["kv_g"], ("v", g - 1, BG - 1) if g else None)
                root(("kv_sq", g), KVR, 0, (k_normed, g) if g else None)
                for b in range(BG):
                    wait_tile(act, "v", g, b)
                    drains(A_(val[:, BG * g + b, :], bank("v", g, b)[:], ACT.Copy), "v", g, b)

            for g in range(G):
                rope_tables(G + g)
                if g > 0:
                    wait_tile(act, "1out", g - 1, KC - 1)
                latents("xq", g, 4, y_t, VEC["q_g"], ("v", G - 1, BG - 1) if g == 0 else ("mix", g - 1, 3))
                root(("q_sq", g), QR, 0, (k_normed, G) if g == 0 else (scaled, g))
                for h in range(H1):
                    wait_tile(act, "q_nope", g, h)
                    drains(A_(q_nope[:, h, :], bank("q_nope", g, h)[:], ACT.Copy), "q_nope", g, h)
                for j in range(4):
                    wait_tile(act, "gate_a", g, j)
                    drains(A_(gate[:, j, :], bank("gate_a", g, j)[:], ACT.Silu), "gate_a", g, j)
                for j in range(4):
                    wait_tile(act, "u", g, j)
                    if g == 0 and j == 0:
                        act.wait_ge(q_rotated, 1)
                    drains(A_(u_in[:, j, HALO:], bank("u", g, j)[:], ACT.Copy), "u", g, j)
                for j in range(4):
                    wait_tile(act, "gate_b", g, j)
                    drains(A_(y_t[:, 4 + j, :], bank("gate_b", g, j)[:], ACT.Silu), "gate_b", g, j)

                units = mla_units(g)
                for u in range(len(units) + 1):
                    if u > 0:
                        i, h = units[u - 1]
                        for c in range(S // TB):
                            m = (H1 * BG * g + u - 1) * (S // TB) + c
                            wait_tile(act, "prob_t", i, h, c)
                            if m >= 2:
                                act.wait_ge(pv_done, m - 1)
                            drains(A_(prob_t[:, m % 2, :], bank("prob_t", i, h, c)[:], ACT.Copy), "prob_t", i, h, c)
                    if u < len(units):
                        n = H1 * BG * g + u
                        act.wait_ge(row_max, n + 1)
                        p = probs[:, (n % 2) * S:(n % 2 + 1) * S]
                        A_(p, p, ACT.Exp, scale=QK_DIM ** -0.5, bias=stat[:, 8 + n % 2:9 + n % 2],
                           accum_out=stat[:, 16 + n % 8:17 + n % 8]).then_inc(probs_made, 1)

                act.wait_ge(centred, g + 1)
                for c in range(KC):
                    A_(sq_view(probs)[:, c, :], x_t[:, c, :], ACT.Square).then_inc(squared, 1)
                root(("1var", g), D, 1)
                for c in range(KC):
                    act.wait_ge(scaled, g + 1)
                    ins = A_(x_t[:, c, :], x_t[:, c, :], ACT.Identity, scale=vec[:, VEC["ln_g"] + c:VEC["ln_g"] + c + 1],
                             bias=vec[:, VEC["ln_b"] + c:VEC["ln_b"] + c + 1])
                    if c < KC - 1:
                        step(act, ins)
                ins.then_inc(x_out, 1)

            second_begins(act)
            wait_tile(act, "m_c")
            A_(tmp[:, 0, 0:META], bank("m_c")[:, 0:META], ACT.Square).then_inc(lb_exp, 1)
            drains(A_(c_t[:, 0:META], bank("m_c")[:, 0:META], ACT.Copy, scale=vec[:, VEC["kv_g2"]:VEC["kv_g2"] + 1]), "m_c")
            wait_tile(act, "m_c_sq")
            drains(A_(std[:, 0:META], bank("m_c_sq")[:, 0:META], ACT.Sqrt, scale=1.0 / P, bias=eps[:, 0:1]), "m_c_sq")
            act.wait_ge(lb_arg, 1)
            A_(lb[:, 0, :], lb[:, 0, :], ACT.Exp).then_inc(lb_exp, 1)
            for h in range(H3):
                wait_tile(act, "m_f", h)
                drains(A_(probs[:, h * META:(h + 1) * META], bank("m_f", h)[:, 0:META], ACT.Sigmoid), "m_f", h)
            act.wait_ge(f_made, 1)
            A_(probs[:, 0:H3 * META], probs[:, 0:H3 * META], ACT.Ln).then_inc(f_log, 1)
            wait_tile(act, "m_i")
            drains(A_(h_i[0:META, 0, :], bank("m_i")[0:META, :], ACT.Copy), "m_i")
            act.wait_ge(lev_diff_meta, 1)
            A_(probs[:, 256:256 + H3 * META], probs[:, 256:256 + H3 * META], ACT.Exp).then_inc(u_meta, 1)
            wait_tile(act, "m_k_t")
            drains(A_(kd_t[0:META, 0, :], bank("m_k_t")[0:META, :], ACT.Copy), "m_k_t")

            for g in range(G):
                for st in second_steps(g):
                    kind = st[0]
                    if kind == "f":
                        h = st[2]
                        if h == 2:
                            wait_tile(act, "o_h", g, 0, BG - 1)
                        elif h == 0 and g > 0:
                            wait_tile(act, "2var", g - 1)
                        elif h == 0:
                            act.wait_ge(u_meta, 2)
                        wait_tile(act, *st)
                        drains(A_(hf[:, h % 2, :], bank(*st)[:], ACT.Sigmoid), *st)
                    elif kind == "hq":
                        h = st[2]
                        wait_tile(act, *st)
                        if h == 2:
                            act.wait_ge(lev_made, level_no(g, 1, 0))
                        drains(A_(hqb[:, h % 2, :], bank(*st)[:], ACT.Silu), *st)
                        if h % 2 == 1:
                            act.wait_ge(f_made, 2 + 2 * g + h // 2)
                            A_(hf, hf, ACT.Ln).then_inc(f_log, 1)
                    elif kind == "gate_h":
                        wait_tile(act, *st)
                        drains(A_(y_t[:, 4 + st[2], :], bank(*st)[:], ACT.Copy), *st)
                    elif kind == "gate2":
                        wait_tile(act, *st)
                        drains(A_(gate[:, st[2], :], bank(*st)[:], ACT.Copy), *st)
                    elif kind == "i":
                        for b in range(BG):
                            wait_tile(act, "i", g, b)
                            drains(A_(h_i[:, b, :], bank("i", g, b)[:], ACT.Copy), "i", g, b)
                    elif kind == "c":
                        wait_tile(act, *st)
                        step(act, A_(tmp[:, 0, :], bank(*st)[:], ACT.Square))
                        drains(A_(c_t[:, g * TB:(g + 1) * TB], bank(*st)[:], ACT.Copy, scale=vec[:, VEC["kv_g2"]:VEC["kv_g2"] + 1]), *st)
                    elif kind == "c_sq":
                        wait_tile(act, *st)
                        act.wait_ge(std_read, C_STD[g])
                        drains(A_(std[:], bank(*st)[:], ACT.Sqrt, scale=1.0 / P, bias=eps[:, 0:1]), *st)
                    elif kind == "v2":
                        wait_tile(act, *st)
                        drains(A_(v2[:, BG * g + st[2], :], bank(*st)[:], ACT.Copy), *st)
                    elif kind == "qa":
                        wait_tile(act, *st)
                        drains(A_(qa[:, st[2], :], bank(*st)[:], ACT.Copy), *st)
                    elif kind == "ql":
                        wait_tile(act, *st)
                        drains(A_(ql[:, st[2], :], bank(*st)[:], ACT.Copy, scale=DH2 ** -0.5), *st)
                    elif kind == "level":
                        pair, lev = st[2], st[3]
                        if lev < len(LEVELS):
                            act.wait_ge(lev_diff, 15 * (2 * g + pair) + 2 * (lev + 1))
                            A_(he, he, ACT.Exp).then_inc(lev_exp, 1)
                    elif kind == "state":
                        pair = st[2]
                        act.wait_ge(lev_made, level_no(g, pair, len(LEVELS)))
                        step(act, A_(decay[:], hb.rearrange("p e (b t) -> p e b t", b=BG)[:, :, :, P - 1], ACT.Exp))
                        A_(he, hb, ACT.Exp).then_inc(lev_exp, 1)
                        act.wait_ge(lev_diff, 15 * (2 * g + pair + 1))
                        A_(he, he, ACT.Exp).then_inc(lev_exp, 1)
                        for b in range(BG):
                            wait_tile(act, "kd_t", g, pair, b)
                            drains(A_(kd_t[:, b // 2, (b % 2) * 256:(b % 2) * 256 + 256], bank("kd_t", g, pair, b)[:, 0:256],
                                      ACT.Copy), "kd_t", g, pair, b)
                        for b in range(BG):
                            wait_tile(act, "o_h", g, pair, b)
                            drains(A_(hb[:, :, b * P:(b + 1) * P], bank("o_h", g, pair, b)[:, 0:256].rearrange("p (e t) -> p e t", e=2),
                                      ACT.Copy, scale=P ** -0.5), "o_h", g, pair, b)
                        for b in range(BG):
                            wait_drained(act, "o_h", g, pair, b)
                        A_(hk, hb, ACT.Square).then_inc(o_squared, 1)
                        if pair == 0:
                            for j in range(4):
                                wait_drained(act, "gate_h", g, j)
                            A_(y_t[:, 4:8, :], y_t[:, 4:8, :], ACT.Silu).then_inc(gates_made, 1)
                        for e in range(2):
                            wait_tile(act, "h_sq", g, pair, e)
                            act.wait_ge(std_read, H_STD[(g, 2 * pair + e)])
                            drains(A_(std[:], bank("h_sq", g, pair, e)[:], ACT.Sqrt, scale=1.0 / P, bias=eps[:, 0:1]),
                                   "h_sq", g, pair, e)

                for j in range(4):
                    wait_drained(act, "gate2", g, j)
                A_(gate[:], gate[:], ACT.Silu).then_inc(gates_made, 1)

                def relus(i):
                    if not needs_topk(i):
                        return
                    m = index_adds_before(i)
                    for c, (_, wide_) in enumerate(index_chunks(i)):
                        for h in range(HI):
                            wait_tile(act, "index", i, c, h)
                            if m >= 2:
                                act.wait_ge(index_added, m - 1)
                            drains(A_(tmp[:, m % 2, 0:wide_], bank("index", i, c, h)[:, 0:wide_], ACT.Relu,
                                      scale=DH2 ** -0.5), "index", i, c, h)
                            m += 1

                units = dsa_units(g)
                relus(BG * g)
                for u in range(len(units) + 4):
                    if u < len(units) and units[u][1] == 0 and units[u][0] + 1 < BG * (g + 1):
                        relus(units[u][0] + 1)
                    if ended(units, u, 2) is not None:
                        i = ended(units, u, 2)
                        wait_tile(act, "pm_t", i)
                        drains(A_(pm_t[:], bank("pm_t", i)[:, 0:P], ACT.Copy), "pm_t", i)
                    if 1 <= u <= len(units):
                        i, h = units[u - 1]
                        for c in range(prob_tiles(i)):
                            m = prob_tiles_before(i, h) + c
                            wide_ = min(TB, keys_of(i) - c * TB)
                            wait_tile(act, "p2_t", i, h, c)
                            if m >= 2:
                                act.wait_ge(pv2_done, m - 1)
                            drains(A_(prob_t[:, m % 2, 0:wide_], bank("p2_t", i, h, c)[:, 0:wide_], ACT.Copy), "p2_t", i, h, c)
                    if u < len(units):
                        i, h = units[u]
                        n = H2 * BG * g + u
                        act.wait_ge(row_max2, n + 1)
                        p = probs[:, (n % 2) * S:(n % 2) * S + keys_of(i)]
                        A_(p, p, ACT.Exp, bias=stat[:, 8 + n % 2:9 + n % 2],
                           accum_out=sums2[:, i % 2, h:h + 1]).then_inc(probs2_made, 1)
                        if h == H2 - 1:
                            act.wait_ge(pm_arg, i + 1)
                            A_(p_meta[:], p_meta[:], ACT.Exp).then_inc(pm_made, 1)

                act.wait_ge(centred, G + g + 1)
                for c in range(KC):
                    A_(sq_view(probs)[:, c, :], x_t[:, c, :], ACT.Square).then_inc(squared, 1)
                act.wait_ge(std_read, N_STD[g])
                root(("2var", g), D, 1)
                for c in range(KC):
                    act.wait_ge(scaled, G + g + 1)
                    ins = A_(x_t[:, c, :], x_t[:, c, :], ACT.Identity, scale=vec[:, VEC["ln_g2"] + c:VEC["ln_g2"] + c + 1],
                             bias=vec[:, VEC["ln_b2"] + c:VEC["ln_b2"] + c + 1])
                    if c < KC - 1:
                        step(act, ins)
                ins.then_inc(x_out, 1)

        @block.vector
        def _(dve):
            step = counter(dve_step)
            V = nc.vector
            TWO_PI = 2.0 * np.pi
            C1 = 6.28125
            C2 = float(np.round((TWO_PI - C1) * 2 ** 23) / 2 ** 23)
            C3 = float(np.float32(TWO_PI - C1 - C2))

            def rope_args(n, g):
                if n > 0:
                    dve.wait_ge(rope_made, n)
                ang, turn = tmp[:, 0, :], tmp[:, 1, :]
                fr = VEC["inv_freq"]
                step(dve, V.tensor_scalar(ang, pos_k[:, g * TB:(g + 1) * TB], vec[:, fr:fr + 1], None, ALU.mult))
                step(dve, V.tensor_scalar(turn, ang, 1.0 / TWO_PI, 12582912.0, ALU.mult, ALU.add))
                step(dve, V.tensor_scalar(turn, turn, 12582912.0, None, ALU.subtract))
                for c in (C1, C2, C3):
                    step(dve, V.scalar_tensor_tensor(out=ang, in0=turn, scalar=-c, in1=ang, op0=ALU.mult, op1=ALU.add))
                sg = VEC["rope_sign"]
                pi = float(np.nextafter(np.float32(np.pi), np.float32(0)))
                step(dve, V.tensor_scalar(ang, ang, pi, -pi, ALU.min, ALU.max))
                step(dve, V.tensor_scalar(sin[:], ang, vec[:, sg:sg + 1], None, ALU.mult))
                step(dve, V.tensor_scalar(turn, ang, float(np.pi / 2), -TWO_PI, ALU.is_gt, ALU.mult))
                step(dve, V.scalar_tensor_tensor(out=ang, in0=ang, scalar=float(np.pi / 2), in1=turn, op0=ALU.add, op1=ALU.add))
                V.tensor_scalar(cos[:], ang, pi, -pi, ALU.min, ALU.max).then_inc(rope_arg, 1)

            def rotate(first, second):
                wait_tile(dve, *first)
                drains(V.tensor_tensor(tmp[:, 0, :], bank(*first)[:], cos[:], ALU.mult), *first)
                wait_tile(dve, *second)
                drains(V.tensor_tensor(tmp[:, 1, :], bank(*second)[:], sin[:], ALU.mult), *second)
                wait_drained(dve, *first)
                wait_drained(dve, *second)

            def wide(ap, n):
                return ap.unsqueeze(1).broadcast_to([P, n, TB])

            dve.wait_ge(const_here, 16 * 7)
            step(dve, V.tensor_copy(pos_k[:], pos_i))
            step(dve, V.tensor_copy(pos_q[:], pos_qi[:]))
            for g in range(G):
                rope_args(g, g)
                dve.wait_ge(rope_made, g + 1)
                rotate(("krope", g, 0), ("krope", g, 1))
                step(dve, V.tensor_tensor(k_rope[:, g * TB:(g + 1) * TB], tmp[:, 0, :], tmp[:, 1, :], ALU.add))
                wait_drained(dve, "kv_sq", g)
                step(dve, V.reciprocal(rstd[:], std[:]))
                V.tensor_tensor(lat[:, 0:2, :], lat[:, 0:2, :], wide(rstd[:], 2), ALU.mult).then_inc(k_normed, 1)
                for h in range(H1):
                    wait_tile(dve, "k_nope", g, h)
                    drains(V.tensor_copy(k_nope[:, h, g * TB:(g + 1) * TB], bank("k_nope", g, h)[:]), "k_nope", g, h)

            def mask_of(i):
                step(dve, V.tensor_scalar(mask[:], pos_k[:], pos_q[:, i:i + 1], MASKED, ALU.is_gt, ALU.mult))

            for g in range(G):
                rope_args(G + g, g)
                dve.wait_ge(rope_made, G + g + 1)
                wait_drained(dve, "q_sq", g)
                step(dve, V.reciprocal(rstd[:], std[:]))
                V.tensor_tensor(lat[:], lat[:], wide(rstd[:], 4), ALU.mult).then_inc(q_normed, 1)
                dve.wait_ge(const_made, 5)
                for pair in range(2):
                    rotate(("q_rope", g, 2 * pair), ("q_rope", g, 2 * pair + 1))
                    for e in range(2):
                        rows = slice(e * ROPE, (e + 1) * ROPE)
                        ins = V.tensor_tensor(q_rope[rows, 2 * pair + e, :], tmp[rows, 0, :], tmp[rows, 1, :], ALU.add)
                        if (pair, e) != (1, 1):
                            step(dve, ins)
                ins.then_inc(q_rotated, 1)
                for j, w in enumerate(POOL_W):
                    dve.wait_ge(win_summed, 4 * g + j + 1)
                    src, u = u_sum[:, j % 2, HALO:], u_in[:, j, HALO:]
                    if g == 0:
                        step(dve, V.tensor_tensor(src[:, 0:HALO], src[:, 0:HALO], pool_cnt[:, j, :], ALU.mult))
                    V.scalar_tensor_tensor(out=lat[:, j, :], in0=src, scalar=1.0 / w, in1=u,
                                           op0=ALU.mult, op1=ALU.subtract).then_inc(pooled, 1)
                for j in range(4):
                    wait_tile(dve, "mix", g, j)
                    wait_drained(dve, "gate_b", g, j)
                    ps = VEC["pool_scale"] + j
                    drains(V.scalar_tensor_tensor(out=y_t[:, 4 + j, :], in0=bank("mix", g, j)[:], scalar=vec[:, ps:ps + 1],
                                                  in1=y_t[:, 4 + j, :], op0=ALU.mult, op1=ALU.mult), "mix", g, j)

                units = mla_units(g)
                dve.wait_ge(pool_step, POOL_STEPS * (g + 1))
                for u in range(len(units) + 2):
                    if u < len(units):
                        i, h = units[u]
                        n = H1 * BG * g + u
                        if h == 0:
                            mask_of(i)
                        if n >= 2:
                            wait_tile(dve, "prob_t", *prev_unit(units, u, g, 2), S // TB - 1)
                        for c in range(S // TB):
                            wait_tile(dve, "score", i, h, c)
                            drains(V.tensor_tensor_reduce(out=probs[:, (n % 2) * S + c * TB:(n % 2) * S + (c + 1) * TB],
                                                          in0=bank("score", i, h, c)[:], in1=mask[:, c * TB:(c + 1) * TB],
                                                          scale=1.0, scalar=-HUGE, op0=ALU.add, op1=ALU.max,
                                                          accum_out=stat[:, c:c + 1]), "score", i, h, c)
                        for c in range(S // TB):
                            wait_drained(dve, "score", i, h, c)
                        step(dve, V.reduce_max(stat[:, 4:5], stat[:, 0:4], AX.X))
                        V.tensor_scalar(stat[:, 8 + n % 2:9 + n % 2], stat[:, 4:5], -QK_DIM ** -0.5, None,
                                        ALU.mult).then_inc(row_max, 1)
                    if 2 <= u and units[u - 2][1] == H1 - 1:
                        i = units[u - 2][0]
                        b = i % BG
                        wait_tile(dve, "o_t", i)
                        drains(V.tensor_tensor(y_t[:, 0:4, b * P:(b + 1) * P],
                                               bank("o_t", i)[:].rearrange("p (j t) -> p j t", j=4),
                                               gate[:, :, b * P:(b + 1) * P], ALU.mult), "o_t", i)
                    if 1 <= u <= len(units) and units[u - 1][1] == H1 - 1:
                        i = units[u - 1][0]
                        dve.wait_ge(pv_done, (i + 1) * H1 * (S // TB))
                        dve.wait_ge(probs_made, (i + 1) * H1)
                        at = 16 + 4 * (i % 2)
                        step(dve, V.reciprocal(stat[:, 32:36], stat[:, at:at + 4]))
                        if i > 0:
                            wait_tile(dve, "o_t", i - 1)
                        V.tensor_tensor(o_sb[:].rearrange("p (h d) -> p h d", h=H1),
                                        o_acc[i % 2][:].rearrange("p (h d) -> p h d", h=H1),
                                        stat[:, 32:36].unsqueeze(2).broadcast_to([P, H1, P]), ALU.mult).then_inc(o_scaled, 1)

                out_norm("1", g, dve, step, V)

            second_begins(dve)
            step(dve, V.tensor_copy(lev_mask[:].rearrange("p l t -> p (l t)"), mask_i))
            wait_tile(dve, "t5_row")
            step(dve, V.tensor_copy(stat[0:H2, 40:41], bank("t5_row")[0:H2, 0:1]))
            drains(V.tensor_scalar(t5_row, bank("t5_row")[0:H2, 0:3 * P], stat[0:H2, 40:41], None, ALU.subtract), "t5_row")
            wait_drained(dve, "t5_row")
            step(dve, V.tensor_copy(t5_row, t5_row))
            V.tensor_copy(stat[0:H2, 41:42], stat[0:H2, 40:41]).then_inc(t5_made, 1)
            for j in range(4):
                wait_tile(dve, "t5", j)
                drains(V.tensor_copy(bias[:, 2 * j:2 * j + 2, :], bank("t5", j)[:].rearrange("p (h n) -> p h n", h=2)), "t5", j)
            lr = VEC["lb_raw"]
            V.tensor_tensor(lb[:, 0, :], vec[:, lr:lr + H3], vec[:, lr:lr + H3], ALU.subtract).then_inc(lb_arg, 1)
            wait_drained(dve, "m_c_sq")
            step(dve, V.reciprocal(rstd[:, 0:META], std[:, 0:META]))
            wait_drained(dve, "m_c")
            V.tensor_tensor(c_meta[:].rearrange("p (h m) -> p h m", h=H2), c_t[:, 0:META].unsqueeze(1).broadcast_to([P, H2, META]),
                            rstd[:, 0:META].unsqueeze(1).broadcast_to([P, H2, META]), ALU.mult).then_inc(c_normed, 1)
            V.tensor_copy(stat[:, 42:43], rstd[:, 0:1]).then_inc(std_read, 1)
            wait_tile(dve, "m_v")
            drains(V.tensor_tensor(v_meta[:], bank("m_v")[:], v_meta[:], ALU.mult), "m_v")
            dve.wait_ge(lb_exp, 2)
            step(dve, V.reciprocal(lb[:, 1, :], lb[:, 0, :]))
            step(dve, V.tensor_tensor(lb[:, 0, :], lb[:, 0, :], lb[:, 1, :], ALU.mult))
            step(dve, V.tensor_tensor(lb[:, 0, :], lb[:, 0, :], lb[:, 0, :], ALU.subtract))
            step(dve, V.tensor_scalar(lb[:, 1, :], lb[:, 0, :], -1.0, 1.0, ALU.mult, ALU.add))
            mf, mk, mb, me = (probs[:, o:o + H3 * META] for o in (0, 64, 128, 256))
            for h in range(H3):
                wait_drained(dve, "m_f", h)
                fh = mf[:, h * META:(h + 1) * META]
                step(dve, V.tensor_scalar(fh, fh, lb[:, 1, h:h + 1], lb[:, 0, h:h + 1], ALU.mult, ALU.add))
            step(dve, V.tensor_scalar(mk, mf, -1.0, 1.0, ALU.mult, ALU.add))
            V.tensor_scalar(mf, mf, 1e-19, None, ALU.max).then_inc(f_made, 1)
            dve.wait_ge(f_log, 1)
            for h in range(H3):
                fh = mf[:, h * META:(h + 1) * META]
                step(dve, V.tensor_tensor_scan(mb[:, h * META:(h + 1) * META], fh, fh, 0.0, ALU.add, ALU.bypass))
            mb3, me3 = (a.rearrange("p (h m) -> p h m", h=H3) for a in (mb, me))
            V.tensor_tensor(me3, mb3[:, :, META - 1:META].broadcast_to([P, H3, META]), mb3, ALU.subtract).then_inc(lev_diff_meta, 1)
            dve.wait_ge(u_meta, 1)
            V.tensor_tensor(me, me, mk, ALU.mult).then_inc(lev_diff_meta, 1)
            wait_tile(dve, "m_u")
            drains(V.tensor_copy(state[:], bank("m_u")[:].rearrange("p (h v) -> p h v", h=H3)), "m_u")
            wait_drained(dve, "m_u")
            V.memset(ha, 0.0).then_inc(u_meta, 1)

            def gates(g, pair):
                for e in range(2):
                    h = 2 * pair + e
                    wait_drained(dve, "f", g, h)
                    step(dve, V.tensor_scalar(hf[:, e, :], hf[:, e, :], lb[:, 1, h:h + 1], lb[:, 0, h:h + 1], ALU.mult, ALU.add))
                step(dve, V.tensor_scalar(hk, hf, -1.0, 1.0, ALU.mult, ALU.add))
                V.tensor_scalar(hf, hf, 1e-19, None, ALU.max).then_inc(f_made, 1)
                dve.wait_ge(f_log, 2 + 2 * g + pair)
                for e in range(2):
                    for b in range(BG):
                        src = hf[:, e, b * P:(b + 1) * P]
                        ins = V.tensor_tensor_scan(hb[:, e, b * P:(b + 1) * P], src, src, 0.0, ALU.add, ALU.bypass)
                        if (e, b) != (1, BG - 1):
                            step(dve, ins)
                ins.then_inc(f_summed, 1)

            def lev_wait(g, pair, k):
                dve.wait_ge(lev_exp, level_no(g, pair, k) + 1)

            def finish_heads(g, pair):
                dve.wait_ge(gates_made, 2 * g + 1)
                for e in range(2):
                    h = 2 * pair + e
                    wait_drained(dve, "h_sq", g, pair, e)
                    V.reciprocal(rstd[:], std[:]).then_inc(std_read, 1)
                    dve.wait_ge(std_read, H_STD[(g, h)] + 1)
                    step(dve, V.tensor_tensor(hb[:, e, :], hb[:, e, :], rstd[:], ALU.mult))
                    hg = VEC["hgrn_g"]
                    V.scalar_tensor_tensor(out=y_t[:, 4 + h, :], in0=hb[:, e, :], scalar=vec[:, hg:hg + 1],
                                           in1=y_t[:, 4 + h, :], op0=ALU.mult, op1=ALU.mult).then_inc(h_free, 1)

            def add_index(i):
                if not needs_topk(i):
                    return
                m = index_adds_before(i)
                n = keys_of(i)
                for c, (at, wide_) in enumerate(index_chunks(i)):
                    dst = index[:, at:at + wide_]
                    for h in range(HI):
                        wait_drained(dve, "index", i, c, h)
                        w = wi[:, i % BG, h:h + 1]
                        src = tmp[:, m % 2, 0:wide_]
                        if h == 0:
                            V.tensor_scalar(dst, src, w, None, ALU.mult).then_inc(index_added, 1)
                        else:
                            V.scalar_tensor_tensor(out=dst, in0=src, scalar=w, in1=dst, op0=ALU.mult, op1=ALU.add)\
                                .then_inc(index_added, 1)
                        m += 1
                        dve.wait_ge(index_added, m)
                low, high, span = stat[:, 48:49], stat[:, 49:50], stat[:, 50:51]
                step(dve, V.tensor_reduce(low, index[:, 0:n], AX.X, ALU.min))
                step(dve, V.tensor_reduce(high, index[:, 0:n], AX.X, ALU.max))
                step(dve, V.tensor_tensor(index[:, n - P:n], index[:, n - P:n], causal[:], ALU.add))
                step(dve, V.tensor_tensor(span, high, low, ALU.subtract))
                step(dve, V.tensor_scalar(steps_[:], halves[:], span, None, ALU.mult))
                step(dve, V.tensor_tensor(mids[:, 0:1], low, steps_[:, 0:1], ALU.add))

            def bisect(i, first, last):
                if not needs_topk(i):
                    return
                n = keys_of(i)
                for r in range(first, min(last, ROUNDS)):
                    step(dve, V.tensor_scalar(above[:, 0:n], index[:, 0:n], mids[:, r:r + 1], 0.0, ALU.is_ge, ALU.add,
                                              accum_out=counts[:, r:r + 1]))
                    if r + 1 < ROUNDS:
                        step(dve, V.scalar_tensor_tensor(out=stat[:, 51:52], in0=counts[:, r:r + 1], scalar=TOPK - 0.5,
                                                         in1=steps_[:, r:r + 1], op0=ALU.is_ge, op1=ALU.mult))
                        step(dve, V.scalar_tensor_tensor(out=mids[:, r + 1:r + 2], in0=stat[:, 51:52], scalar=steps_[:, r + 1:r + 2],
                                                         in1=mids[:, r:r + 1], op0=ALU.subtract, op1=ALU.add))

            def select(i):
                n = keys_of(i)
                out = sel[:, i % 2, 0:n]
                if not needs_topk(i):
                    if n > P:
                        step(dve, V.memset(sel[:, i % 2, 0:n - P], 0.0))
                    V.tensor_copy(sel[:, i % 2, n - P:n], causal[:]).then_inc(sel_made, 1)
                    return
                low, high, quota = stat[:, 48:49], stat[:, 49:50], stat[:, 52:53]
                step(dve, V.tensor_scalar(steps_[:], counts[:], TOPK - 0.5, -HUGE, ALU.is_lt, ALU.mult))
                step(dve, V.tensor_tensor(steps_[:], steps_[:], mids[:], ALU.add))
                step(dve, V.reduce_max(stat[:, 53:54], steps_[:], AX.X))
                step(dve, V.tensor_tensor(low, low, stat[:, 53:54], ALU.max))
                step(dve, V.tensor_scalar(steps_[:], counts[:], TOPK - 0.5, HUGE, ALU.is_ge, ALU.mult))
                step(dve, V.tensor_tensor(steps_[:], steps_[:], mids[:], ALU.add))
                step(dve, V.tensor_reduce(stat[:, 54:55], steps_[:], AX.X, ALU.min))
                step(dve, V.tensor_tensor(high, high, stat[:, 54:55], ALU.min))
                x = index[:, 0:n]
                step(dve, V.tensor_scalar(above[:, 0:n], x, high, 0.0, ALU.is_gt, ALU.add, accum_out=stat[:, 55:56]))
                step(dve, V.tensor_scalar(quota, stat[:, 55:56], -1.0, float(TOPK), ALU.mult, ALU.add))
                step(dve, V.scalar_tensor_tensor(out=band[:, 0:n], in0=x, scalar=low, in1=above[:, 0:n], op0=ALU.is_ge, op1=ALU.subtract))
                step(dve, V.tensor_tensor_scan(rank[:, 0:n], band[:, 0:n], band[:, 0:n], 0.0, ALU.add, ALU.bypass))
                step(dve, V.scalar_tensor_tensor(out=band[:, 0:n], in0=rank[:, 0:n], scalar=quota, in1=band[:, 0:n],
                                                 op0=ALU.is_le, op1=ALU.mult))
                step(dve, V.tensor_tensor(out, above[:, 0:n], band[:, 0:n], ALU.add))
                V.tensor_scalar(out, out, -MASKED, MASKED, ALU.mult, ALU.add).then_inc(sel_made, 1)

            for g in range(G):
                for st in second_steps(g):
                    kind = st[0]
                    if kind == "i":
                        gates(g, 0)
                    elif kind == "c_sq":
                        wait_drained(dve, *st)
                        V.reciprocal(rstd[:], std[:]).then_inc(std_read, 1)
                        dve.wait_ge(std_read, C_STD[g] + 1)
                        c_g = c_t[:, g * TB:(g + 1) * TB]
                        V.tensor_tensor(c_g, c_g, rstd[:], ALU.mult).then_inc(c_normed, 1)
                    elif kind == "ki":
                        wait_tile(dve, *st)
                        drains(V.tensor_copy(ki[:, g * TB:(g + 1) * TB], bank(*st)[:]), *st)
                    elif kind == "qi":
                        wait_tile(dve, *st)
                        dve.wait_ge(const_made, 6)
                        step(dve, V.tensor_copy(qi[0:DH2, 2 * st[2], :], bank(*st)[0:DH2, :]))
                        drains(V.tensor_copy(qi[DH2:P, 2 * st[2] + 1, :], bank(*st)[DH2:P, :]), *st)
                    elif kind == "wi":
                        wait_tile(dve, *st)
                        drains(V.tensor_scalar(wi[:].rearrange("p b h -> p (b h)"), bank(*st)[:, 0:BG * HI], HI ** -0.5, None,
                                               ALU.mult), *st)
                    elif kind == "level":
                        pair, lev = st[2], st[3]
                        if lev == 0:
                            if pair == 1:
                                gates(g, 1)
                            elif g > 0:
                                step(dve, V.memset(ha, 0.0))
                            for e in range(2):
                                wait_drained(dve, "hq", g, 2 * pair + e)
                        if lev < len(LEVELS):
                            w = LEVELS[lev]
                            if lev > 0:
                                wait_tile(dve, "level", g, pair, lev - 1, 1)
                            lev_wait(g, pair, lev)
                            x, e_, k_, q_ = (halved(a, w) for a in (hf, he, hk, hqb))
                            step(dve, V.tensor_tensor(x[:, :, 0:w], e_[:, :, 0:w], k_[:, :, 0:w], ALU.mult))
                            V.tensor_tensor(x[:, :, w:2 * w], e_[:, :, w:2 * w], q_[:, :, w:2 * w], ALU.mult).then_inc(lev_made, 1)
                        for e in range(2):
                            wait_tile(dve, "level", g, pair, lev, e)
                            if lev > 0:
                                wait_drained(dve, "level", g, pair, lev - 1, e)
                            drains(V.copy_predicated(ha[:, e, :].rearrange("p (b t) -> p b t", b=BG),
                                                     lev_mask[:, lev, :].unsqueeze(1).broadcast_to([P, BG, P]),
                                                     bank("level", g, pair, lev, e)[:].rearrange("p (b t) -> p b t", b=BG)),
                                   "level", g, pair, lev, e)
                    elif kind == "state":
                        pair = st[2]
                        lev_wait(g, pair, len(LEVELS))
                        V.tensor_tensor(hf, he, hqb, ALU.mult).then_inc(lev_made, 1)
                        lev_wait(g, pair, len(LEVELS) + 1)
                        V.tensor_tensor(he, he, hk, ALU.mult).then_inc(lev_made, 1)
                        for b in range(BG):
                            name = ("u_h", g, pair, b)
                            wait_tile(dve, *name)
                            for e in range(2):
                                h = 2 * pair + e
                                ins = V.scalar_tensor_tensor(out=state[:, h, :], in0=state[:, h, :], scalar=decay[:, e, b:b + 1],
                                                             in1=bank(*name)[:, e * P:(e + 1) * P], op0=ALU.mult, op1=ALU.add)
                                if e == 0:
                                    step(dve, ins)
                            drains(ins, *name)
                        finish_heads(g, pair)

                units = dsa_units(g)
                for st in second_steps(g):
                    pass
                wait_tile(dve, *tiles_of(st)[-1])
                wait_drained(dve, "wi", g)
                add_index(BG * g)
                bisect(BG * g, 0, ROUNDS)
                select(BG * g)
                for u in range(len(units) + 4):
                    if u < len(units):
                        i, h = units[u]
                        n = H2 * BG * g + u
                        if h == 0:
                            if i + 1 < BG * (g + 1):
                                add_index(i + 1)
                            wait_tile(dve, "score_m", i)
                            src = bank("score_m", i)[:, 0:P].rearrange("p (h m) -> p h m", h=H2)
                            if i == 0:
                                drains(V.tensor_tensor(s_meta[:], src, bias[:, :, P - META:P], ALU.add), "score_m", i)
                            else:
                                drains(V.tensor_copy(s_meta[:], src), "score_m", i)
                            wait_drained(dve, "score_m", i)
                            step(dve, V.tensor_reduce(mx[:, :, 0:1], s_meta[:], AX.X, ALU.max))
                        if u >= 2:
                            pi_, ph = units[u - 2]
                            wait_tile(dve, "p2_t", pi_, ph, prob_tiles(pi_) - 1)
                        base = (n % 2) * S
                        chunks = far_chunks(i)
                        for c, (at, wide_) in enumerate(chunks):
                            wait_tile(dve, "far", i, h, c)
                            drains(V.tensor_tensor_reduce(out=probs[:, base + at:base + at + wide_], in0=bank("far", i, h, c)[:, 0:wide_],
                                                          in1=sel[:, i % 2, at:at + wide_], scale=1.0, scalar=-HUGE, op0=ALU.add,
                                                          op1=ALU.max, accum_out=mx[:, h, 1 + c:2 + c]), "far", i, h, c)
                        wn, last = near_width(i), 1 + len(chunks)
                        wait_tile(dve, "near", i, h)
                        dve.wait_ge(near_made, n + 1)
                        drains(V.tensor_tensor_reduce(out=probs[:, base + keys_of(i) - wn:base + keys_of(i)],
                                                      in0=bank("near", i, h)[:, 0:wn], in1=near[:, h, NEAR - wn:], scale=1.0,
                                                      scalar=-HUGE, op0=ALU.add, op1=ALU.max,
                                                      accum_out=mx[:, h, last:last + 1]), "near", i, h)
                        for c in range(len(chunks)):
                            wait_drained(dve, "far", i, h, c)
                        wait_drained(dve, "near", i, h)
                        step(dve, V.reduce_max(m2[:, i % 2, h:h + 1], mx[:, h, 0:last + 1], AX.X))
                        V.tensor_scalar(stat[:, 8 + n % 2:9 + n % 2], m2[:, i % 2, h:h + 1], -1.0, None, ALU.mult).then_inc(row_max2, 1)
                        if h == H2 - 1:
                            V.tensor_tensor(p_meta[:].rearrange("p (h m) -> p h m", h=H2), s_meta[:],
                                            m2[:, i % 2, :].unsqueeze(2).broadcast_to([P, H2, META]), ALU.subtract).then_inc(pm_arg, 1)
                        if i + 1 < BG * (g + 1):
                            if h < H2 - 1:
                                bisect(i + 1, 4 * h, 4 * h + 4)
                            else:
                                select(i + 1)
                    if ended(units, u, 3) is not None:
                        i = ended(units, u, 3)
                        b = i % BG
                        dve.wait_ge(gates_made, 2 * g + 2)
                        wait_tile(dve, "o2_t", i)
                        drains(V.tensor_tensor(y_t[:, 0:4, b * P:(b + 1) * P],
                                               bank("o2_t", i)[:].rearrange("p (j t) -> p j t", j=4),
                                               gate[:, :, b * P:(b + 1) * P], ALU.mult), "o2_t", i)
                    if ended(units, u, 2) is not None:
                        i = ended(units, u, 2)
                        dve.wait_ge(pm_made, i + 1)
                        step(dve, V.tensor_reduce(stat[:, 24:32], p_meta[:].rearrange("p (h m) -> p h m", h=H2), AX.X, ALU.add))
                        dve.wait_ge(probs2_made, H2 * (i + 1))
                        step(dve, V.tensor_tensor(stat[:, 24:32], stat[:, 24:32], sums2[:, i % 2, :], ALU.add))
                        step(dve, V.reciprocal(stat[:, 32:40], stat[:, 24:32]))
                        dve.wait_ge(pvm_done, i + 1)
                        V.tensor_tensor(o_sb[:].rearrange("p (h d) -> p h d", h=H2),
                                        o_acc[i % 2][:].rearrange("p (h d) -> p h d", h=H2),
                                        stat[:, 32:40].unsqueeze(2).broadcast_to([P, H2, DH2]), ALU.mult).then_inc(o2_scaled, 1)
                dve.wait_ge(x_here, 32 * (2 * G + 2 * g + 2))
                out_norm("2", g, dve, step, V)

        @block.tensor
        def _(pe):
            M = nc.tensor.matmul
            done = [0]

            def claim(*name):
                assert T[name] == done[0]
                done[0] += 1
                n = T[name]
                if n >= RING:
                    pe.wait_ge(drained[n % RING], n // RING)

            def project(name, rhs, chunks):
                n = WSLOT[name]
                pe.wait_ge(w_here[n % SLOTS], 16 * (n // SLOTS + 1))
                claim(*name)
                for k in range(chunks):
                    ins = M(bank(*name)[:], ring[n % SLOTS][:, k * P:(k + 1) * P], rhs[:, k, :],
                            start=(k == 0), stop=(k == chunks - 1))
                ins.then_inc(tile_ready, 1)

            def squares(name, rhs, chunks):
                claim(*name)
                for k in range(chunks):
                    ins = M(bank(*name)[:], ones[:], rhs[:, k, :], start=(k == 0), stop=(k == chunks - 1))
                ins.then_inc(tile_ready, 1)

            pe.wait_ge(const_here, 16 * 7)
            pe.wait_ge(const_made, 5)
            for g in range(G):
                pe.wait_ge(x_here, 32 * (g + 1))
                for j in range(2):
                    project(("kv", g, j), x_t, KC)
                for j in range(2):
                    project(("krope", g, j), x_t, KC)
                for j in range(2):
                    wait_drained(pe, "kv", g, j)
                squares(("kv_sq", g), y_t, 2)
                pe.wait_ge(k_normed, g + 1)
                for h in range(H1):
                    name = ("k_nope", g, h)
                    claim(*name)
                    for j in range(2):
                        ins = M(bank(*name)[:], w_ukv[:, j, h * P:(h + 1) * P], lat[:, j, :], start=(j == 0), stop=(j == 1))
                    ins.then_inc(tile_ready, 1)
                for b in range(BG):
                    name = ("v", g, b)
                    claim(*name)
                    for j in range(2):
                        ins = M(bank(*name)[:], lat[:, j, b * P:(b + 1) * P], w_ukv[:, 2 + j, :], start=(j == 0), stop=(j == 1))
                    ins.then_inc(tile_ready, 1)

            for g in range(G):
                pe.wait_ge(x_here, 32 * (G + g + 1))
                for j in range(4):
                    project(("xq", g, j), x_t, KC)
                for j in range(4):
                    wait_drained(pe, "xq", g, j)
                squares(("q_sq", g), y_t, 4)
                pe.wait_ge(q_normed, g + 1)
                for h in range(H1):
                    project(("q_nope", g, h), lat, 4)
                for j in range(4):
                    project(("q_rope", g, j), lat, 4)
                for tag in ("gate_a", "u", "gate_b"):
                    for j in range(4):
                        project((tag, g, j), x_t, KC)
                for j in range(4):
                    name = ("mix", g, j)
                    pe.wait_ge(pooled, 4 * g + j + 1)
                    claim(*name)
                    M(bank(*name)[:], pool_w[:, j, :], lat[:, j, :], start=True, stop=True).then_inc(tile_ready, 1)

                units = mla_units(g)
                for u in range(len(units) + 2):
                    if u < len(units):
                        i, h = units[u]
                        b = i % BG
                        if u == 0:
                            for hh in range(H1):
                                wait_drained(pe, "q_nope", g, hh)
                            pe.wait_ge(q_rotated, g + 1)
                        if g == 0 and u == 0:
                            for hh in range(H1):
                                wait_drained(pe, "k_nope", G - 1, hh)
                        for c in range(S // TB):
                            name = ("score", i, h, c)
                            claim(*name)
                            M(bank(*name)[:], q_nope[:, h, b * P:(b + 1) * P], k_nope[:, h, c * TB:(c + 1) * TB],
                              start=True, stop=False)
                            M(bank(*name)[:], q_rope[:, h, b * P:(b + 1) * P],
                              k_rope[:, c * TB:(c + 1) * TB], start=False, stop=True).then_inc(tile_ready, 1)
                    if 2 <= u and units[u - 2][1] == H1 - 1:
                        i = units[u - 2][0]
                        pe.wait_ge(o_scaled, i + 1)
                        claim("o_t", i)
                        for j in range(4):
                            ins = nc.tensor.transpose(bank("o_t", i)[:, j * P:(j + 1) * P], o_sb[:, j * P:(j + 1) * P], ident[:])
                        ins.then_inc(tile_ready, 1)
                    if 1 <= u <= len(units):
                        i, h = units[u - 1]
                        n = H1 * BG * g + u - 1
                        pe.wait_ge(probs_made, n + 1)
                        if h == 0 and i >= 2:
                            pe.wait_ge(o_scaled, i - 1)

                        def transposes(c):
                            name = ("prob_t", i, h, c)
                            claim(*name)
                            for k in range(BG):
                                col = (n % 2) * S + c * TB + k * P
                                ins = nc.tensor.transpose(bank(*name)[:, k * P:(k + 1) * P], probs[:, col:col + P], ident[:])
                            ins.then_inc(tile_ready, 1)

                        def values(c):
                            wait_drained(pe, "prob_t", i, h, c)
                            m = n * (S // TB) + c
                            for k in range(BG):
                                ins = M(o_acc[i % 2][:, h * P:(h + 1) * P], prob_t[:, m % 2, k * P:(k + 1) * P],
                                        val[:, c * BG + k, h * P:(h + 1) * P],
                                        start=(c == 0 and k == 0), stop=(c == S // TB - 1 and k == BG - 1))
                            ins.then_inc(pv_done, 1)

                        transposes(0)
                        for c in range(1, S // TB):
                            transposes(c)
                            values(c - 1)
                        values(S // TB - 1)

                for b in range(BG):
                    wait_drained(pe, "o_t", BG * g + b)
                for j in range(4):
                    wait_drained(pe, "mix", g, j)
                for c in range(KC):
                    project(("1out", g, c), y_t, KC)
                for c in range(KC):
                    wait_drained(pe, "1out", g, c)
                squares(("1mean", g), x_t, KC)
                claim("1var", g)
                for c in range(KC):
                    pe.wait_ge(squared, KC * g + c + 1)
                    ins = M(bank("1var", g)[:], ones[:], sq_view(probs)[:, c, :], start=(c == 0), stop=(c == KC - 1))
                ins.then_inc(tile_ready, 1)

            second_begins(pe)
            claim("t5_row")
            M(bank("t5_row")[0:H2, 0:3 * P], rel, t5_hot, start=True, stop=True).then_inc(tile_ready, 1)
            pe.wait_ge(t5_here, 32)
            for j in range(4):
                claim("t5", j)
                M(bank("t5", j)[:], anti, index[:, j * TB:(j + 1) * TB], start=True, stop=True).then_inc(tile_ready, 1)

            def weights(key):
                n = WSLOT[key]
                pe.wait_ge(w_here[n % SLOTS], 16 * (n // SLOTS + 1))
                return ring[n % SLOTS]

            def meta_features(name):
                w = weights(name)
                claim(*name)
                for k in range(KC):
                    ins = M(bank(*name)[:, 0:META], w[:, k * P:(k + 1) * P], x_meta[:, k, :], start=(k == 0), stop=(k == KC - 1))
                ins.then_inc(tile_ready, 1)

            meta_features(("m_c",))
            pe.wait_ge(lb_exp, 1)
            claim("m_c_sq")
            M(bank("m_c_sq")[:, 0:META], ones[:], tmp[:, 0, 0:META], start=True, stop=True).then_inc(tile_ready, 1)
            w = weights(("w_uv",))
            pe.wait_ge(c_normed, 1)
            claim("m_v")
            M(bank("m_v")[:], c_meta[:], w[:, 0:TB], start=True, stop=True).then_inc(tile_ready, 1)
            for h in range(H3):
                meta_features(("m_f", h))
            claim("m_i")
            for k in range(KC):
                w = weights(("w_i", (), k // 2))
                ins = M(bank("m_i")[0:META, :], x_meta[:, k, :], w[:, (k % 2) * TB:(k % 2 + 1) * TB], start=(k == 0), stop=(k == KC - 1))
            ins.then_inc(tile_ready, 1)
            pe.wait_ge(lev_diff_meta, 2)
            claim("m_k_t")
            for h in range(H3):
                ins = nc.tensor.transpose(bank("m_k_t")[0:META, h * P:(h + 1) * P], probs[:, 256 + h * META:256 + (h + 1) * META], ident[:])
            ins.then_inc(tile_ready, 1)
            wait_drained(pe, "m_k_t")
            wait_drained(pe, "m_i")
            claim("m_u")
            for h in range(H3):
                ins = M(bank("m_u")[:, h * P:(h + 1) * P], kd_t[0:META, 0, h * P:(h + 1) * P], h_i[0:META, 0, h * P:(h + 1) * P],
                        start=True, stop=True)
            ins.then_inc(tile_ready, 1)

            for g in range(G):
                pe.wait_ge(x_here, 32 * (2 * G + 2 * g + 1))
                for st in second_steps(g):
                    kind = st[0]
                    if kind in SECOND_CHUNKS:
                        project(st, x_t, KC)
                    elif kind == "i":
                        for b in range(BG):
                            claim("i", g, b)
                        for j in range(4):
                            w = weights(("w_i", (g,), j))
                            for b in range(BG):
                                for k in (2 * j, 2 * j + 1):
                                    ins = M(bank("i", g, b)[:], x_t[:, k, b * P:(b + 1) * P], w[:, (k % 2) * TB:(k % 2 + 1) * TB],
                                            start=(k == 0), stop=(k == KC - 1))
                                if j == 3:
                                    ins.then_inc(tile_ready, 1)
                    elif kind == "c_sq":
                        wait_drained(pe, "c", g)
                        claim(*st)
                        M(bank(*st)[:], ones[:], tmp[:, 0, :], start=True, stop=True).then_inc(tile_ready, 1)
                        pe.wait_ge(c_normed, g + 2)
                    elif kind == "ql":
                        w = weights(("w_uk", g))
                        claim(*st)
                        wait_drained(pe, "qa", g, st[2] // 2)
                        M(bank(*st)[:], w[:, st[2] * P:(st[2] + 1) * P], qa[:, st[2] // 2, :], start=True, stop=True).then_inc(tile_ready, 1)
                    elif kind == "v2":
                        w = weights(("w_uv", g))
                        claim(*st)
                        at = g * TB + st[2] * P
                        M(bank(*st)[:], c_t[:, at:at + P], w[:, 0:TB], start=True, stop=True).then_inc(tile_ready, 1)
                    elif kind == "wi":
                        claim(*st)
                        for b in range(BG):
                            for k in range(KC):
                                ins = M(bank(*st)[:, b * HI:(b + 1) * HI], x_t[:, k, b * P:(b + 1) * P], w_wi[:, k, :],
                                        start=(k == 0), stop=(k == KC - 1))
                        ins.then_inc(tile_ready, 1)
                    elif kind == "level":
                        pair, lev = st[2], st[3]
                        if lev < len(LEVELS):
                            pe.wait_ge(lev_made, level_no(g, pair, lev) + 1)
                        for e in range(2):
                            claim(*st, e)
                            for b in range(BG):
                                cols = slice(b * P, (b + 1) * P)
                                keys, queries = (hf, hf) if lev < len(LEVELS) else (hk, hqb)
                                ins = M(bank(*st, e)[:, cols], keys[:, e, cols], queries[:, e, cols], start=True, stop=True)
                            ins.then_inc(tile_ready, 1)
                    elif kind == "state":
                        pair = st[2]
                        pe.wait_ge(lev_made, level_no(g, pair, len(LEVELS) + 1) + 1)
                        for b in range(BG):
                            name = ("kd_t", g, pair, b)
                            claim(*name)
                            for e in range(2):
                                ins = nc.tensor.transpose(bank(*name)[:, e * P:(e + 1) * P], he[:, e, b * P:(b + 1) * P], ident[:])
                            ins.then_inc(tile_ready, 1)
                        for e in range(2):
                            wait_drained(pe, "level", g, pair, len(LEVELS), e)
                        for b in range(BG):
                            wait_drained(pe, "i", g, b)
                        for b in range(BG):
                            cols = slice(b * P, (b + 1) * P)
                            if b > 0:
                                wait_drained(pe, "u_h", g, pair, b - 1)
                            claim("o_h", g, pair, b)
                            for e in range(2):
                                h = 2 * pair + e
                                dst = bank("o_h", g, pair, b)[:, e * P:(e + 1) * P]
                                M(dst, h_i[:, b, h * P:(h + 1) * P], ha[:, e, cols], start=True, stop=False)
                                ins = M(dst, state[:, h, :], hf[:, e, cols], start=False, stop=True)
                            ins.then_inc(tile_ready, 1)
                            wait_drained(pe, "kd_t", g, pair, b)
                            claim("u_h", g, pair, b)
                            for e in range(2):
                                h = 2 * pair + e
                                ins = M(bank("u_h", g, pair, b)[:, e * P:(e + 1) * P],
                                        kd_t[:, b // 2, (b % 2) * 256 + e * P:(b % 2) * 256 + (e + 1) * P],
                                        h_i[:, b, h * P:(h + 1) * P], start=True, stop=True)
                            ins.then_inc(tile_ready, 1)
                        pe.wait_ge(o_squared, 2 * g + pair + 1)
                        for e in range(2):
                            claim("h_sq", g, pair, e)
                            M(bank("h_sq", g, pair, e)[:], ones[:], hk[:, e, :], start=True, stop=True).then_inc(tile_ready, 1)

                def index_scores(i):
                    if not needs_topk(i):
                        return
                    b = i % BG
                    for c, (at, wide_) in enumerate(index_chunks(i)):
                        for h in range(HI):
                            claim("index", i, c, h)
                            M(bank("index", i, c, h)[:, 0:wide_], qi[:, h, b * P:(b + 1) * P], ki[:, at:at + wide_], start=True, stop=True).then_inc(tile_ready, 1)

                wait_drained(pe, "ki", g)
                for j in range(2):
                    wait_drained(pe, "qi", g, j)
                for h in range(H2):
                    wait_drained(pe, "ql", g, h)
                for b in range(BG):
                    wait_drained(pe, "v2", g, b)
                units = dsa_units(g)
                index_scores(BG * g)
                for u in range(len(units) + 4):
                    if u < len(units):
                        i, h = units[u]
                        b = i % BG
                        cols = slice(b * P, (b + 1) * P)
                        if h == 0:
                            if i + 1 < BG * (g + 1):
                                index_scores(i + 1)
                            claim("score_m", i)
                            for hh in range(H2):
                                ins = M(bank("score_m", i)[:, hh * META:(hh + 1) * META], ql[:, hh, cols], c_meta[:, 0:META],
                                        start=True, stop=True)
                            ins.then_inc(tile_ready, 1)
                        query = ql[:, h, cols]
                        for c, (at, wide_) in enumerate(far_chunks(i)):
                            claim("far", i, h, c)
                            M(bank("far", i, h, c)[:, 0:wide_], query, c_t[:, at:at + wide_],
                              start=True, stop=True).then_inc(tile_ready, 1)
                        wn, n_keys = near_width(i), keys_of(i)
                        claim("near", i, h)
                        M(bank("near", i, h)[:, 0:wn], query, c_t[:, n_keys - wn:n_keys],
                          start=True, stop=True).then_inc(tile_ready, 1)
                    over = ended(units, u, 2)
                    if over is not None:
                        pe.wait_ge(pm_made, over + 1)
                        claim("pm_t", over)
                        nc.tensor.transpose(bank("pm_t", over)[:, 0:P], p_meta[:], ident[:]).then_inc(tile_ready, 1)
                        wait_drained(pe, "pm_t", over)
                        M(o_acc[over % 2][:], pm_t[:], v_meta[:], start=False, stop=True, skip_group_check=True).then_inc(pvm_done, 1)
                    if 1 <= u <= len(units):
                        i, h = units[u - 1]
                        n = H2 * BG * g + u - 1
                        pe.wait_ge(probs2_made, n + 1)
                        if h == 0 and i >= 2:
                            pe.wait_ge(o2_scaled, i - 1)
                        count = prob_tiles(i)

                        def transposes2(c):
                            claim("p2_t", i, h, c)
                            for k in range(c * BG, min(c * BG + BG, i + 1)):
                                ins = nc.tensor.transpose(bank("p2_t", i, h, c)[:, (k % BG) * P:(k % BG + 1) * P],
                                                          probs[:, (n % 2) * S + k * P:(n % 2) * S + (k + 1) * P], ident[:])
                            ins.then_inc(tile_ready, 1)

                        def values2(c):
                            wait_drained(pe, "p2_t", i, h, c)
                            m = prob_tiles_before(i, h) + c
                            for k in range(c * BG, min(c * BG + BG, i + 1)):
                                ins = M(o_acc[i % 2][:, h * DH2:(h + 1) * DH2], prob_t[:, m % 2, (k % BG) * P:(k % BG + 1) * P],
                                        v2[:, k, h * DH2:(h + 1) * DH2], start=(h == 0 and k == 0), stop=False, skip_group_check=True)
                            ins.then_inc(pv2_done, 1)

                        transposes2(0)
                        for c in range(1, count):
                            transposes2(c)
                            values2(c - 1)
                        values2(count - 1)
                    over = ended(units, u, 3)
                    if over is not None:
                        pe.wait_ge(o2_scaled, over + 1)
                        claim("o2_t", over)
                        for j in range(4):
                            ins = nc.tensor.transpose(bank("o2_t", over)[:, j * P:(j + 1) * P], o_sb[:, j * P:(j + 1) * P], ident[:])
                        ins.then_inc(tile_ready, 1)

                for b in range(BG):
                    wait_drained(pe, "o2_t", BG * g + b)
                pe.wait_ge(h_free, H3 * (g + 1))
                for c in range(KC):
                    project(("2out", g, c), y_t, KC)
                for c in range(KC):
                    wait_drained(pe, "2out", g, c)
                squares(("2mean", g), x_t, KC)
                claim("2var", g)
                for c in range(KC):
                    pe.wait_ge(squared, KC * (G + g) + c + 1)
                    ins = M(bank("2var", g)[:], ones[:], sq_view(probs)[:, c, :], start=(c == 0), stop=(c == KC - 1))
                ins.then_inc(tile_ready, 1)
            assert done[0] == len(TILES)


def tiled(w, cols):
    k = w.shape[0] // P
    return np.ascontiguousarray(w[:, cols].reshape(k, P, len(cols)).transpose(1, 0, 2).reshape(P, k * len(cols)))


def tokens_last(x):
    return np.ascontiguousarray(x.reshape(KC, P, x.shape[1]).transpose(1, 0, 2))


def t5_bucket(dist):
    n = np.maximum(dist, 0)
    large = 16 + (np.log(np.maximum(n, 1).astype(np.float32) / 16) / np.log(8.0) * 16).astype(np.int32)
    return np.where(n < 16, n, np.minimum(large, 31))


def columns(v):
    return v.reshape(-1, P).T


def lay_out(inp):
    ar = np.arange
    w_in = np.asarray(inp["w_in"])
    rope0 = QR + KVR
    straight = np.concatenate([ar(ROPE), ar(ROPE)])
    swapped = (straight + ROPE // 2) % ROPE
    kv_cols = [QR + ar(P), QR + P + ar(P), rope0 + straight, rope0 + swapped]
    q_cols = [j * P + ar(P) for j in range(4)] + [rope0 + ROPE + j * P + ar(P) for j in range(12)]
    w_uq = np.asarray(inp["w_uq"])
    uq_cols = [h * QK_DIM + ar(P) for h in range(H1)]
    for pair in range(2):
        for s in (ar(ROPE), (ar(ROPE) + ROPE // 2) % ROPE):
            uq_cols.append(np.concatenate([(2 * pair + e) * QK_DIM + P + s for e in range(2)]))
    w_ukv = np.asarray(inp["w_ukv"]).reshape(2, P, H1, 2, P)
    freq = (10000.0 ** (-np.arange(ROPE // 2) / (ROPE // 2))).astype(np.float32)
    sign = np.concatenate([-np.ones(ROPE // 2), np.ones(ROPE // 2)]).astype(np.float32)
    vecs = {"q_g": inp["q_norm_g"], "kv_g": inp["kv_norm_g"], "pool_scale": inp["pool_scale"], "ln_g": inp["ln_g"][0],
            "ln_b": inp["ln_b"][0], "kv_g2": inp["kv_norm_g_2"][0], "hgrn_g": inp["hgrn_norm_g_2"][0],
            "ln_g2": inp["ln_g_2"][0], "ln_b2": inp["ln_b_2"][0], "lb_raw": inp["hgrn_lb_raw_2"][0],
            "inv_freq": np.tile(freq, 4), "rope_sign": np.tile(sign, 2)}
    cnt = np.zeros((P, 4, HALO), np.float32)
    for j, w in enumerate(POOL_W):
        cnt[:, j, :] = w / np.minimum(np.arange(HALO) + 1, w)
    sizes = (512, 128, 256, 64, 4, 512, 512, 512, 512, 512)
    q0, c0, qi0, ki0, wi0, ga0, hq0, hf0, hi0, gh0 = np.cumsum((0,) + sizes[:-1])
    w2 = np.asarray(inp["w_in_2"])[0]
    cols2 = [c0 + ar(P), ki0 + np.tile(ar(DH2), 2)] + [qi0 + j * P + ar(P) for j in range(2)]
    for start in (q0, ga0, hq0, hf0, gh0):
        cols2 += [start + j * P + ar(P) for j in range(4)]
    w_uk = np.zeros((2, DH2, H2, P), np.float32)
    for h in range(H2):
        w_uk[h % 2, :, h] = np.asarray(inp["w_uk_2"])[0, h]
    w_uv = np.asarray(inp["w_uv_2"])[0].transpose(1, 0, 2).reshape(P, TB)
    dist = NEAR - 1 - np.arange(3 * P)
    hot = np.zeros((32, 3 * P), np.float32)
    hot[t5_bucket(dist), np.arange(3 * P)] = 1
    s, t = np.arange(P)[:, None], np.arange(P)[None, :]
    levels = [(s // (2 * w) == t // (2 * w)) & (s % (2 * w) < w) & (t % (2 * w) >= w) for w in LEVELS] + [s == t]
    return {
        "w_in2": np.stack([tiled(w2, c) for c in cols2]),
        "w_uk": w_uk.reshape(1, P, H2 * P),
        "w_uv": np.ascontiguousarray(w_uv)[None],
        "w_i": np.stack([tiled(w2[2 * P * j:2 * P * (j + 1)], hi0 + ar(TB)) for j in range(4)]),
        "w_wi": np.ascontiguousarray(w2[:, wi0:wi0 + HI].reshape(KC, P, HI).transpose(1, 0, 2)),
        "w_out2": np.stack([tiled(np.asarray(inp["w_out_2"])[0], c * P + ar(P)) for c in range(KC)]),
        "meta_t": tokens_last(np.asarray(inp["meta_tokens_2"]).T),
        "rel": np.asarray(inp["rel_bias_2"]),
        "t5_hot": hot,
        "anti": np.ascontiguousarray(np.eye(P, dtype=np.float32)[::-1]),
        "causal": np.where(s >= t, 0.0, MASKED).astype(np.float32),
        "lev_mask": np.stack(levels, axis=1).astype(np.int32).reshape(P, -1),
        "halves": np.tile((0.5 ** (1 + np.arange(ROUNDS))).astype(np.float32), (P, 1)),
        "block_diag": (np.arange(P)[:, None] // META == np.arange(TB)[None, :] // DH2).astype(np.float32),
        "x_t": tokens_last(np.asarray(inp["x"])[0].T),
        "pos_k": np.asarray(inp["positions"]),
        "pos_q": np.ascontiguousarray(np.asarray(inp["positions"])[0].reshape(NB, P).T),
        "w_in_kv": np.stack([tiled(w_in, c) for c in kv_cols]),
        "w_in_q": np.stack([tiled(w_in, c) for c in q_cols]),
        "w_uq": np.stack([tiled(w_uq, c) for c in uq_cols]),
        "w_ukv": np.ascontiguousarray(w_ukv.transpose(3, 0, 1, 2, 4).reshape(4, P, TB).transpose(1, 0, 2)),
        "pool_w": np.ascontiguousarray(np.asarray(inp["pool_w"]).transpose(1, 0, 2)),
        "pool_cnt": cnt,
        "w_out": np.stack([tiled(np.asarray(inp["w_out"]), c * P + ar(P)) for c in range(KC)]),
        "vec": np.ascontiguousarray(np.concatenate([columns(np.asarray(vecs[n])) for n in VEC], axis=1)),
        "ident": np.eye(P, dtype=np.float32),
    }


def kernel(**inputs):
    import concourse.bacc as bacc
    from concourse.bass_utils import run_bass_kernel_spmd as run

    nc = bacc.Bacc("TRN2", target_bir_lowering=False, num_devices=1)
    arrays = lay_out(inputs)
    args = {name: nc.dram_tensor("in_" + name, a.shape, mybir.dt.from_np(a.dtype), kind="ExternalInput").ap()
            for name, a in arrays.items()}
    out = nc.dram_tensor("out_t", (P, KC, S), mybir.dt.float32, kind="ExternalOutput").ap()
    program(nc, args, out)
    result = run(nc, [{"in_" + name: a for name, a in arrays.items()}], core_ids=[0]).results[0]["out_t"]
    return np.ascontiguousarray(result.transpose(2, 1, 0).reshape(1, S, D))
```

```python
import concourse.bass as bass
import numpy as np
from concourse import mybir
from contextlib import ExitStack

D = 1024
S = 2048
P = 128
KC = D // P
TB = 512
G = S // TB
NB = S // P
BG = TB // P
H1 = 4
QR, KVR = 512, 256
ROPE = 64
QK_DIM = 192
RMS_EPS, LN_EPS = 1e-6, 1e-5
ALPHA = 2.0 ** 0.25
POOL_W = (2, 4, 8, 16)
HALO = 16
META = 16
H2, DH2 = 8, 64
HI = 4
TOPK = 256
H3 = 4
LEVELS = (64, 32, 16, 8, 4, 2, 1)
NEAR = 2 * P
ROUNDS = 24
MASKED = -1e30
HUGE = 3e38

RING = 6
SLOTS = 4
PT_SLOTS = 3

VEC = {}
_at = 0
for _name, _n in (("q_g", 4), ("kv_g", 2), ("pool_scale", 4), ("ln_g", 8), ("ln_b", 8),
                  ("kv_g2", 1), ("hgrn_g", 1), ("ln_g2", 8), ("ln_b2", 8), ("lb_raw", 4),
                  ("inv_freq", 1), ("rope_sign", 1)):
    VEC[_name] = _at
    _at += _n
NVEC = _at


def first_pair_steps(g):
    yield from [("kv", g, j) for j in range(2)]
    yield from [("krope", g, j) for j in range(2)]
    yield ("kv_sq", g)
    yield from [("k_nope", g, h) for h in range(H1)]
    yield from [("v", g, b) for b in range(BG)]


def mla_units(g):
    return [(BG * g + b, h) for b in range(BG) for h in range(H1)]


def mla_tiles(g):
    units = mla_units(g)
    for u in range(len(units) + 2):
        if u < len(units):
            yield from [("score", *units[u], c) for c in range(S // TB)]
        if 2 <= u and units[u - 2][1] == H1 - 1:
            yield ("o_t", units[u - 2][0])
        if 1 <= u <= len(units):
            yield from [("prob_t", *units[u - 1], c) for c in range(S // TB)]


def query_tiles(g):
    yield from [("xq", g, j) for j in range(4)]
    yield ("q_sq", g)
    yield from [("q_nope", g, h) for h in range(H1)]
    yield from [("q_rope", g, j) for j in range(4)]
    yield from [("gate_a", g, j) for j in range(4)]
    yield from [("u", g, j) for j in range(4)]
    yield from [("gate_b", g, j) for j in range(4)]
    yield from [("mix", g, j) for j in range(4)]


def out_tiles(g, tag):
    yield from [(tag + "out", g, c) for c in range(KC)]
    yield (tag + "mean", g)
    yield (tag + "var", g)


META_TILES = ([("t5_row",)] + [("t5", j) for j in range(4)] + [("m_c",), ("m_c_sq",), ("m_v",)] + [("m_f", h) for h in range(H3)] + [("m_i",), ("m_k_t",), ("m_u",)])


def second_steps(g):
    first = BG * g
    rows = [("index_row", g, c) for c in range(len(index_chunks(first)))] if needs_topk(first) else []
    fillers = ([[("ki", g)], [("qi", g, 0)], [("qi", g, 1)], [("wi", g)]] + [[("gate_h", g, j)] for j in range(3)] + [[("c", g)]],
               [[("qa", g, j)] for j in range(4)] + [[("gate2", g, j)] for j in range(4)])
    for pair in range(2):
        yield from [("f", g, 2 * pair), ("f", g, 2 * pair + 1), ("hq", g, 2 * pair), ("hq", g, 2 * pair + 1)]
        if pair == 0:
            yield ("i", g)
        else:
            yield ("gate_h", g, 3)
            yield from rows
        for lev in range(len(LEVELS) + 1):
            yield from fillers[pair][lev]
            yield ("level", g, pair, lev)
        yield ("decayed", g, pair)
        if pair == 0:
            yield ("c_sq", g)
        for b in range(BG):
            yield ("chunk", g, pair, b)
            yield from [("v2", g, b)] if pair == 0 else [("ql", g, 2 * b), ("ql", g, 2 * b + 1)]
        yield ("h_norm", g, pair)


def tiles_of(step):
    kind, g = step[0], step[1]
    if kind == "i":
        return [("i", g, b) for b in range(BG)]
    if kind == "level":
        return [(*step, e) for e in range(2)]
    if kind == "decayed":
        return [("kd_t", *step[1:], b) for b in range(BG)]
    if kind == "chunk":
        return [("o_h", *step[1:]), ("u_h", *step[1:])]
    if kind == "h_norm":
        return [("h_sq", *step[1:], e) for e in range(2)]
    if kind == "index_row":
        return [("index", BG * g, step[2], h) for h in range(HI)]
    return [step]


def keys_of(i):
    return (i + 1) * P


def near_width(i):
    return min(NEAR, keys_of(i))


def far_chunks(i):
    n = keys_of(i) - near_width(i)
    return [(c, min(TB, n - c)) for c in range(0, n, TB)]


def index_chunks(i):
    n = keys_of(i)
    return [(c, min(TB, n - c)) for c in range(0, n, TB)]


def needs_topk(i):
    return keys_of(i) > TOPK


def prob_tiles(i):
    return -(-(i + 1) // BG)


def prob_tiles_before(i, h):
    return H2 * sum(prob_tiles(b) for b in range(i)) + h * prob_tiles(i)


def index_adds_before(i):
    return HI * sum(len(index_chunks(b)) for b in range(i) if needs_topk(b))


def index_tiles(i):
    if needs_topk(i):
        yield from [("index", i, c, h) for c in range(len(index_chunks(i))) for h in range(HI)]


def keys_by_act(i):
    return P * (5 * i // 8) if i % BG != 0 else 0


def rounds_before(i, shared=False):
    return ROUNDS * sum(needs_topk(b) and (b % BG != 0 or not shared) for b in range(i))


def rounds_at(i, h, slot):
    per_head = len(far_chunks(i)) + 1
    slots, at = (H2 - 1) * per_head, h * per_head + slot
    if h == H2 - 1 or not needs_topk(i + 1):
        return range(0)
    return range(ROUNDS * at // slots, ROUNDS * (at + 1) // slots)


def dsa_units(g):
    return [(BG * g + b, h) for b in range(BG) for h in range(H2)]


def ended(units, u, back):
    return units[u - back][0] if 0 <= u - back < len(units) and units[u - back][1] == H2 - 1 else None


def dsa_tiles(g):
    units = dsa_units(g)
    for u in range(len(units) + 4):
        if u < len(units):
            i, h = units[u]
            if h == 0:
                if i + 1 < BG * (g + 1):
                    yield from index_tiles(i + 1)
                yield ("score_m", i)
            yield from [("far", i, h, c) for c in range(len(far_chunks(i)))]
            yield ("near", i, h)
        if ended(units, u, 2) is not None:
            yield ("pm_t", ended(units, u, 2))
        if 1 <= u <= len(units):
            i, h = units[u - 1]
            yield from [("p2_t", i, h, c) for c in range(prob_tiles(i))]
        if ended(units, u, 3) is not None:
            yield ("o2_t", ended(units, u, 3))


def schedule():
    tiles = []
    for g in range(G):
        tiles += first_pair_steps(g)
    for g in range(G):
        tiles += query_tiles(g)
        tiles += mla_tiles(g)
        tiles += out_tiles(g, "1")
    tiles += META_TILES
    for g in range(G):
        for step in second_steps(g):
            tiles += tiles_of(step)
        tiles += dsa_tiles(g)
        tiles += out_tiles(g, "2")
    return tiles


TILES = schedule()
T = {name: n for n, name in enumerate(TILES)}
assert len(T) == len(TILES)



def weight_of(name):
    kind = name[0]
    if kind == "kv":
        return ("w_in_kv", name[2])
    if kind == "krope":
        return ("w_in_kv", 2 + name[2])
    if kind in ("xq", "gate_a", "u", "gate_b"):
        return ("w_in_q", 4 * ("xq", "gate_a", "u", "gate_b").index(kind) + name[2])
    if kind in ("q_nope", "q_rope"):
        return ("w_uq", 4 * (kind == "q_rope") + name[2])
    if kind == "1out":
        return ("w_out", name[2])
    if kind == "2out":
        return ("w_out2", name[2])
    if kind in SECOND_CHUNKS:
        return ("w_in2", SECOND_CHUNKS[kind] + (name[2] if len(name) > 2 else 0))
    if kind == "m_c":
        return ("w_in2", SECOND_CHUNKS["c"])
    if kind == "m_f":
        return ("w_in2", SECOND_CHUNKS["f"] + name[1])
    return None


SECOND_CHUNKS = {"c": 0, "ki": 1, "qi": 2, "qa": 4, "gate2": 8, "hq": 12, "f": 16, "gate_h": 20}


def stream_of(tiles):
    out = []
    for name in tiles:
        if weight_of(name):
            out.append((name, *weight_of(name), name))
        if name[0] == "m_v" or (name[0] == "v2" and name[2] == 0):
            out.append((("w_uv",) + name[1:2], "w_uv", 0, name if name[0] == "m_v" else ("v2", name[1], BG - 1)))
        if name[0] == "ql" and name[2] == 0:
            out.append((("w_uk", name[1]), "w_uk", 0, ("ql", name[1], H2 - 1)))
        if name[0] == "m_i" or (name[0] == "i" and name[2] == 0):
            out += [(("w_i", name[1:2], j), "w_i", j, name if name[0] == "m_i" else ("i", name[1], BG - 1)) for j in range(4)]
    return out


def program(nc, A, out_t):
    f32, bf16, i32 = mybir.dt.float32, mybir.dt.bfloat16, mybir.dt.int32
    ALU, ACT, AX = mybir.AluOpType, mybir.ActivationFunctionType, mybir.AxisListType
    u8, u16 = mybir.dt.uint8, mybir.dt.uint16
    x1_t = nc.dram_tensor("x1_t", (P, KC, S), f32, kind="Internal").ap()
    t5_rows = nc.dram_tensor("t5_rows", (H2, 3 * P), f32, kind="Internal").ap()
    STREAM = stream_of(TILES)
    WSLOT = {name: n for n, (name, _, _, _) in enumerate(STREAM)}

    ctx = ExitStack()
    with ctx:
        def sem(name):
            return ctx.enter_context(nc.semaphore(name))

        def alloc(stack, name, shape, dt=f32):
            return stack.enter_context(nc.sbuf_tensor(name, shape, dt))

        ring = [alloc(ctx, f"weights{i}", [P, KC * P]) for i in range(SLOTS)]
        ident = alloc(ctx, "ident", [P, P])
        ones = alloc(ctx, "ones", [P, P])
        vec = alloc(ctx, "vec", [P, NVEC])
        eps = alloc(ctx, "eps", [P, 2])
        even_odd = [alloc(ctx, f"group_{n}", [P, KC, TB]) for n in ("even", "odd")]
        probs = alloc(ctx, "probs", [P, 2 * S])
        prob_t = alloc(ctx, "prob_t", [P, PT_SLOTS, TB])
        gate = alloc(ctx, "gate", [P, 4, TB])
        std = alloc(ctx, "std", [P, TB])
        rstd = alloc(ctx, "rstd", [P, TB])
        tmp = alloc(ctx, "tmp", [P, 2, TB])
        o_sb = alloc(ctx, "o_sb", [P, TB])
        stat = alloc(ctx, "stat", [P, 64])

        one = ExitStack()
        k_nope = alloc(one, "k_nope", [P, H1, S])
        k_rope = alloc(one, "k_rope", [P, S])
        val = alloc(one, "val", [P, NB, TB])
        q_nope = alloc(one, "q_nope", [P, H1, TB])
        q_rope = alloc(one, "q_rope", [P, H1, TB])
        lat = alloc(one, "lat", [P, 4, TB])
        cos = alloc(one, "cos", [P, TB])
        sin = alloc(one, "sin", [P, TB])
        pos_k = alloc(one, "pos_k", [P, S])
        pos_i = probs[:, 0:S].bitcast(i32)
        pos_q = alloc(one, "pos_q", [P, NB])
        pos_qi = alloc(one, "pos_qi", [P, NB], i32)
        mask = alloc(one, "mask", [P, S], bf16)
        pool_w = alloc(one, "pool_w", [P, 4, P])
        pool_cnt = alloc(one, "pool_cnt", [P, 4, HALO])
        halo = alloc(one, "halo", [P, 4, HALO])
        w_ukv = gate[:, :, :]
        u_in = probs[:, 0:4 * (TB + HALO)].rearrange("p (j t) -> p j t", j=4)
        u_sum = probs[:, 4 * (TB + HALO):6 * (TB + HALO)].rearrange("p (j t) -> p j t", j=2)
        one.close()

        two = ExitStack()
        c_t = alloc(two, "c_t", [P, S])
        v2 = alloc(two, "v2", [P, NB, TB])
        ki = alloc(two, "ki", [P, S])
        qa = alloc(two, "qa", [P, 4, TB])
        ql = alloc(two, "ql", [P, H2, TB])
        qi = alloc(two, "qi", [P, HI, TB])
        wi = alloc(two, "wi", [P, BG, HI])
        bias = alloc(two, "bias", [P, H2, NEAR])
        state = alloc(two, "state", [P, H3, P])
        index = alloc(two, "index", [P, S])
        sel = alloc(two, "sel", [P, 2, S], bf16)
        x_meta = alloc(two, "x_meta", [P, KC, META])
        v_meta = alloc(two, "v_meta", [P, TB])
        c_meta = alloc(two, "c_meta", [P, P])
        s_meta = alloc(two, "s_meta", [P, H2, META])
        p_meta = alloc(two, "p_meta", [P, P])
        pm_t = alloc(two, "pm_t", [P, P])
        causal = alloc(two, "causal", [P, P])
        lev_mask = alloc(two, "lev_mask", [P, len(LEVELS) + 1, P], u8)
        halves = alloc(two, "halves", [P, ROUNDS])
        steps_ = alloc(two, "steps", [P, ROUNDS])
        mids = alloc(two, "mids", [P, ROUNDS])
        counts = alloc(two, "counts", [P, ROUNDS])
        signs = alloc(two, "signs", [P, ROUNDS])
        w_wi = alloc(two, "w_wi", [P, KC, HI])
        mx = alloc(two, "mx", [P, H2, 8])
        m2 = alloc(two, "m2", [P, 2, H2])
        sums2 = alloc(two, "sums2", [P, 2, H2])
        lb = alloc(two, "lb", [P, 2, H3])
        decay = alloc(two, "decay", [P, 2, BG])
        two.close()
        mask_i = probs[:, S:S + KC * P].bitcast(i32)
        anti, rel, t5_hot, t5_row = qa[:, 1, 0:P], qa[0:32, 3, 0:H2], qa[0:32, 0, 0:3 * P], qa[0:H2, 2, 0:3 * P]
        hf, hk, hb, hqb = (probs[:, n * 1024:(n + 1) * 1024].rearrange("p (e t) -> p e t", e=2) for n in range(4))
        hx = (hf, ql[:, 2:4, :])
        h_i = sel[:, :, :].bitcast(f32).rearrange("p a n -> p (a n)").rearrange("p (b n) -> p b n", b=BG)
        kd_t = prob_t[:, 0:2, :]

        def x_of(g):
            return even_odd[g % 2]

        def y_of(g):
            return even_odd[(g + 1) % 2]

        def he_of(g):
            return y_of(g)[:, 0:2, :], ql[:, 0:2, :]

        def ha_of(g):
            return y_of(g)[:, 2:4, :]

        def near_of(g):
            return x_of(g)[:, 0:4, :].rearrange("p k t -> p (k t)").rearrange("p (h n) -> p h n", h=H2)

        def selecting(i):
            n = keys_of(i)
            if i % BG == 0:
                return probs[:, 0:512].bitcast(u8)[:, 0:n], probs[:, 512:1024].bitcast(u8)[:, 0:n], probs[:, 3072:4096].bitcast(u16)[:, 0:n]
            x_hi = x_of(i // BG)[:, 4:8, :].rearrange("p k t -> p (k t)")
            return x_hi[:, 1024:1536].bitcast(u8)[:, 0:n], x_hi[:, 1536:2048].bitcast(u8)[:, 0:n], x_hi[:, 0:1024].bitcast(u16)[:, 0:n]

        def tested(i):
            return sel[:, i % 2, 0:keys_of(i)] if i % BG != 0 else ql[:, 4, :].bitcast(u8)[:, 0:keys_of(i)]


        banks = [ctx.enter_context(nc.psum_tensor(f"bank{i}", [P, TB], f32)) for i in range(RING)]
        o_acc = [ctx.enter_context(nc.psum_tensor(f"o_acc{i}", [P, TB], f32)) for i in range(2)]

        tile_ready = sem("tile_ready")
        drained = [sem(f"drained{i}") for i in range(RING)]
        w_here = [sem(f"w_here{i}") for i in range(SLOTS)]
        const_here = sem("const_here")
        x_here = [sem(f"x_here{i}") for i in range(2)]
        const_made = sem("const_made")
        act_step = sem("act_step")
        dve_step = sem("dve_step")
        pool_step = sem("pool_step")
        rope_arg = sem("rope_arg")
        rope_made = sem("rope_made")
        k_normed = sem("k_normed")
        q_normed = sem("q_normed")
        q_rotated = sem("q_rotated")
        win_summed = sem("win_summed")
        pooled = sem("pooled")
        row_max = sem("row_max")
        probs_made = sem("probs_made")
        pv_done = sem("pv_done")
        o_scaled = sem("o_scaled")
        centred = sem("centred")
        squared = sem("squared")
        scaled = sem("scaled")
        x_out = sem("x_out")
        stored = sem("stored")
        const2_here = sem("const2_here")
        t5_made = sem("t5_made")
        t5_here = sem("t5_here")
        std_read = sem("std_read")
        c_normed = sem("c_normed")
        lb_arg = sem("lb_arg")
        lb_exp = sem("lb_exp")
        f_made = sem("f_made")
        f_log = sem("f_log")
        f_summed = sem("f_summed")
        lev_diff = sem("lev_diff")
        lev_exp = sem("lev_exp")
        lev_made = sem("lev_made")
        h_free = sem("h_free")
        o_squared = sem("o_squared")
        u_meta = sem("u_meta")
        lev_diff_meta = sem("lev_diff_meta")
        index_added = sem("index_added")
        counted = sem("counted")
        signs_summed = sem("signs_summed")
        mid_made = sem("mid_made")
        sel_made = sem("sel_made")
        near_made = sem("near_made")
        row_max2 = sem("row_max2")
        probs2_made = sem("probs2_made")
        pm_arg = sem("pm_arg")
        pm_made = sem("pm_made")
        pv2_done = sem("pv2_done")
        pvm_done = sem("pvm_done")
        o2_scaled = sem("o2_scaled")
        gates_made = sem("gates_made")
        stored2 = sem("stored2")
        block = ctx.enter_context(nc.Block())

        def counter(semaphore):
            count = [0]

            def step(eng, ins):
                count[0] += 1
                ins.then_inc(semaphore, 1)
                eng.wait_ge(semaphore, count[0])
            return step

        def wait_x(eng, g, before):
            eng.wait_ge(x_here[g % 2], 32 * (before + 1))

        def wait_tile(eng, *name):
            eng.wait_ge(tile_ready, T[name] + 1)

        def wait_drained(eng, *name):
            n = T[name]
            eng.wait_ge(drained[n % RING], n // RING + 1)

        def bank(*name):
            return banks[T[name] % RING]

        def drains(ins, *name):
            ins.then_inc(drained[T[name] % RING], 1)

        def sq_view(buf):
            return buf[:].rearrange("p (k t) -> p k t", k=KC)

        POOL_STEPS = 4 + (0 + 1 + 2 + 3) + 4

        def prev_unit(units, u, g, back):
            return units[u - back] if u >= back else mla_units(g - 1)[u - back]

        def out_norm(tag, g, dve, step, V):
            x_t = x_of(g)
            for c in range(KC):
                wait_tile(dve, tag + "out", g, c)
                drains(V.scalar_tensor_tensor(out=x_t[:, c, :], in0=x_t[:, c, :], scalar=ALPHA,
                                              in1=bank(tag + "out", g, c)[:], op0=ALU.mult, op1=ALU.add), tag + "out", g, c)
            wait_tile(dve, tag + "mean", g)
            drains(V.tensor_scalar(rstd[:], bank(tag + "mean", g)[:], -1.0 / D, None, ALU.mult), tag + "mean", g)
            wait_drained(dve, tag + "mean", g)
            V.tensor_tensor(x_t[:], x_t[:], rstd[:].unsqueeze(1).broadcast_to([P, KC, TB]), ALU.add).then_inc(centred, 1)
            wait_drained(dve, tag + "var", g)
            dve.wait_ge(centred, g + 1 + (0 if tag == "1" else G))
            if tag == "1":
                step(dve, V.reciprocal(rstd[:], std[:]))
            else:
                V.reciprocal(rstd[:], std[:]).then_inc(std_read, 1)
                dve.wait_ge(std_read, N_STD[g] + 1)
            V.tensor_tensor(x_t[:], x_t[:], rstd[:].unsqueeze(1).broadcast_to([P, KC, TB]), ALU.mult).then_inc(scaled, 1)

        SECOND_CONSTANTS = ((rel, A["rel"]), (t5_hot, A["t5_hot"]), (anti, A["anti"]), (x_meta[:], A["meta_t"]),
                            (causal[:], A["causal"]), (mask_i, A["lev_mask"]), (halves[:], A["halves"]),
                            (w_wi[:], A["w_wi"]), (v_meta[:], A["block_diag"]))
        N_CONST2 = 16 * len(SECOND_CONSTANTS)

        def second_begins(eng):
            wait_tile(eng, "1var", G - 1)
            eng.wait_ge(const2_here, N_CONST2)

        def wait_stored(eng, g):
            if g > 0:
                eng.wait_ge(stored2, 16 * g)
            else:
                eng.wait_ge(stored, 16 * G)

        def level_no(g, pair, k):
            return (2 * g + pair) * (len(LEVELS) + 2) + k

        C_STD, H_STD, N_STD = {}, {}, {}
        reads = 1
        for g in range(G):
            for st in second_steps(g):
                if st[0] == "c_sq":
                    C_STD[g] = reads
                    reads += 1
                if st[0] == "h_norm":
                    for e in range(2):
                        H_STD[(g, 2 * st[2] + e)] = reads
                        reads += 1
            N_STD[g] = reads
            reads += 1

        def halved(ap, w):
            return ap.rearrange("p e (n t) -> p (e n) t", t=2 * w)

        @block.sync
        def _(sp):
            first_constants = ((vec[:], A["vec"]), (pos_qi[:], A["pos_q"]), (pos_i, A["pos_k"].broadcast_to([P, S])),
                               (w_ukv, A["w_ukv"]), (ident[:], A["ident"]), (pool_w[:], A["pool_w"]), (pool_cnt[:], A["pool_cnt"]))

            def load_x(g, src):
                for k in range(0, KC, 4):
                    sp.dma_start(x_of(g)[:, k:k + 4, :], src[:, k:k + 4, g * TB:(g + 1) * TB]).then_inc(x_here[g % 2], 16)

            sent = 0
            for name, arr, idx, _ in STREAM:
                if name[0] == "kv" and name[2] == 0:
                    if name[1] > 1:
                        wait_tile(sp, "krope", name[1] - 2, 1)
                    load_x(name[1], A["x_t"])
                if name[0] == "xq" and name[2] == 0:
                    if name[1] == 0:
                        wait_tile(sp, "krope", G - 2, 1)
                    else:
                        wait_tile(sp, "1out", name[1] - 1, KC - 1)
                    load_x(name[1], A["x_t"])
                if name[0] == "m_c":
                    wait_tile(sp, "1var", G - 1)
                    for dst, src in SECOND_CONSTANTS:
                        sp.dma_start(dst, src).then_inc(const2_here, 16)
                if name[0] == "f" and name[2] == 0:
                    if name[1] > 0:
                        wait_tile(sp, "2out", name[1] - 1, KC - 1)
                    else:
                        sp.wait_ge(stored, 16 * G)
                    load_x(name[1], x1_t)
                if name[0] == "2out" and name[2] == 0:
                    sp.wait_ge(row_max2, H2 * BG * (name[1] + 1))
                    load_x(name[1], x1_t)
                if sent == SLOTS:
                    for dst, const in first_constants:
                        sp.dma_start(dst, const).then_inc(const_here, 16)
                if sent >= SLOTS:
                    wait_tile(sp, *STREAM[sent - SLOTS][3])
                src = A[arr][idx]
                sp.dma_start(ring[sent % SLOTS][:, 0:src.shape[1]], src).then_inc(w_here[sent % SLOTS], 16)
                sent += 1
            sp.wait_ge(stored2, 16 * G)

        @block.gpsimd
        def _(pool):
            step = counter(pool_step)
            pool.memset(ones[:], 1.0).then_inc(const_made, 1)
            pool.memset(eps[:, 0:1], RMS_EPS).then_inc(const_made, 1)
            pool.memset(eps[:, 1:2], LN_EPS).then_inc(const_made, 1)
            pool.memset(halo[:], 0.0).then_inc(const_made, 1)
            pool.memset(q_rope[:], 0.0).then_inc(const_made, 1)
            pool.wait_ge(const_made, 5)
            for g in range(G):
                for j in range(4):
                    wait_drained(pool, "u", g, j)
                    step(pool, pool.tensor_copy(u_in[:, j, 0:HALO], halo[:, j, :]))
                    src = u_in[:, j, :]
                    for s in range(j + 1):
                        lo = 2 ** (s + 1) - 1
                        if s == 0 and j > 0:
                            pool.wait_ge(pooled, 4 * g + j)
                        if s == 0 and j == 0:
                            wait_tile(pool, "q_rope", g, 3)
                        dst = u_sum[:, s % 2, :]
                        ins = pool.tensor_tensor(dst[:, lo:], src[:, lo:], src[:, lo - 2 ** s:TB + HALO - 2 ** s], ALU.add)
                        if s < j:
                            step(pool, ins)
                        src = dst
                    ins.then_inc(win_summed, 1)
                for j in range(4):
                    ins = pool.tensor_copy(halo[:, j, :], u_in[:, j, TB:TB + HALO])
                    step(pool, ins)
            pool.wait_ge(win_summed, 4 * G)

            second_begins(pool)
            pool.memset(qi[:], 0.0).then_inc(const_made, 1)
            pool.wait_ge(t5_made, 1)
            pool.dma_start(t5_rows, t5_row).then_inc(t5_here, 16)
            pool.wait_ge(t5_here, 16)
            pool.dma_start(index[:].rearrange("p (h n) -> p h n", h=H2),
                           bass.AP(t5_rows.tensor, 0, [[1, P], [3 * P, H2], [1, NEAR]])).then_inc(t5_here, 16)
            for g in range(G):
                he, near = he_of(g), near_of(g)
                wait_stored(pool, g)
                for pair in range(2):
                    pool.wait_ge(f_summed, 2 * g + pair + 1)
                    for k, w in enumerate(LEVELS):
                        n = level_no(g, pair, k)
                        if k >= 2:
                            pool.wait_ge(lev_made, n - 1)
                        b, e = halved(hb, w), halved(he[k % 2], w)
                        mid = b[:, :, w - 1:w].broadcast_to([P, 2 * TB // (2 * w), w])
                        pool.tensor_tensor(e[:, :, 0:w], mid, b[:, :, 0:w], ALU.subtract).then_inc(lev_diff, 1)
                        pool.tensor_tensor(e[:, :, w:2 * w], b[:, :, w:2 * w], mid, ALU.subtract).then_inc(lev_diff, 1)
                    pool.wait_ge(lev_made, level_no(g, pair, len(LEVELS)))
                    b, e = halved(hb, P // 2), halved(he[0], P // 2)
                    pool.tensor_tensor(e, b[:, :, P - 1:P].broadcast_to([P, 2 * BG, P]), b, ALU.subtract).then_inc(lev_diff, 1)
                wait_tile(pool, "gate2", g, 3)
                for b in range(BG):
                    i = BG * g + b
                    pool.wait_ge(sel_made, i + 1)
                    wn = near_width(i)
                    n = keys_of(i)
                    for h in range(H2):
                        if b > 0:
                            pool.wait_ge(row_max2, H2 * (i - 1) + h + 1)
                        pool.tensor_tensor(near[:, h, NEAR - wn:], bias[:, h, NEAR - wn:], sel[:, i % 2, n - wn:n],
                                           ALU.add).then_inc(near_made, 1)

        @block.scalar
        def _(act):
            step = counter(act_step)
            A_ = nc.scalar.activation

            def rope_tables(n):
                act.wait_ge(rope_arg, n + 1)
                step(act, A_(cos[:], cos[:], ACT.Sin))
                A_(sin[:], sin[:], ACT.Sin).then_inc(rope_made, 1)

            def latents(tag, g, n, sq, gain, before):
                for j in range(n):
                    wait_tile(act, tag, g, j)
                    step(act, A_(sq[:, j, :], bank(tag, g, j)[:], ACT.Square))
                    if j == 0 and before is not None:
                        wait_tile(act, *before)
                    drains(A_(lat[:, j, :], bank(tag, g, j)[:], ACT.Copy, scale=vec[:, gain + j:gain + j + 1]), tag, g, j)

            def root(name, width, e, free=None):
                wait_tile(act, *name)
                if free is not None:
                    act.wait_ge(*free)
                drains(A_(std[:], bank(*name)[:], ACT.Sqrt, scale=1.0 / width, bias=eps[:, e:e + 1]), *name)

            act.wait_ge(const_here, 16 * 7)
            act.wait_ge(const_made, 5)
            for g in range(G):
                rope_tables(g)
                if g > 0:
                    wait_tile(act, "kv_sq", g - 1)
                latents("kv", g, 2, prob_t, VEC["kv_g"], ("v", g - 1, BG - 1) if g else None)
                root(("kv_sq", g), KVR, 0, (k_normed, g) if g else None)
                for b in range(BG):
                    wait_tile(act, "v", g, b)
                    drains(A_(val[:, BG * g + b, :], bank("v", g, b)[:], ACT.Copy), "v", g, b)

            for g in range(G):
                rope_tables(G + g)
                if g > 0:
                    act.wait_ge(stored, 16 * g)
                latents("xq", g, 4, y_of(g), VEC["q_g"], ("v", G - 1, BG - 1) if g == 0 else ("mix", g - 1, 3))
                root(("q_sq", g), QR, 0, (k_normed, G) if g == 0 else (scaled, g))
                for h in range(H1):
                    wait_tile(act, "q_nope", g, h)
                    drains(A_(q_nope[:, h, :], bank("q_nope", g, h)[:], ACT.Copy), "q_nope", g, h)
                for j in range(4):
                    wait_tile(act, "gate_a", g, j)
                    drains(A_(gate[:, j, :], bank("gate_a", g, j)[:], ACT.Silu), "gate_a", g, j)
                for j in range(4):
                    wait_tile(act, "u", g, j)
                    if g == 0 and j == 0:
                        act.wait_ge(q_rotated, 1)
                    drains(A_(u_in[:, j, HALO:], bank("u", g, j)[:], ACT.Copy), "u", g, j)
                for j in range(4):
                    wait_tile(act, "gate_b", g, j)
                    drains(A_(y_of(g)[:, 4 + j, :], bank("gate_b", g, j)[:], ACT.Silu), "gate_b", g, j)

                units = mla_units(g)
                for u in range(len(units) + 1):
                    if u > 0:
                        i, h = units[u - 1]
                        for c in range(S // TB):
                            m = (H1 * BG * g + u - 1) * (S // TB) + c
                            wait_tile(act, "prob_t", i, h, c)
                            if m >= PT_SLOTS:
                                act.wait_ge(pv_done, m - PT_SLOTS + 1)
                            drains(A_(prob_t[:, m % PT_SLOTS, :], bank("prob_t", i, h, c)[:], ACT.Copy), "prob_t", i, h, c)
                    if u < len(units):
                        n = H1 * BG * g + u
                        act.wait_ge(row_max, n + 1)
                        p = probs[:, (n % 2) * S:(n % 2 + 1) * S]
                        A_(p, p, ACT.Exp, scale=QK_DIM ** -0.5, bias=stat[:, 8 + n % 2:9 + n % 2],
                           accum_out=stat[:, 16 + n % 8:17 + n % 8]).then_inc(probs_made, 1)

                act.wait_ge(centred, g + 1)
                for c in range(KC):
                    A_(sq_view(probs)[:, c, :], x_of(g)[:, c, :], ACT.Square).then_inc(squared, 1)
                root(("1var", g), D, 1)
                for c in range(KC):
                    act.wait_ge(scaled, g + 1)
                    ins = A_(x_of(g)[:, c, :], x_of(g)[:, c, :], ACT.Identity, scale=vec[:, VEC["ln_g"] + c:VEC["ln_g"] + c + 1],
                             bias=vec[:, VEC["ln_b"] + c:VEC["ln_b"] + c + 1])
                    if c < KC - 1:
                        step(act, ins)
                ins.then_inc(x_out, 1)
                act.wait_ge(x_out, g + 1)
                act.dma_start(x1_t[:, :, g * TB:(g + 1) * TB], x_of(g)[:]).then_inc(stored, 16)

            second_begins(act)
            wait_tile(act, "m_c")
            A_(tmp[:, 0, 0:META], bank("m_c")[:, 0:META], ACT.Square).then_inc(lb_exp, 1)
            drains(A_(c_t[:, 0:META], bank("m_c")[:, 0:META], ACT.Copy, scale=vec[:, VEC["kv_g2"]:VEC["kv_g2"] + 1]), "m_c")
            wait_tile(act, "m_c_sq")
            drains(A_(std[:, 0:META], bank("m_c_sq")[:, 0:META], ACT.Sqrt, scale=1.0 / P, bias=eps[:, 0:1]), "m_c_sq")
            act.wait_ge(lb_arg, 1)
            A_(lb[:, 0, :], lb[:, 0, :], ACT.Exp).then_inc(lb_exp, 1)
            for h in range(H3):
                wait_tile(act, "m_f", h)
                drains(A_(probs[:, h * META:(h + 1) * META], bank("m_f", h)[:, 0:META], ACT.Sigmoid), "m_f", h)
            act.wait_ge(f_made, 1)
            A_(probs[:, 0:H3 * META], probs[:, 0:H3 * META], ACT.Ln).then_inc(f_log, 1)
            wait_tile(act, "m_i")
            drains(A_(h_i[0:META, 0, :], bank("m_i")[0:META, :], ACT.Copy), "m_i")
            act.wait_ge(lev_diff_meta, 1)
            A_(probs[:, 256:256 + H3 * META], probs[:, 256:256 + H3 * META], ACT.Exp).then_inc(u_meta, 1)
            wait_tile(act, "m_k_t")
            drains(A_(kd_t[0:META, 0, :], bank("m_k_t")[0:META, :], ACT.Copy), "m_k_t")

            def relus(i, c):
                wide_ = index_chunks(i)[c][1]
                for h in range(HI):
                    m = index_adds_before(i) + c * HI + h
                    wait_tile(act, "index", i, c, h)
                    if m >= 2:
                        act.wait_ge(index_added, m - 1)
                    drains(A_(tmp[:, m % 2, 0:wide_], bank("index", i, c, h)[:, 0:wide_], ACT.Relu,
                              scale=DH2 ** -0.5), "index", i, c, h)

            def counts_of(i, h, slot):
                for r in rounds_at(i, h, slot):
                    keys = slice(keys_of(i + 1) - keys_by_act(i + 1), keys_of(i + 1))
                    act.wait_ge(mid_made, rounds_before(i + 1) + r + 1)
                    A_(tested(i + 1)[:, keys], index[:, keys], ACT.Sign, scale=-1.0, bias=mids[:, r:r + 1],
                       accum_out=signs[:, r:r + 1]).then_inc(signs_summed, 1)

            for g in range(G):
                he = he_of(g)
                for st in second_steps(g):
                    kind = st[0]
                    if kind == "f":
                        h = st[2]
                        if h == 2:
                            wait_tile(act, "u_h", g, 0, BG - 1)
                        elif h == 0 and g > 0:
                            wait_tile(act, "2var", g - 1)
                        elif h == 0:
                            act.wait_ge(u_meta, 2)
                        wait_tile(act, *st)
                        drains(A_(hf[:, h % 2, :], bank(*st)[:], ACT.Sigmoid), *st)
                    elif kind == "hq":
                        h = st[2]
                        wait_tile(act, *st)
                        if h == 2:
                            act.wait_ge(lev_made, level_no(g, 1, 0))
                        drains(A_(hqb[:, h % 2, :], bank(*st)[:], ACT.Silu), *st)
                        if h % 2 == 1:
                            act.wait_ge(f_made, 2 + 2 * g + h // 2)
                            A_(hf, hf, ACT.Ln).then_inc(f_log, 1)
                    elif kind == "gate_h":
                        wait_stored(act, g)
                        wait_tile(act, *st)
                        drains(A_(y_of(g)[:, 4 + st[2], :], bank(*st)[:], ACT.Copy), *st)
                    elif kind == "gate2":
                        wait_tile(act, *st)
                        drains(A_(gate[:, st[2], :], bank(*st)[:], ACT.Copy), *st)
                    elif kind == "i":
                        for b in range(BG):
                            wait_tile(act, "i", g, b)
                            drains(A_(h_i[:, b, :], bank("i", g, b)[:], ACT.Copy), "i", g, b)
                    elif kind == "index_row":
                        if st[2] == 0:
                            wait_tile(act, "c_sq", g)
                        relus(BG * g, st[2])
                    elif kind == "c":
                        wait_tile(act, *st)
                        step(act, A_(tmp[:, 0, :], bank(*st)[:], ACT.Square))
                        drains(A_(c_t[:, g * TB:(g + 1) * TB], bank(*st)[:], ACT.Copy, scale=vec[:, VEC["kv_g2"]:VEC["kv_g2"] + 1]), *st)
                    elif kind == "c_sq":
                        wait_tile(act, *st)
                        act.wait_ge(std_read, C_STD[g])
                        drains(A_(std[:], bank(*st)[:], ACT.Sqrt, scale=1.0 / P, bias=eps[:, 0:1]), *st)
                    elif kind == "v2":
                        wait_tile(act, *st)
                        drains(A_(v2[:, BG * g + st[2], :], bank(*st)[:], ACT.Copy), *st)
                    elif kind == "qa":
                        wait_tile(act, *st)
                        drains(A_(qa[:, st[2], :], bank(*st)[:], ACT.Copy), *st)
                    elif kind == "ql":
                        wait_tile(act, *st)
                        drains(A_(ql[:, st[2], :], bank(*st)[:], ACT.Copy, scale=DH2 ** -0.5), *st)
                    elif kind == "level":
                        pair, lev = st[2], st[3]
                        if lev < len(LEVELS):
                            act.wait_ge(lev_diff, 15 * (2 * g + pair) + 2 * (lev + 1))
                            A_(he[lev % 2], he[lev % 2], ACT.Exp).then_inc(lev_exp, 1)
                    elif kind == "decayed":
                        pair = st[2]
                        act.wait_ge(lev_made, level_no(g, pair, len(LEVELS) - 1))
                        step(act, A_(decay[:], hb.rearrange("p e (b t) -> p e b t", b=BG)[:, :, :, P - 1], ACT.Exp))
                        A_(he[1], hb, ACT.Exp).then_inc(lev_exp, 1)
                        act.wait_ge(lev_diff, 15 * (2 * g + pair + 1))
                        A_(he[0], he[0], ACT.Exp).then_inc(lev_exp, 1)
                        for b in range(BG):
                            wait_tile(act, "kd_t", g, pair, b)
                            drains(A_(kd_t[:, b // 2, (b % 2) * 256:(b % 2) * 256 + 256], bank("kd_t", g, pair, b)[:, 0:256],
                                      ACT.Copy), "kd_t", g, pair, b)
                    elif kind == "chunk":
                        pair, b = st[2], st[3]
                        wait_tile(act, "o_h", g, pair, b)
                        drains(A_(hb[:, :, b * P:(b + 1) * P], bank("o_h", g, pair, b)[:, 0:256].rearrange("p (e t) -> p e t", e=2),
                                  ACT.Copy, scale=P ** -0.5), "o_h", g, pair, b)
                    elif kind == "h_norm":
                        pair = st[2]
                        for b in range(BG):
                            wait_drained(act, "o_h", g, pair, b)
                        A_(hk, hb, ACT.Square).then_inc(o_squared, 1)
                        gates = y_of(g)[:, 4:7, :] if pair == 0 else y_of(g)[:, 7, :]
                        for j in (range(3) if pair == 0 else (3,)):
                            wait_drained(act, "gate_h", g, j)
                        A_(gates, gates, ACT.Silu).then_inc(gates_made, 1)
                        for e in range(2):
                            wait_tile(act, "h_sq", g, pair, e)
                            act.wait_ge(std_read, H_STD[(g, 2 * pair + e)])
                            drains(A_(std[:], bank("h_sq", g, pair, e)[:], ACT.Sqrt, scale=1.0 / P, bias=eps[:, 0:1]),
                                   "h_sq", g, pair, e)

                for j in range(4):
                    wait_drained(act, "gate2", g, j)
                A_(gate[:], gate[:], ACT.Silu).then_inc(gates_made, 1)

                units = dsa_units(g)
                for u in range(len(units) + 4):
                    ahead = u < len(units) and units[u][0] + 1 < BG * (g + 1) and needs_topk(units[u][0] + 1)
                    if ahead and units[u][1] == 0:
                        for c in range(len(index_chunks(units[u][0] + 1))):
                            relus(units[u][0] + 1, c)
                    if ended(units, u, 2) is not None:
                        i = ended(units, u, 2)
                        wait_tile(act, "pm_t", i)
                        drains(A_(pm_t[:], bank("pm_t", i)[:, 0:P], ACT.Copy), "pm_t", i)
                    if 1 <= u <= len(units):
                        i, h = units[u - 1]
                        for c in range(prob_tiles(i)):
                            if ahead and c <= len(far_chunks(units[u][0])):
                                counts_of(*units[u], c)
                            m = prob_tiles_before(i, h) + c
                            wide_ = min(TB, keys_of(i) - c * TB)
                            wait_tile(act, "p2_t", i, h, c)
                            if m >= PT_SLOTS:
                                act.wait_ge(pv2_done, m - PT_SLOTS + 1)
                            drains(A_(prob_t[:, m % PT_SLOTS, 0:wide_], bank("p2_t", i, h, c)[:, 0:wide_], ACT.Copy), "p2_t", i, h, c)
                    if u < len(units):
                        i, h = units[u]
                        n = H2 * BG * g + u
                        if ahead:
                            for slot in range(prob_tiles(units[u - 1][0]) if u > 0 else 0, len(far_chunks(i)) + 1):
                                counts_of(i, h, slot)
                        act.wait_ge(row_max2, n + 1)
                        p = probs[:, (n % 2) * S:(n % 2) * S + keys_of(i)]
                        A_(p, p, ACT.Exp, bias=stat[:, 8 + n % 2:9 + n % 2],
                           accum_out=sums2[:, i % 2, h:h + 1]).then_inc(probs2_made, 1)
                        if h == H2 - 1:
                            act.wait_ge(pm_arg, i + 1)
                            A_(p_meta[:], p_meta[:], ACT.Exp).then_inc(pm_made, 1)

                act.wait_ge(centred, G + g + 1)
                for c in range(KC):
                    A_(sq_view(probs)[:, c, :], x_of(g)[:, c, :], ACT.Square).then_inc(squared, 1)
                act.wait_ge(std_read, N_STD[g])
                root(("2var", g), D, 1)
                for c in range(KC):
                    act.wait_ge(scaled, G + g + 1)
                    ins = A_(x_of(g)[:, c, :], x_of(g)[:, c, :], ACT.Identity, scale=vec[:, VEC["ln_g2"] + c:VEC["ln_g2"] + c + 1],
                             bias=vec[:, VEC["ln_b2"] + c:VEC["ln_b2"] + c + 1])
                    if c < KC - 1:
                        step(act, ins)
                ins.then_inc(x_out, 1)
                act.wait_ge(x_out, G + g + 1)
                act.dma_start(out_t[:, :, g * TB:(g + 1) * TB], x_of(g)[:]).then_inc(stored2, 16)

        @block.vector
        def _(dve):
            step = counter(dve_step)
            V = nc.vector
            TWO_PI = 2.0 * np.pi
            C1 = 6.28125
            C2 = float(np.round((TWO_PI - C1) * 2 ** 23) / 2 ** 23)
            C3 = float(np.float32(TWO_PI - C1 - C2))

            def rope_args(n, g):
                if n > 0:
                    dve.wait_ge(rope_made, n)
                ang, turn = tmp[:, 0, :], tmp[:, 1, :]
                fr = VEC["inv_freq"]
                step(dve, V.tensor_scalar(ang, pos_k[:, g * TB:(g + 1) * TB], vec[:, fr:fr + 1], None, ALU.mult))
                step(dve, V.tensor_scalar(turn, ang, 1.0 / TWO_PI, 12582912.0, ALU.mult, ALU.add))
                step(dve, V.tensor_scalar(turn, turn, 12582912.0, None, ALU.subtract))
                for c in (C1, C2, C3):
                    step(dve, V.scalar_tensor_tensor(out=ang, in0=turn, scalar=-c, in1=ang, op0=ALU.mult, op1=ALU.add))
                sg = VEC["rope_sign"]
                pi = float(np.nextafter(np.float32(np.pi), np.float32(0)))
                step(dve, V.tensor_scalar(ang, ang, pi, -pi, ALU.min, ALU.max))
                step(dve, V.tensor_scalar(sin[:], ang, vec[:, sg:sg + 1], None, ALU.mult))
                step(dve, V.tensor_scalar(turn, ang, float(np.pi / 2), -TWO_PI, ALU.is_gt, ALU.mult))
                step(dve, V.scalar_tensor_tensor(out=ang, in0=ang, scalar=float(np.pi / 2), in1=turn, op0=ALU.add, op1=ALU.add))
                V.tensor_scalar(cos[:], ang, pi, -pi, ALU.min, ALU.max).then_inc(rope_arg, 1)

            def rotate(first, second):
                wait_tile(dve, *first)
                drains(V.tensor_tensor(tmp[:, 0, :], bank(*first)[:], cos[:], ALU.mult), *first)
                wait_tile(dve, *second)
                drains(V.tensor_tensor(tmp[:, 1, :], bank(*second)[:], sin[:], ALU.mult), *second)
                wait_drained(dve, *first)
                wait_drained(dve, *second)

            def wide(ap, n):
                return ap.unsqueeze(1).broadcast_to([P, n, TB])

            dve.wait_ge(const_here, 16 * 7)
            step(dve, V.tensor_copy(pos_k[:], pos_i))
            step(dve, V.tensor_copy(pos_q[:], pos_qi[:]))
            for g in range(G):
                rope_args(g, g)
                dve.wait_ge(rope_made, g + 1)
                rotate(("krope", g, 0), ("krope", g, 1))
                step(dve, V.tensor_tensor(k_rope[:, g * TB:(g + 1) * TB], tmp[:, 0, :], tmp[:, 1, :], ALU.add))
                wait_drained(dve, "kv_sq", g)
                step(dve, V.reciprocal(rstd[:], std[:]))
                V.tensor_tensor(lat[:, 0:2, :], lat[:, 0:2, :], wide(rstd[:], 2), ALU.mult).then_inc(k_normed, 1)
                for h in range(H1):
                    wait_tile(dve, "k_nope", g, h)
                    drains(V.tensor_copy(k_nope[:, h, g * TB:(g + 1) * TB], bank("k_nope", g, h)[:]), "k_nope", g, h)

            def mask_of(i):
                step(dve, V.tensor_scalar(mask[:], pos_k[:], pos_q[:, i:i + 1], MASKED, ALU.is_gt, ALU.mult))

            for g in range(G):
                rope_args(G + g, g)
                dve.wait_ge(rope_made, G + g + 1)
                wait_drained(dve, "q_sq", g)
                step(dve, V.reciprocal(rstd[:], std[:]))
                V.tensor_tensor(lat[:], lat[:], wide(rstd[:], 4), ALU.mult).then_inc(q_normed, 1)
                dve.wait_ge(const_made, 5)
                for pair in range(2):
                    rotate(("q_rope", g, 2 * pair), ("q_rope", g, 2 * pair + 1))
                    for e in range(2):
                        rows = slice(e * ROPE, (e + 1) * ROPE)
                        ins = V.tensor_tensor(q_rope[rows, 2 * pair + e, :], tmp[rows, 0, :], tmp[rows, 1, :], ALU.add)
                        if (pair, e) != (1, 1):
                            step(dve, ins)
                ins.then_inc(q_rotated, 1)
                for j, w in enumerate(POOL_W):
                    dve.wait_ge(win_summed, 4 * g + j + 1)
                    src, u = u_sum[:, j % 2, HALO:], u_in[:, j, HALO:]
                    if g == 0:
                        step(dve, V.tensor_tensor(src[:, 0:HALO], src[:, 0:HALO], pool_cnt[:, j, :], ALU.mult))
                    V.scalar_tensor_tensor(out=lat[:, j, :], in0=src, scalar=1.0 / w, in1=u,
                                           op0=ALU.mult, op1=ALU.subtract).then_inc(pooled, 1)
                for j in range(4):
                    wait_tile(dve, "mix", g, j)
                    wait_drained(dve, "gate_b", g, j)
                    ps = VEC["pool_scale"] + j
                    drains(V.scalar_tensor_tensor(out=y_of(g)[:, 4 + j, :], in0=bank("mix", g, j)[:], scalar=vec[:, ps:ps + 1],
                                                  in1=y_of(g)[:, 4 + j, :], op0=ALU.mult, op1=ALU.mult), "mix", g, j)

                units = mla_units(g)
                dve.wait_ge(pool_step, POOL_STEPS * (g + 1))
                for u in range(len(units) + 2):
                    if u < len(units):
                        i, h = units[u]
                        n = H1 * BG * g + u
                        if h == 0:
                            mask_of(i)
                        if n >= 2:
                            wait_tile(dve, "prob_t", *prev_unit(units, u, g, 2), S // TB - 1)
                        for c in range(S // TB):
                            wait_tile(dve, "score", i, h, c)
                            drains(V.tensor_tensor_reduce(out=probs[:, (n % 2) * S + c * TB:(n % 2) * S + (c + 1) * TB],
                                                          in0=bank("score", i, h, c)[:], in1=mask[:, c * TB:(c + 1) * TB],
                                                          scale=1.0, scalar=-HUGE, op0=ALU.add, op1=ALU.max,
                                                          accum_out=stat[:, c:c + 1]), "score", i, h, c)
                        for c in range(S // TB):
                            wait_drained(dve, "score", i, h, c)
                        step(dve, V.reduce_max(stat[:, 4:5], stat[:, 0:4], AX.X))
                        V.tensor_scalar(stat[:, 8 + n % 2:9 + n % 2], stat[:, 4:5], -QK_DIM ** -0.5, None,
                                        ALU.mult).then_inc(row_max, 1)
                    if 2 <= u and units[u - 2][1] == H1 - 1:
                        i = units[u - 2][0]
                        b = i % BG
                        wait_tile(dve, "o_t", i)
                        drains(V.tensor_tensor(y_of(g)[:, 0:4, b * P:(b + 1) * P],
                                               bank("o_t", i)[:].rearrange("p (j t) -> p j t", j=4),
                                               gate[:, :, b * P:(b + 1) * P], ALU.mult), "o_t", i)
                    if 1 <= u <= len(units) and units[u - 1][1] == H1 - 1:
                        i = units[u - 1][0]
                        dve.wait_ge(pv_done, (i + 1) * H1 * (S // TB))
                        dve.wait_ge(probs_made, (i + 1) * H1)
                        at = 16 + 4 * (i % 2)
                        step(dve, V.reciprocal(stat[:, 32:36], stat[:, at:at + 4]))
                        if i > 0:
                            wait_tile(dve, "o_t", i - 1)
                        V.tensor_tensor(o_sb[:].rearrange("p (h d) -> p h d", h=H1),
                                        o_acc[i % 2][:].rearrange("p (h d) -> p h d", h=H1),
                                        stat[:, 32:36].unsqueeze(2).broadcast_to([P, H1, P]), ALU.mult).then_inc(o_scaled, 1)

                out_norm("1", g, dve, step, V)

            second_begins(dve)
            step(dve, V.tensor_copy(lev_mask[:].rearrange("p l t -> p (l t)"), mask_i))
            wait_tile(dve, "t5_row")
            step(dve, V.tensor_copy(stat[0:H2, 40:41], bank("t5_row")[0:H2, 0:1]))
            drains(V.tensor_scalar(t5_row, bank("t5_row")[0:H2, 0:3 * P], stat[0:H2, 40:41], None, ALU.subtract), "t5_row")
            wait_drained(dve, "t5_row")
            step(dve, V.tensor_copy(t5_row, t5_row))
            V.tensor_copy(stat[0:H2, 41:42], stat[0:H2, 40:41]).then_inc(t5_made, 1)
            for j in range(4):
                wait_tile(dve, "t5", j)
                drains(V.tensor_copy(bias[:, 2 * j:2 * j + 2, :], bank("t5", j)[:].rearrange("p (h n) -> p h n", h=2)), "t5", j)
            lr = VEC["lb_raw"]
            V.tensor_tensor(lb[:, 0, :], vec[:, lr:lr + H3], vec[:, lr:lr + H3], ALU.subtract).then_inc(lb_arg, 1)
            wait_drained(dve, "m_c_sq")
            step(dve, V.reciprocal(rstd[:, 0:META], std[:, 0:META]))
            wait_drained(dve, "m_c")
            V.tensor_tensor(c_meta[:].rearrange("p (h m) -> p h m", h=H2), c_t[:, 0:META].unsqueeze(1).broadcast_to([P, H2, META]),
                            rstd[:, 0:META].unsqueeze(1).broadcast_to([P, H2, META]), ALU.mult).then_inc(c_normed, 1)
            V.tensor_copy(stat[:, 42:43], rstd[:, 0:1]).then_inc(std_read, 1)
            wait_tile(dve, "m_v")
            drains(V.tensor_tensor(v_meta[:], bank("m_v")[:], v_meta[:], ALU.mult), "m_v")
            dve.wait_ge(lb_exp, 2)
            step(dve, V.reciprocal(lb[:, 1, :], lb[:, 0, :]))
            step(dve, V.tensor_tensor(lb[:, 0, :], lb[:, 0, :], lb[:, 1, :], ALU.mult))
            step(dve, V.tensor_tensor(lb[:, 0, :], lb[:, 0, :], lb[:, 0, :], ALU.subtract))
            step(dve, V.tensor_scalar(lb[:, 1, :], lb[:, 0, :], -1.0, 1.0, ALU.mult, ALU.add))
            mf, mk, mb, me = (probs[:, o:o + H3 * META] for o in (0, 64, 128, 256))
            for h in range(H3):
                wait_drained(dve, "m_f", h)
                fh = mf[:, h * META:(h + 1) * META]
                step(dve, V.tensor_scalar(fh, fh, lb[:, 1, h:h + 1], lb[:, 0, h:h + 1], ALU.mult, ALU.add))
            step(dve, V.tensor_scalar(mk, mf, -1.0, 1.0, ALU.mult, ALU.add))
            V.tensor_scalar(mf, mf, 1e-19, None, ALU.max).then_inc(f_made, 1)
            dve.wait_ge(f_log, 1)
            for h in range(H3):
                fh = mf[:, h * META:(h + 1) * META]
                step(dve, V.tensor_tensor_scan(mb[:, h * META:(h + 1) * META], fh, fh, 0.0, ALU.add, ALU.bypass))
            mb3, me3 = (a.rearrange("p (h m) -> p h m", h=H3) for a in (mb, me))
            V.tensor_tensor(me3, mb3[:, :, META - 1:META].broadcast_to([P, H3, META]), mb3, ALU.subtract).then_inc(lev_diff_meta, 1)
            dve.wait_ge(u_meta, 1)
            V.tensor_tensor(me, me, mk, ALU.mult).then_inc(lev_diff_meta, 1)
            wait_tile(dve, "m_u")
            drains(V.tensor_copy(state[:], bank("m_u")[:].rearrange("p (h v) -> p h v", h=H3)), "m_u")
            wait_drained(dve, "m_u")
            wait_stored(dve, 0)
            V.memset(ha_of(0), 0.0).then_inc(u_meta, 1)

            def gates(g, pair):
                for e in range(2):
                    h = 2 * pair + e
                    wait_drained(dve, "f", g, h)
                    step(dve, V.tensor_scalar(hf[:, e, :], hf[:, e, :], lb[:, 1, h:h + 1], lb[:, 0, h:h + 1], ALU.mult, ALU.add))
                step(dve, V.tensor_scalar(hk, hf, -1.0, 1.0, ALU.mult, ALU.add))
                V.tensor_scalar(hf, hf, 1e-19, None, ALU.max).then_inc(f_made, 1)
                dve.wait_ge(f_log, 2 + 2 * g + pair)
                for e in range(2):
                    for b in range(BG):
                        src = hf[:, e, b * P:(b + 1) * P]
                        ins = V.tensor_tensor_scan(hb[:, e, b * P:(b + 1) * P], src, src, 0.0, ALU.add, ALU.bypass)
                        if (e, b) != (1, BG - 1):
                            step(dve, ins)
                ins.then_inc(f_summed, 1)

            def lev_wait(g, pair, k):
                dve.wait_ge(lev_exp, level_no(g, pair, k) + 1)

            def finish_heads(g, pair):
                dve.wait_ge(gates_made, 3 * g + 1 + pair)
                for e in range(2):
                    h = 2 * pair + e
                    wait_drained(dve, "h_sq", g, pair, e)
                    V.reciprocal(rstd[:], std[:]).then_inc(std_read, 1)
                    dve.wait_ge(std_read, H_STD[(g, h)] + 1)
                    step(dve, V.tensor_tensor(hb[:, e, :], hb[:, e, :], rstd[:], ALU.mult))
                    hg = VEC["hgrn_g"]
                    V.scalar_tensor_tensor(out=y_of(g)[:, 4 + h, :], in0=hb[:, e, :], scalar=vec[:, hg:hg + 1],
                                           in1=y_of(g)[:, 4 + h, :], op0=ALU.mult, op1=ALU.mult).then_inc(h_free, 1)

            def add_index(i, c):
                at, wide_ = index_chunks(i)[c]
                dst = index[:, at:at + wide_]
                for h in range(HI):
                    m = index_adds_before(i) + c * HI + h
                    wait_drained(dve, "index", i, c, h)
                    w = wi[:, i % BG, h:h + 1]
                    src = tmp[:, m % 2, 0:wide_]
                    if h == 0:
                        V.tensor_scalar(dst, src, w, None, ALU.mult).then_inc(index_added, 1)
                    else:
                        V.scalar_tensor_tensor(out=dst, in0=src, scalar=w, in1=dst, op0=ALU.mult, op1=ALU.add)\
                            .then_inc(index_added, 1)
                    dve.wait_ge(index_added, m + 1)

            def bracket(i):
                n = keys_of(i)
                low, high, span = stat[:, 48:49], stat[:, 49:50], stat[:, 50:51]
                step(dve, V.tensor_reduce(low, index[:, 0:TOPK], AX.X, ALU.min))
                step(dve, V.tensor_reduce(high, index[:, 0:n], AX.X, ALU.max))
                step(dve, V.tensor_tensor(index[:, n - P:n], index[:, n - P:n], causal[:], ALU.add))
                step(dve, V.tensor_tensor(span, high, low, ALU.subtract))
                step(dve, V.tensor_scalar(steps_[:], halves[:], span, None, ALU.mult))
                V.tensor_tensor(mids[:, 0:1], low, steps_[:, 0:1], ALU.add).then_inc(mid_made, 1)
                count(i, 0)

            def count(i, r):
                n = keys_of(i) - keys_by_act(i)
                dve.wait_ge(mid_made, rounds_before(i) + r + 1)
                V.tensor_scalar(tested(i)[:, 0:n], index[:, 0:n], mids[:, r:r + 1], 0.0, ALU.is_ge, ALU.add,
                                accum_out=counts[:, r:r + 1]).then_inc(counted, 1)

            def enough(i):
                return TOPK - 0.5 - 0.5 * keys_by_act(i)

            def halve(i, r):
                dve.wait_ge(counted, rounds_before(i) + r + 1)
                if keys_by_act(i):
                    dve.wait_ge(signs_summed, rounds_before(i, shared=True) + r + 1)
                    step(dve, V.scalar_tensor_tensor(out=counts[:, r:r + 1], in0=signs[:, r:r + 1], scalar=-0.5,
                                                     in1=counts[:, r:r + 1], op0=ALU.mult, op1=ALU.add))
                if r + 1 == ROUNDS:
                    return
                step(dve, V.scalar_tensor_tensor(out=stat[:, 51:52], in0=counts[:, r:r + 1], scalar=enough(i),
                                                 in1=steps_[:, r:r + 1], op0=ALU.is_ge, op1=ALU.mult))
                V.scalar_tensor_tensor(out=mids[:, r + 1:r + 2], in0=stat[:, 51:52], scalar=steps_[:, r + 1:r + 2],
                                       in1=mids[:, r:r + 1], op0=ALU.subtract, op1=ALU.add).then_inc(mid_made, 1)
                count(i, r + 1)

            SELECT_PARTS = 6

            def select(i, part):
                n = keys_of(i)
                out = sel[:, i % 2, 0:n]
                if not needs_topk(i):
                    if part == 0:
                        if n > P:
                            step(dve, V.memset(sel[:, i % 2, 0:n - P], 0.0))
                        V.tensor_copy(sel[:, i % 2, n - P:n], causal[:]).then_inc(sel_made, 1)
                    return
                above_, band_, rank_ = selecting(i)
                low, high, quota = stat[:, 48:49], stat[:, 49:50], stat[:, 52:53]
                x = index[:, 0:n]
                if part == 0:
                    step(dve, V.tensor_scalar(steps_[:], counts[:], enough(i), -HUGE, ALU.is_lt, ALU.mult))
                    step(dve, V.tensor_tensor(steps_[:], steps_[:], mids[:], ALU.add))
                    step(dve, V.reduce_max(stat[:, 53:54], steps_[:], AX.X))
                    step(dve, V.tensor_tensor(low, low, stat[:, 53:54], ALU.max))
                    step(dve, V.tensor_scalar(steps_[:], counts[:], enough(i), HUGE, ALU.is_ge, ALU.mult))
                    step(dve, V.tensor_tensor(steps_[:], steps_[:], mids[:], ALU.add))
                    step(dve, V.tensor_reduce(stat[:, 54:55], steps_[:], AX.X, ALU.min))
                    step(dve, V.tensor_tensor(high, high, stat[:, 54:55], ALU.min))
                elif part == 1:
                    step(dve, V.tensor_scalar(above_, x, high, 0.0, ALU.is_gt, ALU.add, accum_out=stat[:, 55:56]))
                elif part == 2:
                    step(dve, V.tensor_scalar(quota, stat[:, 55:56], -1.0, float(TOPK), ALU.mult, ALU.add))
                    step(dve, V.scalar_tensor_tensor(out=band_, in0=x, scalar=low, in1=above_, op0=ALU.is_ge, op1=ALU.subtract))
                elif part == 3:
                    step(dve, V.tensor_tensor_scan(rank_, band_, band_, 0.0, ALU.add, ALU.bypass))
                elif part == 4:
                    step(dve, V.scalar_tensor_tensor(out=band_, in0=rank_, scalar=quota, in1=band_, op0=ALU.is_le, op1=ALU.mult))
                else:
                    step(dve, V.tensor_tensor(out, above_, band_, ALU.add))
                    V.tensor_scalar(out, out, -MASKED, MASKED, ALU.mult, ALU.add).then_inc(sel_made, 1)

            def beside(i, h, slot):
                if (i + 1) % BG == 0:
                    return
                for r in rounds_at(i, h, slot):
                    halve(i + 1, r)
                if h == H2 - 1:
                    slots = len(far_chunks(i)) + 1
                    for part in range(SELECT_PARTS * slot // slots, SELECT_PARTS * (slot + 1) // slots):
                        select(i + 1, part)

            def decayed(g, pair, lev):
                w = LEVELS[lev]
                lev_wait(g, pair, lev)
                x, e_, k_, q_ = (halved(a, w) for a in (hx[lev % 2], he_of(g)[lev % 2], hk, hqb))
                step(dve, V.tensor_tensor(x[:, :, 0:w], e_[:, :, 0:w], k_[:, :, 0:w], ALU.mult))
                V.tensor_tensor(x[:, :, w:2 * w], e_[:, :, w:2 * w], q_[:, :, w:2 * w], ALU.mult).then_inc(lev_made, 1)

            for g in range(G):
                he, ha, near = he_of(g), ha_of(g), near_of(g)
                for st in second_steps(g):
                    kind = st[0]
                    if kind == "i":
                        gates(g, 0)
                    elif kind == "hq" and st[2] == H3 - 1:
                        gates(g, 1)
                    elif kind == "c_sq":
                        wait_drained(dve, *st)
                        V.reciprocal(rstd[:], std[:]).then_inc(std_read, 1)
                        dve.wait_ge(std_read, C_STD[g] + 1)
                        c_g = c_t[:, g * TB:(g + 1) * TB]
                        V.tensor_tensor(c_g, c_g, rstd[:], ALU.mult).then_inc(c_normed, 1)
                    elif kind == "ki":
                        wait_tile(dve, *st)
                        drains(V.tensor_copy(ki[:, g * TB:(g + 1) * TB], bank(*st)[:]), *st)
                    elif kind == "qi":
                        wait_tile(dve, *st)
                        dve.wait_ge(const_made, 6)
                        step(dve, V.tensor_copy(qi[0:DH2, 2 * st[2], :], bank(*st)[0:DH2, :]))
                        drains(V.tensor_copy(qi[DH2:P, 2 * st[2] + 1, :], bank(*st)[DH2:P, :]), *st)
                    elif kind == "wi":
                        wait_tile(dve, *st)
                        drains(V.tensor_scalar(wi[:].rearrange("p b h -> p (b h)"), bank(*st)[:, 0:BG * HI], HI ** -0.5, None,
                                               ALU.mult), *st)
                    elif kind == "level":
                        pair, lev = st[2], st[3]
                        if lev == 0:
                            if pair == 0 and g > 0:
                                wait_stored(dve, g)
                                step(dve, V.memset(ha, 0.0))
                            for e in range(2):
                                wait_drained(dve, "hq", g, 2 * pair + e)
                            decayed(g, pair, 0)
                        if lev + 1 < len(LEVELS):
                            decayed(g, pair, lev + 1)
                        for e in range(2):
                            wait_tile(dve, "level", g, pair, lev, e)
                            if lev > 0:
                                wait_drained(dve, "level", g, pair, lev - 1, e)
                            drains(V.copy_predicated(ha[:, e, :].rearrange("p (b t) -> p b t", b=BG),
                                                     lev_mask[:, lev, :].unsqueeze(1).broadcast_to([P, BG, P]),
                                                     bank("level", g, pair, lev, e)[:].rearrange("p (b t) -> p b t", b=BG)),
                                   "level", g, pair, lev, e)
                        if pair == 1 and needs_topk(BG * g):
                            for r in range(ROUNDS * lev // (len(LEVELS) + 1), ROUNDS * (lev + 1) // (len(LEVELS) + 1)):
                                halve(BG * g, r)
                    elif kind == "index_row":
                        if st[2] == 0:
                            wait_drained(dve, "wi", g)
                        add_index(BG * g, st[2])
                        if st[2] == len(index_chunks(BG * g)) - 1:
                            bracket(BG * g)
                    elif kind == "decayed":
                        pair = st[2]
                        lev_wait(g, pair, len(LEVELS))
                        V.tensor_tensor(hf, he[1], hqb, ALU.mult).then_inc(lev_made, 1)
                        lev_wait(g, pair, len(LEVELS) + 1)
                        V.tensor_tensor(he[0], he[0], hk, ALU.mult).then_inc(lev_made, 1)
                    elif kind == "chunk":
                        pair, b = st[2], st[3]
                        name = ("u_h", g, pair, b)
                        wait_tile(dve, *name)
                        for e in range(2):
                            h = 2 * pair + e
                            ins = V.scalar_tensor_tensor(out=state[:, h, :], in0=state[:, h, :], scalar=decay[:, e, b:b + 1],
                                                         in1=bank(*name)[:, e * P:(e + 1) * P], op0=ALU.mult, op1=ALU.add)
                            if e == 0:
                                step(dve, ins)
                        drains(ins, *name)
                    elif kind == "h_norm":
                        finish_heads(g, st[2])

                units = dsa_units(g)
                for part in range(SELECT_PARTS):
                    select(BG * g, part)
                for u in range(len(units) + 4):
                    if u < len(units):
                        i, h = units[u]
                        n = H2 * BG * g + u
                        if h == 0:
                            if i + 1 < BG * (g + 1) and needs_topk(i + 1):
                                for c in range(len(index_chunks(i + 1))):
                                    add_index(i + 1, c)
                                bracket(i + 1)
                            wait_tile(dve, "score_m", i)
                            src = bank("score_m", i)[:, 0:P].rearrange("p (h m) -> p h m", h=H2)
                            if i == 0:
                                drains(V.tensor_tensor(s_meta[:], src, bias[:, :, P - META:P], ALU.add), "score_m", i)
                            else:
                                drains(V.tensor_copy(s_meta[:], src), "score_m", i)
                            wait_drained(dve, "score_m", i)
                            step(dve, V.tensor_reduce(mx[:, :, 0:1], s_meta[:], AX.X, ALU.max))
                        if u >= 2:
                            pi_, ph = units[u - 2]
                            wait_tile(dve, "p2_t", pi_, ph, prob_tiles(pi_) - 1)
                        base = (n % 2) * S
                        chunks = far_chunks(i)
                        for c, (at, wide_) in enumerate(chunks):
                            wait_tile(dve, "far", i, h, c)
                            drains(V.tensor_tensor_reduce(out=probs[:, base + at:base + at + wide_], in0=bank("far", i, h, c)[:, 0:wide_],
                                                          in1=sel[:, i % 2, at:at + wide_], scale=1.0, scalar=-HUGE, op0=ALU.add,
                                                          op1=ALU.max, accum_out=mx[:, h, 1 + c:2 + c]), "far", i, h, c)
                            beside(i, h, c)
                        wn, last = near_width(i), 1 + len(chunks)
                        wait_tile(dve, "near", i, h)
                        dve.wait_ge(near_made, n + 1)
                        drains(V.tensor_tensor_reduce(out=probs[:, base + keys_of(i) - wn:base + keys_of(i)],
                                                      in0=bank("near", i, h)[:, 0:wn], in1=near[:, h, NEAR - wn:], scale=1.0,
                                                      scalar=-HUGE, op0=ALU.add, op1=ALU.max,
                                                      accum_out=mx[:, h, last:last + 1]), "near", i, h)
                        for c in range(len(chunks)):
                            wait_drained(dve, "far", i, h, c)
                        wait_drained(dve, "near", i, h)
                        step(dve, V.reduce_max(m2[:, i % 2, h:h + 1], mx[:, h, 0:last + 1], AX.X))
                        V.tensor_scalar(stat[:, 8 + n % 2:9 + n % 2], m2[:, i % 2, h:h + 1], -1.0, None, ALU.mult).then_inc(row_max2, 1)
                        if h == H2 - 1:
                            V.tensor_tensor(p_meta[:].rearrange("p (h m) -> p h m", h=H2), s_meta[:],
                                            m2[:, i % 2, :].unsqueeze(2).broadcast_to([P, H2, META]), ALU.subtract).then_inc(pm_arg, 1)
                        beside(i, h, len(chunks))
                    if ended(units, u, 3) is not None:
                        i = ended(units, u, 3)
                        b = i % BG
                        dve.wait_ge(gates_made, 3 * g + 3)
                        wait_tile(dve, "o2_t", i)
                        drains(V.tensor_tensor(y_of(g)[:, 0:4, b * P:(b + 1) * P],
                                               bank("o2_t", i)[:].rearrange("p (j t) -> p j t", j=4),
                                               gate[:, :, b * P:(b + 1) * P], ALU.mult), "o2_t", i)
                    if ended(units, u, 2) is not None:
                        i = ended(units, u, 2)
                        dve.wait_ge(pm_made, i + 1)
                        step(dve, V.tensor_reduce(stat[:, 24:32], p_meta[:].rearrange("p (h m) -> p h m", h=H2), AX.X, ALU.add))
                        dve.wait_ge(probs2_made, H2 * (i + 1))
                        step(dve, V.tensor_tensor(stat[:, 24:32], stat[:, 24:32], sums2[:, i % 2, :], ALU.add))
                        step(dve, V.reciprocal(stat[:, 32:40], stat[:, 24:32]))
                        dve.wait_ge(pvm_done, i + 1)
                        V.tensor_tensor(o_sb[:].rearrange("p (h d) -> p h d", h=H2),
                                        o_acc[i % 2][:].rearrange("p (h d) -> p h d", h=H2),
                                        stat[:, 32:40].unsqueeze(2).broadcast_to([P, H2, DH2]), ALU.mult).then_inc(o2_scaled, 1)
                wait_x(dve, g, G + 2 * (g // 2) + 1)
                out_norm("2", g, dve, step, V)

        @block.tensor
        def _(pe):
            M = nc.tensor.matmul
            done = [0]

            def claim(*name):
                assert T[name] == done[0]
                done[0] += 1
                n = T[name]
                if n >= RING:
                    pe.wait_ge(drained[n % RING], n // RING)

            def project(name, rhs, chunks):
                n = WSLOT[name]
                pe.wait_ge(w_here[n % SLOTS], 16 * (n // SLOTS + 1))
                claim(*name)
                for k in range(chunks):
                    ins = M(bank(*name)[:], ring[n % SLOTS][:, k * P:(k + 1) * P], rhs[:, k, :],
                            start=(k == 0), stop=(k == chunks - 1))
                ins.then_inc(tile_ready, 1)

            def squares(name, rhs, chunks):
                claim(*name)
                for k in range(chunks):
                    ins = M(bank(*name)[:], ones[:], rhs[:, k, :], start=(k == 0), stop=(k == chunks - 1))
                ins.then_inc(tile_ready, 1)

            pe.wait_ge(const_made, 5)
            for g in range(G):
                wait_x(pe, g, g // 2)
                for j in range(2):
                    project(("kv", g, j), x_of(g), KC)
                for j in range(2):
                    project(("krope", g, j), x_of(g), KC)
                for j in range(2):
                    wait_drained(pe, "kv", g, j)
                squares(("kv_sq", g), prob_t, 2)
                if g == 0:
                    pe.wait_ge(const_here, 16 * 7)
                pe.wait_ge(k_normed, g + 1)
                for h in range(H1):
                    name = ("k_nope", g, h)
                    claim(*name)
                    for j in range(2):
                        ins = M(bank(*name)[:], w_ukv[:, j, h * P:(h + 1) * P], lat[:, j, :], start=(j == 0), stop=(j == 1))
                    ins.then_inc(tile_ready, 1)
                for b in range(BG):
                    name = ("v", g, b)
                    claim(*name)
                    for j in range(2):
                        ins = M(bank(*name)[:], lat[:, j, b * P:(b + 1) * P], w_ukv[:, 2 + j, :], start=(j == 0), stop=(j == 1))
                    ins.then_inc(tile_ready, 1)

            for g in range(G):
                wait_x(pe, g, G // 2 + g // 2)
                for j in range(4):
                    project(("xq", g, j), x_of(g), KC)
                for j in range(4):
                    wait_drained(pe, "xq", g, j)
                squares(("q_sq", g), y_of(g), 4)
                pe.wait_ge(q_normed, g + 1)
                for h in range(H1):
                    project(("q_nope", g, h), lat, 4)
                for j in range(4):
                    project(("q_rope", g, j), lat, 4)
                for tag in ("gate_a", "u", "gate_b"):
                    for j in range(4):
                        project((tag, g, j), x_of(g), KC)
                for j in range(4):
                    name = ("mix", g, j)
                    pe.wait_ge(pooled, 4 * g + j + 1)
                    claim(*name)
                    M(bank(*name)[:], pool_w[:, j, :], lat[:, j, :], start=True, stop=True).then_inc(tile_ready, 1)

                units = mla_units(g)
                for u in range(len(units) + 2):
                    if u < len(units):
                        i, h = units[u]
                        b = i % BG
                        if u == 0:
                            for hh in range(H1):
                                wait_drained(pe, "q_nope", g, hh)
                            pe.wait_ge(q_rotated, g + 1)
                        if g == 0 and u == 0:
                            for hh in range(H1):
                                wait_drained(pe, "k_nope", G - 1, hh)
                        for c in range(S // TB):
                            name = ("score", i, h, c)
                            claim(*name)
                            M(bank(*name)[:], q_nope[:, h, b * P:(b + 1) * P], k_nope[:, h, c * TB:(c + 1) * TB],
                              start=True, stop=False)
                            M(bank(*name)[:], q_rope[:, h, b * P:(b + 1) * P],
                              k_rope[:, c * TB:(c + 1) * TB], start=False, stop=True).then_inc(tile_ready, 1)
                    if 2 <= u and units[u - 2][1] == H1 - 1:
                        i = units[u - 2][0]
                        pe.wait_ge(o_scaled, i + 1)
                        claim("o_t", i)
                        for j in range(4):
                            ins = nc.tensor.transpose(bank("o_t", i)[:, j * P:(j + 1) * P], o_sb[:, j * P:(j + 1) * P], ident[:])
                        ins.then_inc(tile_ready, 1)
                    if 1 <= u <= len(units):
                        i, h = units[u - 1]
                        n = H1 * BG * g + u - 1
                        pe.wait_ge(probs_made, n + 1)
                        if h == 0 and i >= 2:
                            pe.wait_ge(o_scaled, i - 1)

                        def transposes(c):
                            name = ("prob_t", i, h, c)
                            claim(*name)
                            for k in range(BG):
                                col = (n % 2) * S + c * TB + k * P
                                ins = nc.tensor.transpose(bank(*name)[:, k * P:(k + 1) * P], probs[:, col:col + P], ident[:])
                            ins.then_inc(tile_ready, 1)

                        def values(c):
                            wait_drained(pe, "prob_t", i, h, c)
                            m = n * (S // TB) + c
                            for k in range(BG):
                                ins = M(o_acc[i % 2][:, h * P:(h + 1) * P], prob_t[:, m % PT_SLOTS, k * P:(k + 1) * P],
                                        val[:, c * BG + k, h * P:(h + 1) * P],
                                        start=(c == 0 and k == 0), stop=(c == S // TB - 1 and k == BG - 1))
                            ins.then_inc(pv_done, 1)

                        transposes(0)
                        for c in range(1, S // TB):
                            transposes(c)
                            values(c - 1)
                        values(S // TB - 1)

                for b in range(BG):
                    wait_drained(pe, "o_t", BG * g + b)
                for j in range(4):
                    wait_drained(pe, "mix", g, j)
                for c in range(KC):
                    project(("1out", g, c), y_of(g), KC)
                for c in range(KC):
                    wait_drained(pe, "1out", g, c)
                squares(("1mean", g), x_of(g), KC)
                claim("1var", g)
                for c in range(KC):
                    pe.wait_ge(squared, KC * g + c + 1)
                    ins = M(bank("1var", g)[:], ones[:], sq_view(probs)[:, c, :], start=(c == 0), stop=(c == KC - 1))
                ins.then_inc(tile_ready, 1)

            second_begins(pe)
            claim("t5_row")
            M(bank("t5_row")[0:H2, 0:3 * P], rel, t5_hot, start=True, stop=True).then_inc(tile_ready, 1)
            pe.wait_ge(t5_here, 32)
            for j in range(4):
                claim("t5", j)
                M(bank("t5", j)[:], anti, index[:, j * TB:(j + 1) * TB], start=True, stop=True).then_inc(tile_ready, 1)

            def weights(key):
                n = WSLOT[key]
                pe.wait_ge(w_here[n % SLOTS], 16 * (n // SLOTS + 1))
                return ring[n % SLOTS]

            def meta_features(name):
                w = weights(name)
                claim(*name)
                for k in range(KC):
                    ins = M(bank(*name)[:, 0:META], w[:, k * P:(k + 1) * P], x_meta[:, k, :], start=(k == 0), stop=(k == KC - 1))
                ins.then_inc(tile_ready, 1)

            meta_features(("m_c",))
            pe.wait_ge(lb_exp, 1)
            claim("m_c_sq")
            M(bank("m_c_sq")[:, 0:META], ones[:], tmp[:, 0, 0:META], start=True, stop=True).then_inc(tile_ready, 1)
            w = weights(("w_uv",))
            pe.wait_ge(c_normed, 1)
            claim("m_v")
            M(bank("m_v")[:], c_meta[:], w[:, 0:TB], start=True, stop=True).then_inc(tile_ready, 1)
            for h in range(H3):
                meta_features(("m_f", h))
            claim("m_i")
            for k in range(KC):
                w = weights(("w_i", (), k // 2))
                ins = M(bank("m_i")[0:META, :], x_meta[:, k, :], w[:, (k % 2) * TB:(k % 2 + 1) * TB], start=(k == 0), stop=(k == KC - 1))
            ins.then_inc(tile_ready, 1)
            pe.wait_ge(lev_diff_meta, 2)
            claim("m_k_t")
            for h in range(H3):
                ins = nc.tensor.transpose(bank("m_k_t")[0:META, h * P:(h + 1) * P], probs[:, 256 + h * META:256 + (h + 1) * META], ident[:])
            ins.then_inc(tile_ready, 1)
            wait_drained(pe, "m_k_t")
            wait_drained(pe, "m_i")
            claim("m_u")
            for h in range(H3):
                ins = M(bank("m_u")[:, h * P:(h + 1) * P], kd_t[0:META, 0, h * P:(h + 1) * P], h_i[0:META, 0, h * P:(h + 1) * P],
                        start=True, stop=True)
            ins.then_inc(tile_ready, 1)

            def index_scores(i, c):
                b = i % BG
                at, wide_ = index_chunks(i)[c]
                for h in range(HI):
                    claim("index", i, c, h)
                    M(bank("index", i, c, h)[:, 0:wide_], qi[:, h, b * P:(b + 1) * P], ki[:, at:at + wide_],
                      start=True, stop=True).then_inc(tile_ready, 1)

            for g in range(G):
                wait_x(pe, g, G + 2 * (g // 2))
                he, ha = he_of(g), ha_of(g)
                for st in second_steps(g):
                    kind = st[0]
                    if kind in SECOND_CHUNKS:
                        project(st, x_of(g), KC)
                    elif kind == "i":
                        for b in range(BG):
                            claim("i", g, b)
                        for j in range(4):
                            w = weights(("w_i", (g,), j))
                            for b in range(BG):
                                for k in (2 * j, 2 * j + 1):
                                    ins = M(bank("i", g, b)[:], x_of(g)[:, k, b * P:(b + 1) * P], w[:, (k % 2) * TB:(k % 2 + 1) * TB],
                                            start=(k == 0), stop=(k == KC - 1))
                                if j == 3:
                                    ins.then_inc(tile_ready, 1)
                    elif kind == "c_sq":
                        wait_drained(pe, "c", g)
                        claim(*st)
                        M(bank(*st)[:], ones[:], tmp[:, 0, :], start=True, stop=True).then_inc(tile_ready, 1)
                    elif kind == "ql":
                        w = weights(("w_uk", g))
                        claim(*st)
                        wait_drained(pe, "qa", g, st[2] // 2)
                        M(bank(*st)[:], w[:, st[2] * P:(st[2] + 1) * P], qa[:, st[2] // 2, :], start=True, stop=True).then_inc(tile_ready, 1)
                    elif kind == "v2":
                        w = weights(("w_uv", g))
                        pe.wait_ge(c_normed, g + 2)
                        claim(*st)
                        at = g * TB + st[2] * P
                        M(bank(*st)[:], c_t[:, at:at + P], w[:, 0:TB], start=True, stop=True).then_inc(tile_ready, 1)
                    elif kind == "wi":
                        claim(*st)
                        for b in range(BG):
                            for k in range(KC):
                                ins = M(bank(*st)[:, b * HI:(b + 1) * HI], x_of(g)[:, k, b * P:(b + 1) * P], w_wi[:, k, :],
                                        start=(k == 0), stop=(k == KC - 1))
                        ins.then_inc(tile_ready, 1)
                    elif kind == "level":
                        pair, lev = st[2], st[3]
                        if lev < len(LEVELS):
                            pe.wait_ge(lev_made, level_no(g, pair, lev) + 1)
                        for e in range(2):
                            claim(*st, e)
                            for b in range(BG):
                                cols = slice(b * P, (b + 1) * P)
                                keys, queries = (hx[lev % 2], hx[lev % 2]) if lev < len(LEVELS) else (hk, hqb)
                                ins = M(bank(*st, e)[:, cols], keys[:, e, cols], queries[:, e, cols], start=True, stop=True)
                            ins.then_inc(tile_ready, 1)
                    elif kind == "index_row":
                        if st[2] == 0:
                            wait_drained(pe, "ki", g)
                            for j in range(2):
                                wait_drained(pe, "qi", g, j)
                        index_scores(BG * g, st[2])
                    elif kind == "decayed":
                        pair = st[2]
                        pe.wait_ge(lev_made, level_no(g, pair, len(LEVELS) + 1) + 1)
                        for b in range(BG):
                            name = ("kd_t", g, pair, b)
                            claim(*name)
                            for e in range(2):
                                ins = nc.tensor.transpose(bank(*name)[:, e * P:(e + 1) * P], he[0][:, e, b * P:(b + 1) * P], ident[:])
                            ins.then_inc(tile_ready, 1)
                        for e in range(2):
                            wait_drained(pe, "level", g, pair, len(LEVELS), e)
                        for b in range(BG):
                            wait_drained(pe, "i", g, b)
                    elif kind == "chunk":
                        pair, b = st[2], st[3]
                        cols = slice(b * P, (b + 1) * P)
                        if b > 0:
                            wait_drained(pe, "u_h", g, pair, b - 1)
                        claim("o_h", g, pair, b)
                        for e in range(2):
                            h = 2 * pair + e
                            dst = bank("o_h", g, pair, b)[:, e * P:(e + 1) * P]
                            M(dst, h_i[:, b, h * P:(h + 1) * P], ha[:, e, cols], start=True, stop=False)
                            ins = M(dst, state[:, h, :], hf[:, e, cols], start=False, stop=True)
                        ins.then_inc(tile_ready, 1)
                        wait_drained(pe, "kd_t", g, pair, b)
                        claim("u_h", g, pair, b)
                        for e in range(2):
                            h = 2 * pair + e
                            ins = M(bank("u_h", g, pair, b)[:, e * P:(e + 1) * P],
                                    kd_t[:, b // 2, (b % 2) * 256 + e * P:(b % 2) * 256 + (e + 1) * P],
                                    h_i[:, b, h * P:(h + 1) * P], start=True, stop=True)
                        ins.then_inc(tile_ready, 1)
                    elif kind == "h_norm":
                        pair = st[2]
                        pe.wait_ge(o_squared, 2 * g + pair + 1)
                        for e in range(2):
                            claim("h_sq", g, pair, e)
                            M(bank("h_sq", g, pair, e)[:], ones[:], hk[:, e, :], start=True, stop=True).then_inc(tile_ready, 1)

                wait_drained(pe, "ki", g)
                for j in range(2):
                    wait_drained(pe, "qi", g, j)
                for h in range(H2):
                    wait_drained(pe, "ql", g, h)
                for b in range(BG):
                    wait_drained(pe, "v2", g, b)
                units = dsa_units(g)
                for u in range(len(units) + 4):
                    if u < len(units):
                        i, h = units[u]
                        b = i % BG
                        cols = slice(b * P, (b + 1) * P)
                        if h == 0:
                            if i + 1 < BG * (g + 1) and needs_topk(i + 1):
                                for c in range(len(index_chunks(i + 1))):
                                    index_scores(i + 1, c)
                            claim("score_m", i)
                            for hh in range(H2):
                                ins = M(bank("score_m", i)[:, hh * META:(hh + 1) * META], ql[:, hh, cols], c_meta[:, 0:META],
                                        start=True, stop=True)
                            ins.then_inc(tile_ready, 1)
                        query = ql[:, h, cols]
                        for c, (at, wide_) in enumerate(far_chunks(i)):
                            claim("far", i, h, c)
                            M(bank("far", i, h, c)[:, 0:wide_], query, c_t[:, at:at + wide_],
                              start=True, stop=True).then_inc(tile_ready, 1)
                        wn, n_keys = near_width(i), keys_of(i)
                        claim("near", i, h)
                        M(bank("near", i, h)[:, 0:wn], query, c_t[:, n_keys - wn:n_keys],
                          start=True, stop=True).then_inc(tile_ready, 1)
                    over = ended(units, u, 2)
                    if over is not None:
                        pe.wait_ge(pm_made, over + 1)
                        claim("pm_t", over)
                        nc.tensor.transpose(bank("pm_t", over)[:, 0:P], p_meta[:], ident[:]).then_inc(tile_ready, 1)
                        wait_drained(pe, "pm_t", over)
                        M(o_acc[over % 2][:], pm_t[:], v_meta[:], start=False, stop=True, skip_group_check=True).then_inc(pvm_done, 1)
                    if 1 <= u <= len(units):
                        i, h = units[u - 1]
                        n = H2 * BG * g + u - 1
                        pe.wait_ge(probs2_made, n + 1)
                        if h == 0 and i >= 2:
                            pe.wait_ge(o2_scaled, i - 1)
                        count = prob_tiles(i)

                        def transposes2(c):
                            claim("p2_t", i, h, c)
                            for k in range(c * BG, min(c * BG + BG, i + 1)):
                                ins = nc.tensor.transpose(bank("p2_t", i, h, c)[:, (k % BG) * P:(k % BG + 1) * P],
                                                          probs[:, (n % 2) * S + k * P:(n % 2) * S + (k + 1) * P], ident[:])
                            ins.then_inc(tile_ready, 1)

                        def values2(c):
                            wait_drained(pe, "p2_t", i, h, c)
                            m = prob_tiles_before(i, h) + c
                            for k in range(c * BG, min(c * BG + BG, i + 1)):
                                ins = M(o_acc[i % 2][:, h * DH2:(h + 1) * DH2], prob_t[:, m % PT_SLOTS, (k % BG) * P:(k % BG + 1) * P],
                                        v2[:, k, h * DH2:(h + 1) * DH2], start=(h == 0 and k == 0), stop=False, skip_group_check=True)
                            ins.then_inc(pv2_done, 1)

                        transposes2(0)
                        for c in range(1, count):
                            transposes2(c)
                            values2(c - 1)
                        values2(count - 1)
                    over = ended(units, u, 3)
                    if over is not None:
                        pe.wait_ge(o2_scaled, over + 1)
                        claim("o2_t", over)
                        for j in range(4):
                            ins = nc.tensor.transpose(bank("o2_t", over)[:, j * P:(j + 1) * P], o_sb[:, j * P:(j + 1) * P], ident[:])
                        ins.then_inc(tile_ready, 1)

                for b in range(BG):
                    wait_drained(pe, "o2_t", BG * g + b)
                pe.wait_ge(h_free, H3 * (g + 1))
                for c in range(KC):
                    project(("2out", g, c), y_of(g), KC)
                for c in range(KC):
                    wait_drained(pe, "2out", g, c)
                squares(("2mean", g), x_of(g), KC)
                claim("2var", g)
                for c in range(KC):
                    pe.wait_ge(squared, KC * (G + g) + c + 1)
                    ins = M(bank("2var", g)[:], ones[:], sq_view(probs)[:, c, :], start=(c == 0), stop=(c == KC - 1))
                ins.then_inc(tile_ready, 1)
            assert done[0] == len(TILES)


def tiled(w, cols):
    k = w.shape[0] // P
    return np.ascontiguousarray(w[:, cols].reshape(k, P, len(cols)).transpose(1, 0, 2).reshape(P, k * len(cols)))


def tokens_last(x):
    return np.ascontiguousarray(x.reshape(KC, P, x.shape[1]).transpose(1, 0, 2))


def t5_bucket(dist):
    n = np.maximum(dist, 0)
    large = 16 + (np.log(np.maximum(n, 1).astype(np.float32) / 16) / np.log(8.0) * 16).astype(np.int32)
    return np.where(n < 16, n, np.minimum(large, 31))


def columns(v):
    return v.reshape(-1, P).T


def lay_out(inp):
    ar = np.arange
    w_in = np.asarray(inp["w_in"])
    rope0 = QR + KVR
    straight = np.concatenate([ar(ROPE), ar(ROPE)])
    swapped = (straight + ROPE // 2) % ROPE
    kv_cols = [QR + ar(P), QR + P + ar(P), rope0 + straight, rope0 + swapped]
    q_cols = [j * P + ar(P) for j in range(4)] + [rope0 + ROPE + j * P + ar(P) for j in range(12)]
    w_uq = np.asarray(inp["w_uq"])
    uq_cols = [h * QK_DIM + ar(P) for h in range(H1)]
    for pair in range(2):
        for s in (ar(ROPE), (ar(ROPE) + ROPE // 2) % ROPE):
            uq_cols.append(np.concatenate([(2 * pair + e) * QK_DIM + P + s for e in range(2)]))
    w_ukv = np.asarray(inp["w_ukv"]).reshape(2, P, H1, 2, P)
    freq = (10000.0 ** (-np.arange(ROPE // 2) / (ROPE // 2))).astype(np.float32)
    sign = np.concatenate([-np.ones(ROPE // 2), np.ones(ROPE // 2)]).astype(np.float32)
    vecs = {"q_g": inp["q_norm_g"], "kv_g": inp["kv_norm_g"], "pool_scale": inp["pool_scale"], "ln_g": inp["ln_g"][0],
            "ln_b": inp["ln_b"][0], "kv_g2": inp["kv_norm_g_2"][0], "hgrn_g": inp["hgrn_norm_g_2"][0],
            "ln_g2": inp["ln_g_2"][0], "ln_b2": inp["ln_b_2"][0], "lb_raw": inp["hgrn_lb_raw_2"][0],
            "inv_freq": np.tile(freq, 4), "rope_sign": np.tile(sign, 2)}
    cnt = np.zeros((P, 4, HALO), np.float32)
    for j, w in enumerate(POOL_W):
        cnt[:, j, :] = w / np.minimum(np.arange(HALO) + 1, w)
    sizes = (512, 128, 256, 64, 4, 512, 512, 512, 512, 512)
    q0, c0, qi0, ki0, wi0, ga0, hq0, hf0, hi0, gh0 = np.cumsum((0,) + sizes[:-1])
    w2 = np.asarray(inp["w_in_2"])[0]
    cols2 = [c0 + ar(P), ki0 + np.tile(ar(DH2), 2)] + [qi0 + j * P + ar(P) for j in range(2)]
    for start in (q0, ga0, hq0, hf0, gh0):
        cols2 += [start + j * P + ar(P) for j in range(4)]
    w_uk = np.zeros((2, DH2, H2, P), np.float32)
    for h in range(H2):
        w_uk[h % 2, :, h] = np.asarray(inp["w_uk_2"])[0, h]
    w_uv = np.asarray(inp["w_uv_2"])[0].transpose(1, 0, 2).reshape(P, TB)
    dist = NEAR - 1 - np.arange(3 * P)
    hot = np.zeros((32, 3 * P), np.float32)
    hot[t5_bucket(dist), np.arange(3 * P)] = 1
    s, t = np.arange(P)[:, None], np.arange(P)[None, :]
    levels = [(s // (2 * w) == t // (2 * w)) & (s % (2 * w) < w) & (t % (2 * w) >= w) for w in LEVELS] + [s == t]
    return {
        "w_in2": np.stack([tiled(w2, c) for c in cols2]),
        "w_uk": w_uk.reshape(1, P, H2 * P),
        "w_uv": np.ascontiguousarray(w_uv)[None],
        "w_i": np.stack([tiled(w2[2 * P * j:2 * P * (j + 1)], hi0 + ar(TB)) for j in range(4)]),
        "w_wi": np.ascontiguousarray(w2[:, wi0:wi0 + HI].reshape(KC, P, HI).transpose(1, 0, 2)),
        "w_out2": np.stack([tiled(np.asarray(inp["w_out_2"])[0], c * P + ar(P)) for c in range(KC)]),
        "meta_t": tokens_last(np.asarray(inp["meta_tokens_2"]).T),
        "rel": np.asarray(inp["rel_bias_2"]),
        "t5_hot": hot,
        "anti": np.ascontiguousarray(np.eye(P, dtype=np.float32)[::-1]),
        "causal": np.where(s >= t, 0.0, MASKED).astype(np.float32),
        "lev_mask": np.stack(levels, axis=1).astype(np.int32).reshape(P, -1),
        "halves": np.tile((0.5 ** (1 + np.arange(ROUNDS))).astype(np.float32), (P, 1)),
        "block_diag": (np.arange(P)[:, None] // META == np.arange(TB)[None, :] // DH2).astype(np.float32),
        "x_t": tokens_last(np.asarray(inp["x"])[0].T),
        "pos_k": np.asarray(inp["positions"]),
        "pos_q": np.ascontiguousarray(np.asarray(inp["positions"])[0].reshape(NB, P).T),
        "w_in_kv": np.stack([tiled(w_in, c) for c in kv_cols]),
        "w_in_q": np.stack([tiled(w_in, c) for c in q_cols]),
        "w_uq": np.stack([tiled(w_uq, c) for c in uq_cols]),
        "w_ukv": np.ascontiguousarray(w_ukv.transpose(3, 0, 1, 2, 4).reshape(4, P, TB).transpose(1, 0, 2)),
        "pool_w": np.ascontiguousarray(np.asarray(inp["pool_w"]).transpose(1, 0, 2)),
        "pool_cnt": cnt,
        "w_out": np.stack([tiled(np.asarray(inp["w_out"]), c * P + ar(P)) for c in range(KC)]),
        "vec": np.ascontiguousarray(np.concatenate([columns(np.asarray(vecs[n])) for n in VEC], axis=1)),
        "ident": np.eye(P, dtype=np.float32),
    }


def kernel(**inputs):
    import concourse.bacc as bacc
    from concourse.bass_utils import run_bass_kernel_spmd as run

    nc = bacc.Bacc("TRN2", target_bir_lowering=False, num_devices=1)
    arrays = lay_out(inputs)
    args = {name: nc.dram_tensor("in_" + name, a.shape, mybir.dt.from_np(a.dtype), kind="ExternalInput").ap()
            for name, a in arrays.items()}
    out = nc.dram_tensor("out_t", (P, KC, S), mybir.dt.float32, kind="ExternalOutput").ap()
    program(nc, args, out)
    result = run(nc, [{"in_" + name: a for name, a in arrays.items()}], core_ids=[0]).results[0]["out_t"]
    return np.ascontiguousarray(result.transpose(2, 1, 0).reshape(1, S, D))
```
